# Optimizing a Trainium2 kernel written in Bass

```python
import math
import jax, jax.numpy as jnp
from jax import lax
import numpy as np

D_MODEL = 1024
BATCH = 1
SEQ = 256
DEPTH = 1

HEAD_DIM = 64
NSA_HEADS = 8
NSA_KV_HEADS = 2
NSA_GROUP = NSA_HEADS // NSA_KV_HEADS
SB_HEADS = 8
CMP_BLOCK = 32
CMP_STRIDE = 16
CMP_HIDDEN = HEAD_DIM
SEL_BLOCK = 64
SEL_TOPK = 16
WINDOW = 512
NSA_QBLOCK = 64
SB_QBLOCK = 128
N_BUCKETS = 32
MAX_DISTANCE = 128
D_FF = 4 * D_MODEL
EPS = 1e-6
FORCED_BONUS = 1e4
NEG_BLOCK = -1e9
NEG_LOGIT = -1e30

Q_A_W = NSA_HEADS * HEAD_DIM
KV_A_W = NSA_KV_HEADS * HEAD_DIM
GATE_A_W = NSA_HEADS * 3
SB_W = SB_HEADS * HEAD_DIM
IN_SPLITS = (Q_A_W, KV_A_W, KV_A_W, KV_A_W, KV_A_W, KV_A_W, KV_A_W, GATE_A_W, SB_W, SB_W, SB_W, D_MODEL, D_MODEL)
IN_WIDTH = Q_A_W + 6 * KV_A_W + GATE_A_W + 3 * SB_W + 2 * D_MODEL


def rms_norm(x, g):
    x32 = x.astype(jnp.float32)
    y = x32 * lax.rsqrt(jnp.mean(x32 * x32, axis=-1, keepdims=True) + EPS)
    return (y * g.astype(jnp.float32)).astype(x.dtype)

def rel_bucket(dist):
    n = jnp.maximum(dist, 0)
    max_exact = N_BUCKETS // 2
    nf = jnp.maximum(n, 1).astype(jnp.float32)
    large = max_exact + (jnp.log(nf / max_exact) / math.log(MAX_DISTANCE / max_exact) * (N_BUCKETS - max_exact)).astype(jnp.int32)
    large = jnp.minimum(large, N_BUCKETS - 1)
    return jnp.where(n < max_exact, n, large)

def masked_softmax(logits, mask):
    masked = jnp.where(mask, logits, NEG_LOGIT)
    m = jnp.max(masked, axis=-1, keepdims=True)
    e = jnp.where(mask, jnp.exp(masked - m), 0.0)
    return e / jnp.maximum(jnp.sum(e, axis=-1, keepdims=True), 1e-30)

def compress_blocks(src, pos, w1, w2):
    B, S = src.shape[0], src.shape[1]
    nc = (S - CMP_BLOCK) // CMP_STRIDE + 1
    idx = jnp.arange(nc)[:, None] * CMP_STRIDE + jnp.arange(CMP_BLOCK)[None, :]
    blk = src[:, idx] + pos[None, None, :, None, :]
    blk = blk.transpose(0, 1, 3, 2, 4).reshape(B, nc, NSA_KV_HEADS, CMP_BLOCK * HEAD_DIM)
    return jax.nn.silu(blk @ w1) @ w2

def cmp_to_sel_overlap(nc, nsel):
    c_start = jnp.arange(nc) * CMP_STRIDE
    s_start = jnp.arange(nsel) * SEL_BLOCK
    ov = jnp.minimum(c_start[:, None] + CMP_BLOCK, s_start[None, :] + SEL_BLOCK) - jnp.maximum(c_start[:, None], s_start[None, :])
    return jnp.clip(ov, 0, CMP_BLOCK).astype(jnp.float32) / CMP_BLOCK

def nsa_attention(q, k_cmp, v_cmp, k_slc, v_slc, k_win, v_win, gates, rel_bias):
    B, S = q.shape[0], q.shape[1]
    nc = k_cmp.shape[1]
    nsel = S // SEL_BLOCK
    n_top = min(SEL_TOPK, nsel)
    scale = HEAD_DIM ** -0.5
    cmp_last = jnp.arange(nc) * CMP_STRIDE + CMP_BLOCK - 1
    overlap = cmp_to_sel_overlap(nc, nsel)
    tbl = rel_bias.astype(jnp.float32)
    tbl_g = tbl.reshape(N_BUCKETS, NSA_KV_HEADS, NSA_GROUP)
    ksel = k_slc.reshape(B, nsel, SEL_BLOCK, NSA_KV_HEADS, HEAD_DIM).transpose(0, 3, 1, 2, 4)
    vsel = v_slc.reshape(B, nsel, SEL_BLOCK, NSA_KV_HEADS, HEAD_DIM).transpose(0, 3, 1, 2, 4)
    kw_pad = jnp.pad(k_win, ((0, 0), (WINDOW, 0), (0, 0), (0, 0)))
    vw_pad = jnp.pad(v_win, ((0, 0), (WINDOW, 0), (0, 0), (0, 0)))
    bidx = jnp.arange(B)[:, None, None, None]
    hidx = jnp.arange(NSA_KV_HEADS)[None, :, None, None]
    blk = jnp.arange(nsel)
    tok_in_blk = jnp.arange(SEL_BLOCK)
    win_off = jnp.arange(WINDOW + NSA_QBLOCK)

    def head_bias(dist):
        b = tbl[rel_bucket(dist)]
        return jnp.moveaxis(b, -1, 0).reshape(NSA_KV_HEADS, NSA_GROUP, dist.shape[0], dist.shape[1])

    def block(i):
        start = i * NSA_QBLOCK
        t = start + jnp.arange(NSA_QBLOCK)
        qb = lax.dynamic_slice_in_dim(q, start, NSA_QBLOCK, axis=1)
        gb = lax.dynamic_slice_in_dim(gates, start, NSA_QBLOCK, axis=1)
        dist_c = t[:, None] - cmp_last[None, :]
        s_c = jnp.einsum('bqhgd,bchd->bhgqc', qb, k_cmp).astype(jnp.float32) * scale + head_bias(dist_c)
        p_c = masked_softmax(s_c, dist_c >= 0)
        o_c = jnp.einsum('bhgqc,bchd->bqhgd', p_c.astype(v_cmp.dtype), v_cmp)
        imp = jnp.einsum('bhgqc,cn->bhqn', p_c, overlap)
        cur = (t // SEL_BLOCK)[:, None]
        forced = (blk == 0) | (blk == cur) | (blk == cur - 1)
        imp = jnp.where(blk > cur, NEG_BLOCK, imp + jnp.where(forced, FORCED_BONUS, 0.0))
        _, top = lax.top_k(imp, n_top)
        kg = ksel[bidx, hidx, top]
        vg = vsel[bidx, hidx, top]
        tok = top[..., None] * SEL_BLOCK + tok_in_blk
        dist_s = t[:, None, None] - tok
        bias_s = jnp.moveaxis(tbl_g[rel_bucket(dist_s), hidx[..., None]], -1, 2)
        s_s = jnp.einsum('bqhgd,bhqnkd->bhgqnk', qb, kg).astype(jnp.float32) * scale + bias_s
        shp = s_s.shape
        m_s = (dist_s >= 0)[:, :, None].reshape(B, NSA_KV_HEADS, 1, NSA_QBLOCK, -1)
        p_s = masked_softmax(s_s.reshape(shp[0], shp[1], shp[2], shp[3], -1), m_s).reshape(shp)
        o_s = jnp.einsum('bhgqnk,bhqnkd->bqhgd', p_s.astype(vg.dtype), vg)
        kwb = lax.dynamic_slice_in_dim(kw_pad, start, WINDOW + NSA_QBLOCK, axis=1)
        vwb = lax.dynamic_slice_in_dim(vw_pad, start, WINDOW + NSA_QBLOCK, axis=1)
        s_pos = start - WINDOW + win_off
        dist_w = t[:, None] - s_pos[None, :]
        m_w = (dist_w >= 0) & (dist_w < WINDOW) & (s_pos >= 0)[None, :]
        s_w = jnp.einsum('bqhgd,bkhd->bhgqk', qb, kwb).astype(jnp.float32) * scale + head_bias(dist_w)
        p_w = masked_softmax(s_w, m_w)
        o_w = jnp.einsum('bhgqk,bkhd->bqhgd', p_w.astype(vwb.dtype), vwb)
        return gb[..., 0:1] * o_c + gb[..., 1:2] * o_s + gb[..., 2:3] * o_w

    out = lax.map(block, jnp.arange(S // NSA_QBLOCK))
    return jnp.swapaxes(out, 0, 1).reshape(B, S, NSA_HEADS * HEAD_DIM)

def stick_breaking_attention(q, k, v):
    B, S = q.shape[0], q.shape[1]
    scale = HEAD_DIM ** -0.5
    key_pos = jnp.arange(S)

    def block(i):
        start = i * SB_QBLOCK
        t = start + jnp.arange(SB_QBLOCK)
        qb = lax.dynamic_slice_in_dim(q, start, SB_QBLOCK, axis=1)
        z = jnp.einsum('bqhd,bshd->bhqs', qb, k).astype(jnp.float32) * scale
        mask = key_pos[None, :] < t[:, None]
        log_keep = jnp.where(mask, jax.nn.log_sigmoid(-z), 0.0)
        suffix = lax.cumsum(log_keep, axis=3, reverse=True) - log_keep
        a = jnp.where(mask, jnp.exp(jax.nn.log_sigmoid(z) + suffix), 0.0)
        return jnp.einsum('bhqs,bshd->bqhd', a.astype(v.dtype), v)

    out = lax.map(block, jnp.arange(S // SB_QBLOCK))
    return jnp.swapaxes(out, 0, 1).reshape(B, S, SB_HEADS * HEAD_DIM)

def first_inputs(seed: int = 0) -> dict:
    key = jax.random.key(seed)
    ks = jax.random.split(key, 20)
    f32 = jnp.float32
    nrm = lambda k, shape, s: jax.random.normal(k, shape, f32) * s
    gain = lambda k, shape: 1.0 + 0.02 * jax.random.normal(k, shape, f32)
    return {
        'x': nrm(ks[0], (BATCH, SEQ, D_MODEL), 1.0),
        'c': nrm(ks[1], (BATCH, D_MODEL), 1.0),
        'rel_bias': nrm(ks[2], (N_BUCKETS, NSA_HEADS), 0.5),
        'ada_w': nrm(ks[3], (DEPTH, D_MODEL, 6 * D_MODEL), 0.5 * D_MODEL ** -0.5),
        'ada_b': nrm(ks[4], (DEPTH, 6 * D_MODEL), 0.02),
        'norm1_g': gain(ks[5], (DEPTH, D_MODEL)),
        'norm2_g': gain(ks[6], (DEPTH, D_MODEL)),
        'w_in': nrm(ks[7], (DEPTH, D_MODEL, IN_WIDTH), D_MODEL ** -0.5),
        'cmp_pos': nrm(ks[8], (DEPTH, CMP_BLOCK, HEAD_DIM), 0.5),
        'cmp_k_w1': nrm(ks[9], (DEPTH, CMP_BLOCK * HEAD_DIM, CMP_HIDDEN), (CMP_BLOCK * HEAD_DIM) ** -0.5),
        'cmp_k_w2': nrm(ks[10], (DEPTH, CMP_HIDDEN, HEAD_DIM), CMP_HIDDEN ** -0.5),
        'cmp_v_w1': nrm(ks[11], (DEPTH, CMP_BLOCK * HEAD_DIM, CMP_HIDDEN), (CMP_BLOCK * HEAD_DIM) ** -0.5),
        'cmp_v_w2': nrm(ks[12], (DEPTH, CMP_HIDDEN, HEAD_DIM), CMP_HIDDEN ** -0.5),
        'q_norm_g': gain(ks[13], (DEPTH, HEAD_DIM)),
        'k_norm_g': gain(ks[14], (DEPTH, 3, HEAD_DIM)),
        'w_up_nsa': nrm(ks[15], (DEPTH, Q_A_W, D_MODEL), Q_A_W ** -0.5),
        'w_up_sb': nrm(ks[16], (DEPTH, SB_W, D_MODEL), SB_W ** -0.5),
        'w_out': nrm(ks[17], (DEPTH, D_MODEL, D_MODEL), D_MODEL ** -0.5),
        'mlp_w1': nrm(ks[18], (DEPTH, D_MODEL, D_FF), D_MODEL ** -0.5),
        'mlp_w2': nrm(ks[19], (DEPTH, D_FF, D_MODEL), D_FF ** -0.5),
    }

def first_block(x, c, rel_bias, ada_w, ada_b, norm1_g, norm2_g, w_in, cmp_pos, cmp_k_w1, cmp_k_w2, cmp_v_w1, cmp_v_w2, q_norm_g, k_norm_g, w_up_nsa, w_up_sb, w_out, mlp_w1, mlp_w2):
    B, S, _ = x.shape
    split_at = np.cumsum(IN_SPLITS)[:-1].tolist()
    kv_shape = (B, S, NSA_KV_HEADS, HEAD_DIM)
    sb_shape = (B, S, SB_HEADS, HEAD_DIM)
    h = x
    for layer in range(DEPTH):
        mod = jax.nn.silu(c) @ ada_w[layer] + ada_b[layer]
        shift1, scale1, gate1, shift2, scale2, gate2 = [m[:, None, :] for m in jnp.split(mod, 6, axis=-1)]
        u = rms_norm(h, norm1_g[layer]) * (1 + scale1) + shift1
        z = u @ w_in[layer]
        q_a, kc, vc, ksl, vsl, kwn, vwn, g_a, q_b, k_b, v_b, m_a, m_b = jnp.split(z, split_at, axis=-1)
        q_a = rms_norm(q_a.reshape(B, S, NSA_HEADS, HEAD_DIM), q_norm_g[layer]).reshape(B, S, NSA_KV_HEADS, NSA_GROUP, HEAD_DIM)
        k_cmp = rms_norm(compress_blocks(kc.reshape(kv_shape), cmp_pos[layer], cmp_k_w1[layer], cmp_k_w2[layer]), k_norm_g[layer, 0])
        v_cmp = compress_blocks(vc.reshape(kv_shape), cmp_pos[layer], cmp_v_w1[layer], cmp_v_w2[layer])
        k_slc = rms_norm(ksl.reshape(kv_shape), k_norm_g[layer, 1])
        k_win = rms_norm(kwn.reshape(kv_shape), k_norm_g[layer, 2])
        g_nsa = jax.nn.sigmoid(g_a).reshape(B, S, NSA_KV_HEADS, NSA_GROUP, 3)
        y_a = nsa_attention(q_a, k_cmp, v_cmp, k_slc, vsl.reshape(kv_shape), k_win, vwn.reshape(kv_shape), g_nsa, rel_bias) @ w_up_nsa[layer]
        y_b = stick_breaking_attention(q_b.reshape(sb_shape), k_b.reshape(sb_shape), v_b.reshape(sb_shape)) @ w_up_sb[layer]
        mixed = (jax.nn.sigmoid(m_a) * y_a + jax.nn.sigmoid(m_b) * y_b) @ w_out[layer]
        h = h + gate1 * mixed
        u2 = rms_norm(h, norm2_g[layer]) * (1 + scale2) + shift2
        ff = jnp.square(jax.nn.relu(u2 @ mlp_w1[layer])) @ mlp_w2[layer]
        h = h + gate2 * ff
    return h


MEM_LEN = 256
CHUNK = 128
SG_GROUPS = 8
SG_GROUP_DIM = 64
SG_WIDTH = SG_GROUPS * SG_GROUP_DIM
MLA_HEADS = 8
MLA_NOPE = 64
MLA_ROPE = 32
MLA_V = 64
MLA_QK = MLA_NOPE + MLA_ROPE
MLA_Q_RANK = 384
MLA_KV_RANK = 256
MLA_WIDTH = MLA_HEADS * MLA_V
MEM_HEADS = 4
MEM_HEAD_DIM = 128
MEM_WIDTH = MEM_HEADS * MEM_HEAD_DIM
N_BRANCH = 3
D_FF_2 = 2816
ROPE_BASE = 10000.0
Q_BLOCK = 128
NEG = -1e30

COL_U = 0
COL_V = COL_U + SG_WIDTH
COL_CQ = COL_V + SG_WIDTH
COL_CKV = COL_CQ + MLA_Q_RANK
COL_KR = COL_CKV + MLA_KV_RANK
COL_QM = COL_KR + MLA_ROPE
COL_GATE = COL_QM + MEM_WIDTH
IN_COLS = COL_GATE + N_BRANCH * D_MODEL


def rmsnorm(x, g):
    xf = x.astype(jnp.float32)
    y = xf * lax.rsqrt(jnp.mean(xf * xf, axis=-1, keepdims=True) + EPS)
    return (y * g.astype(jnp.float32)).astype(x.dtype)

def layernorm(x, g, b):
    xf = x.astype(jnp.float32)
    mu = jnp.mean(xf, axis=-1, keepdims=True)
    xc = xf - mu
    y = xc * lax.rsqrt(jnp.mean(xc * xc, axis=-1, keepdims=True) + EPS)
    return (y * g.astype(jnp.float32) + b.astype(jnp.float32)).astype(x.dtype)

def rope(x, positions):
    half = x.shape[-1] // 2
    inv = ROPE_BASE ** (-jnp.arange(half, dtype=jnp.float32) / half)
    ang = positions.astype(jnp.float32)[:, :, None] * inv
    cos = jnp.cos(ang)[:, :, None, :]
    sin = jnp.sin(ang)[:, :, None, :]
    x1 = x[..., :half].astype(jnp.float32)
    x2 = x[..., half:].astype(jnp.float32)
    return jnp.concatenate([x1 * cos - x2 * sin, x2 * cos + x1 * sin], axis=-1).astype(x.dtype)

def swiglu(x, w_gu, w_down):
    g, u = jnp.split(x @ w_gu, 2, axis=-1)
    return (jax.nn.silu(g) * u) @ w_down

def spatial_gating(u, v, ln_g, ln_b, w_s, b_s):
    B, S, _ = v.shape
    nc = S // CHUNK
    v = layernorm(v, ln_g, ln_b).reshape(B, nc, CHUNK, SG_GROUPS, SG_GROUP_DIM)
    causal = jnp.tril(jnp.ones((CHUNK, CHUNK), dtype=bool))
    w = jnp.where(causal[None], w_s, jnp.zeros_like(w_s))
    mixed = jnp.einsum('gts,bcsgd->bctgd', w, v) + b_s.T[None, None, :, :, None]
    return u * mixed.reshape(B, S, SG_WIDTH)

def causal_block_attention(q, k, v):
    B, S, H, Dqk = q.shape
    Dv = v.shape[-1]
    nb = S // Q_BLOCK
    scale = Dqk ** -0.5
    qb = q.reshape(B, nb, Q_BLOCK, H, Dqk).transpose(1, 0, 2, 3, 4)
    kpos = jnp.arange(S)

    def one_block(args):
        i, qi = args
        s = jnp.einsum('bqhd,bkhd->bhqk', qi, k).astype(jnp.float32) * scale
        qpos = i * Q_BLOCK + jnp.arange(Q_BLOCK)
        mask = kpos[None, :] <= qpos[:, None]
        s = jnp.where(mask[None, None], s, NEG)
        p = jax.nn.softmax(s, axis=-1)
        return jnp.einsum('bhqk,bkhd->bqhd', p.astype(v.dtype), v)

    out = lax.map(one_block, (jnp.arange(nb), qb))
    return out.transpose(1, 0, 2, 3, 4).reshape(B, S, H * Dv)

def mla(c_q, c_kv, k_rope, positions, cq_norm, w_uq, ckv_norm, w_ukv, q_norm, k_norm):
    B, S, _ = c_q.shape
    q = (rmsnorm(c_q, cq_norm) @ w_uq).reshape(B, S, MLA_HEADS, MLA_QK)
    q = rmsnorm(q, q_norm)
    q = jnp.concatenate([q[..., :MLA_NOPE], rope(q[..., MLA_NOPE:], positions)], axis=-1)
    kv = (rmsnorm(c_kv, ckv_norm) @ w_ukv).reshape(B, S, MLA_HEADS, MLA_NOPE + MLA_V)
    k_nope, v = kv[..., :MLA_NOPE], kv[..., MLA_NOPE:]
    k_pe = jnp.broadcast_to(k_rope[:, :, None, :], (B, S, MLA_HEADS, MLA_ROPE))
    k = rmsnorm(jnp.concatenate([k_nope, k_pe], axis=-1), k_norm)
    k = jnp.concatenate([k[..., :MLA_NOPE], rope(k[..., MLA_NOPE:], positions)], axis=-1)
    return causal_block_attention(q, k, v)

def memory_attention(q_m, mem, mem_norm, w_kv, q_norm, k_norm):
    B, S, _ = q_m.shape
    q = rmsnorm(q_m.reshape(B, S, MEM_HEADS, MEM_HEAD_DIM), q_norm)
    kv = rmsnorm(mem, mem_norm) @ w_kv
    M = mem.shape[1]
    k = rmsnorm(kv[..., :MEM_WIDTH].reshape(B, M, MEM_HEADS, MEM_HEAD_DIM), k_norm)
    v = kv[..., MEM_WIDTH:].reshape(B, M, MEM_HEADS, MEM_HEAD_DIM)
    s = jnp.einsum('bshd,bmhd->bhsm', q, k).astype(jnp.float32) * (MEM_HEAD_DIM ** -0.5)
    p = jax.nn.softmax(s, axis=-1)
    return jnp.einsum('bhsm,bmhd->bshd', p.astype(v.dtype), v).reshape(B, S, MEM_WIDTH)

def second_inputs(seed: int = 0) -> dict:
    key = jax.random.key(seed)
    ks = iter(jax.random.split(key, 40))

    def nrm(shape, scale):
        return jax.random.normal(next(ks), shape, jnp.float32) * scale

    def gain(n):
        return 1.0 + nrm((DEPTH, n), 0.05)

    L = DEPTH
    d = D_MODEL
    x = nrm((BATCH, SEQ, d), 1.0)
    mem = nrm((BATCH, MEM_LEN, d), 1.0)
    offset = jax.random.randint(next(ks), (BATCH, 1), 0, 1024, dtype=jnp.int32)
    positions = offset + jnp.arange(SEQ, dtype=jnp.int32)[None, :]
    return {
        "x": x,
        "mem": mem,
        "positions": positions,
        "ffn1_norm": gain(d),
        "ffn1_w_gu": nrm((L, d, 2 * D_FF_2), d ** -0.5),
        "ffn1_w_down": nrm((L, D_FF_2, d), D_FF_2 ** -0.5),
        "mix_norm": gain(d),
        "w_in": nrm((L, d, IN_COLS), d ** -0.5),
        "b_gate": nrm((L, N_BRANCH * d), 0.02),
        "sg_ln_g": gain(SG_WIDTH),
        "sg_ln_b": nrm((L, SG_WIDTH), 0.02),
        "sg_w": nrm((L, SG_GROUPS, CHUNK, CHUNK), 0.5 * CHUNK ** -0.5),
        "sg_b": 1.0 + nrm((L, SG_GROUPS, CHUNK), 0.1),
        "mla_cq_norm": gain(MLA_Q_RANK),
        "mla_w_uq": nrm((L, MLA_Q_RANK, MLA_HEADS * MLA_QK), MLA_Q_RANK ** -0.5),
        "mla_ckv_norm": gain(MLA_KV_RANK),
        "mla_w_ukv": nrm((L, MLA_KV_RANK, MLA_HEADS * (MLA_NOPE + MLA_V)), MLA_KV_RANK ** -0.5),
        "mla_q_norm": gain(MLA_QK),
        "mla_k_norm": gain(MLA_QK),
        "mem_norm": gain(d),
        "mem_w_kv": nrm((L, d, 2 * MEM_WIDTH), d ** -0.5),
        "mem_q_norm": gain(MEM_HEAD_DIM),
        "mem_k_norm": gain(MEM_HEAD_DIM),
        "w_branch_a": nrm((L, SG_WIDTH, d), SG_WIDTH ** -0.5),
        "w_branch_b": nrm((L, MLA_WIDTH, d), MLA_WIDTH ** -0.5),
        "w_branch_c": nrm((L, MEM_WIDTH, d), MEM_WIDTH ** -0.5),
        "w_out": nrm((L, d, d), d ** -0.5),
        "ffn2_norm": gain(d),
        "ffn2_w_gu": nrm((L, d, 2 * D_FF_2), d ** -0.5),
        "ffn2_w_down": nrm((L, D_FF_2, d), D_FF_2 ** -0.5),
    }

def second_block(x, mem, positions, ffn1_norm, ffn1_w_gu, ffn1_w_down, mix_norm, w_in, b_gate,
              sg_ln_g, sg_ln_b, sg_w, sg_b, mla_cq_norm, mla_w_uq, mla_ckv_norm, mla_w_ukv,
              mla_q_norm, mla_k_norm, mem_norm, mem_w_kv, mem_q_norm, mem_k_norm,
              w_branch_a, w_branch_b, w_branch_c, w_out, ffn2_norm, ffn2_w_gu, ffn2_w_down):
    B, S, _ = x.shape
    for l in range(DEPTH):
        x = x + 0.5 * swiglu(rmsnorm(x, ffn1_norm[l]), ffn1_w_gu[l], ffn1_w_down[l])
        h = rmsnorm(x, mix_norm[l])
        z = h @ w_in[l]
        u = jax.nn.gelu(z[..., COL_U:COL_V], approximate=False)
        v = jax.nn.gelu(z[..., COL_V:COL_CQ], approximate=False)
        y_a = spatial_gating(u, v, sg_ln_g[l], sg_ln_b[l], sg_w[l], sg_b[l])
        y_b = mla(z[..., COL_CQ:COL_CKV], z[..., COL_CKV:COL_KR], z[..., COL_KR:COL_QM], positions,
                  mla_cq_norm[l], mla_w_uq[l], mla_ckv_norm[l], mla_w_ukv[l],
                  mla_q_norm[l], mla_k_norm[l])
        y_c = memory_attention(z[..., COL_QM:COL_GATE], mem, mem_norm[l], mem_w_kv[l],
                               mem_q_norm[l], mem_k_norm[l])
        gates = jax.nn.sigmoid(z[..., COL_GATE:] + b_gate[l]).reshape(B, S, N_BRANCH, D_MODEL)
        merged = (gates[:, :, 0] * (y_a @ w_branch_a[l])
                  + gates[:, :, 1] * (y_b @ w_branch_b[l])
                  + gates[:, :, 2] * (y_c @ w_branch_c[l]))
        x = x + merged @ w_out[l]
        x = x + 0.5 * swiglu(rmsnorm(x, ffn2_norm[l]), ffn2_w_gu[l], ffn2_w_down[l])
    return x


def setup_inputs(seed=0):
    out = dict(first_inputs(seed))
    for name, value in second_inputs(seed + 1).items():
        if name != "x":
            out[name + "_2"] = value
    return out


def reference(
    x, c, rel_bias, ada_w, ada_b, norm1_g, norm2_g, w_in, cmp_pos, cmp_k_w1, cmp_k_w2, cmp_v_w1,
    cmp_v_w2, q_norm_g, k_norm_g, w_up_nsa, w_up_sb, w_out, mlp_w1, mlp_w2, mem_2, positions_2,
    ffn1_norm_2, ffn1_w_gu_2, ffn1_w_down_2, mix_norm_2, w_in_2, b_gate_2, sg_ln_g_2, sg_ln_b_2,
    sg_w_2, sg_b_2, mla_cq_norm_2, mla_w_uq_2, mla_ckv_norm_2, mla_w_ukv_2, mla_q_norm_2,
    mla_k_norm_2, mem_norm_2, mem_w_kv_2, mem_q_norm_2, mem_k_norm_2, w_branch_a_2,
    w_branch_b_2, w_branch_c_2, w_out_2, ffn2_norm_2, ffn2_w_gu_2, ffn2_w_down_2,
):
    x = first_block(
        x, c, rel_bias, ada_w, ada_b, norm1_g, norm2_g, w_in, cmp_pos, cmp_k_w1, cmp_k_w2,
        cmp_v_w1, cmp_v_w2, q_norm_g, k_norm_g, w_up_nsa, w_up_sb, w_out, mlp_w1, mlp_w2,
    )
    return second_block(
        x, mem_2, positions_2, ffn1_norm_2, ffn1_w_gu_2, ffn1_w_down_2, mix_norm_2, w_in_2,
        b_gate_2, sg_ln_g_2, sg_ln_b_2, sg_w_2, sg_b_2, mla_cq_norm_2, mla_w_uq_2,
        mla_ckv_norm_2, mla_w_ukv_2, mla_q_norm_2, mla_k_norm_2, mem_norm_2, mem_w_kv_2,
        mem_q_norm_2, mem_k_norm_2, w_branch_a_2, w_branch_b_2, w_branch_c_2, w_out_2,
        ffn2_norm_2, ffn2_w_gu_2, ffn2_w_down_2,
    )


_drawn_inputs = setup_inputs


def setup_inputs(seed=0):
    import zlib

    import numpy as np

    out = dict(_drawn_inputs(seed))
    spreads = {}
    factors = {'rel_bias': 3.27,
     'norm1_g': 8.0,
     'norm2_g': 5.325,
     'cmp_k_w1': 3.374,
     'cmp_k_w2': 3.211,
     'q_norm_g': 8.0,
     'k_norm_g': 8.0,
     'ffn1_norm_2': 2.901,
     'mix_norm_2': 2.846,
     'b_gate_2': 21.573,
     'sg_ln_g_2': 39.058,
     'sg_ln_b_2': 64.0,
     'mla_cq_norm_2': 8.0,
     'mla_ckv_norm_2': 8.0,
     'mla_q_norm_2': 8.0,
     'mla_k_norm_2': 8.0,
     'mem_norm_2': 8.0,
     'mem_q_norm_2': 8.0,
     'mem_k_norm_2': 8.0,
     'ffn2_norm_2': 10.623,
     'sg_b_2': 6.536}
    for name, (base, spread) in spreads.items():
        noise = np.random.default_rng([zlib.crc32(name.encode()), seed]).standard_normal(out[name].shape)
        drawn = base * np.exp(spread * noise) if base else spread * noise
        out[name] = __import__('jax').numpy.asarray(drawn.astype(out[name].dtype))
    for name, factor in factors.items():
        out[name] = (out[name] * factor).astype(out[name].dtype)
    return out
```

```python
from contextlib import ExitStack

import numpy as np

import concourse.bass as bass
from concourse import mybir

F32 = mybir.dt.float32
I32 = mybir.dt.int32
ACT = mybir.ActivationFunctionType
ALU = mybir.AluOpType
AX = mybir.AxisListType

P = 128
T = 256
TT = T // P
D = 1024
KD = D // P
HD = 64
DFF, DFF2 = 4096, 2816
KF, KF2 = DFF // P, DFF2 // P
NEG = -1e30
EPS = 1e-6
N_CMP = 15
CMP_STRIDE = 16
SLOT = 8
SQ = 4
RING = 8
ADA_RING = 4
BIG = 12582912.0
TWO_PI = 6.283185307179586
PI_1 = 6.28125
PI_2 = 0.0019350051879882812
PI_3 = float(np.float32(TWO_PI - PI_1 - PI_2))
PI_LIMIT = 3.1415925

C_QA, C_KC, C_VC, C_KS, C_VS, C_KW, C_VW, C_GA, C_QB, C_KB, C_VB, C_MA, C_MB = (
    0, 512, 640, 768, 896, 1024, 1152, 1280, 1304, 1816, 2328, 2840, 3864)
D_U, D_V, D_CQ, D_CKV, D_KR, D_QM, D_GATE = 0, 512, 1024, 1408, 1664, 1696, 2208


def span(first, n=P):
    return list(range(first, first + n))


def rot(cols):
    half = len(cols) // 2
    return cols[half:] + cols[:half]


def mla_q_cols(h):
    nope, rope = span(h * 96, 64), span(h * 96 + 64, 32)
    pe = rope + rot(rope)
    return nope + pe if h % 2 == 0 else pe + nope


def stream_chunks():
    out = []

    def stationary(name, cols, rows):
        for r in rows:
            out.append((name, r, cols))

    def moving(name, first, n, k):
        for kk in range(k):
            for j in range(n // P):
                out.append((name, span(kk * P), span(first + j * P)))

    full = [span(k * P) for k in range(KD)]
    half = [span(k * P) for k in range(4)]
    for b in range(4):
        stationary("mem_w_kv_2", span(b * P), full)
    moving("mem_w_kv_2", 512, 512, KD)
    for k in range(KD):
        out.append(("w_in", span(k * P), span(C_VS)))
        out.append(("w_in", span(k * P), span(C_VW)))
    moving("w_in", C_VB, 512, KD)
    for c in (C_KC, C_VC, C_KS, C_KW):
        stationary("w_in", span(c), full)
    for b in range(4):
        stationary("w_in", span(b * HD, HD) + span((4 + b) * HD, HD), full)
    for c in (C_KB, C_QB):
        for b in range(4):
            stationary("w_in", span(c + b * P), full)
    for name in ("cmp_k_w1", "cmp_v_w1"):
        for j in range(32):
            out.append((name, j, None))
    for c in (C_MA, C_MB):
        for b in range(KD):
            stationary("w_in", span(c + b * P), full)
    for m in range(KD):
        stationary("w_up_nsa", span(m * P), [span(b * HD, HD) + span((4 + b) * HD, HD) for b in range(4)])
        stationary("w_up_sb", span(m * P), half)
    for m in range(KD):
        stationary("w_out", span(m * P), full)
    for m in range(KF):
        stationary("mlp_w1", span(m * P), full)
    for m in range(KD):
        stationary("mlp_w2", span(m * P), [span(k * P) for k in range(KF)])

    def swiglu(gu, down):
        for m in range(KF2):
            stationary(gu, span(m * P), full)
            stationary(gu, span(DFF2 + m * P), full)
        for m in range(KD):
            stationary(down, span(m * P), [span(k * P) for k in range(KF2)])

    swiglu("ffn1_w_gu_2", "ffn1_w_down_2")
    for b in range(3):
        stationary("w_in_2", span(D_CQ + b * P), full)
    for b in range(2):
        stationary("w_in_2", span(D_CKV + b * P), full)
    stationary("w_in_2", 4 * span(D_KR, 32), full)
    for b in range(4):
        stationary("w_in_2", span(D_QM + b * P), full)
    for h in range(8):
        stationary("mla_w_uq_2", mla_q_cols(h), [span(k * P) for k in range(3)])
    for b in range(4):
        stationary("mla_w_ukv_2", span(2 * b * P, HD) + span((2 * b + 1) * P, HD), [span(0), span(P)])
    for k in range(2):
        for j in range(4):
            out.append(("mla_w_ukv_2", span(k * P), span(2 * j * P + HD, HD) + span((2 * j + 1) * P + HD, HD)))
    moving("w_in_2", D_V, 512, KD)
    for b in range(4):
        stationary("w_in_2", span(D_U + b * P), full)
    for b in range(24):
        stationary("w_in_2", span(D_GATE + b * P), full)
    for m in range(KD):
        for name in ("w_branch_a_2", "w_branch_b_2", "w_branch_c_2"):
            stationary(name, span(m * P), half)
    for m in range(KD):
        stationary("w_out_2", span(m * P), full)
    swiglu("ffn2_w_gu_2", "ffn2_w_down_2")
    return out


VECTORS = [("norm1_g", 8), ("norm2_g", 8), ("ffn1_norm_2", 8), ("mix_norm_2", 8), ("ffn2_norm_2", 8),
           ("mem_norm_2", 8), ("c", 8), ("ada_b", 48), ("b_gate_2", 24), ("mla_cq_norm_2", 3),
           ("mla_ckv_norm_2", 2), ("q_norm", 1), ("k_cmp_norm", 1), ("k_slc_norm", 1), ("k_win_norm", 1),
           ("mla_q_even", 1), ("mla_q_odd", 1), ("mla_k_nope", 1), ("mla_k_rope", 1), ("mem_q_norm_2", 1),
           ("mem_k_norm_2", 1), ("angle", 4), ("phase", 4), ("sees_a_block", 2), ("eps", 1)]
AT = {}
_n = 0
for _name, _k in VECTORS:
    AT[_name] = _n
    _n += _k
N_COLS = _n
ROPE_QE, ROPE_QO, ROPE_C, ROPE_S = range(4)

MATRICES = ["ident", "ones", "halves", "q_even", "q_odd", "rotate", "neg_suffix",
            "neg_ones", "before", "not_before", "not_after", "spread"]
MAT = {n: i for i, n in enumerate(MATRICES)}


def shape_constants():
    i = np.arange(P)
    k, q = i[:, None], i[None, :]
    m = np.zeros((len(MATRICES), P, P), np.float32)
    m[MAT["ident"]] = np.eye(P)
    m[MAT["ones"]] = 1
    m[MAT["halves"]] = (k // 64) == (q // 64)
    m[MAT["q_even"]] = (k < 96) + 0 * q
    m[MAT["q_odd"]] = ((k < 32) | (k >= 64)) + 0 * q
    m[MAT["rotate"]] = (k // 32 == q // 32) & ((k % 32) == (q % 32 + 16) % 32)
    m[MAT["neg_suffix"]] = -1.0 * (k >= q)
    m[MAT["neg_ones"]] = -1
    m[MAT["before"]] = k < q
    m[MAT["not_before"]] = np.where(k < q, 0, NEG)
    m[MAT["not_after"]] = np.where(q <= k, 0, NEG)
    m[MAT["spread"]] = ((k == q) | (k == N_CMP + 1)) & (q < N_CMP)
    dist = 255 - np.arange(512)
    n = np.maximum(dist, 0)
    nf = np.maximum(n, 1).astype(np.float32)
    large = 16 + (np.log(nf / np.float32(16)) / np.float32(np.log(128 / 16)) * 16).astype(np.int32)
    bucket = np.where(n < 16, n, np.minimum(large, 31))
    buckets = np.zeros((33, 512), np.float32)
    buckets[bucket, np.arange(512)] = dist >= 0
    buckets[32] = np.where(dist >= 0, 0, NEG)
    inv = (np.float32(10000.0) ** (-np.arange(16, dtype=np.float32) / np.float32(16))).astype(np.float32)
    pair = inv[i % 16]
    sign = np.where(i % 32 < 16, -1, 1)
    angle, phase = np.zeros((4, P)), np.zeros((4, P))
    half_pi = np.pi / 2
    angle[ROPE_QE] = np.where(i < 64, 0, np.where(i < 96, pair, sign * pair))
    phase[ROPE_QE] = np.where(i < 96, half_pi, 0)
    angle[ROPE_QO] = np.where(i >= 64, 0, np.where(i < 32, pair, sign * pair))
    phase[ROPE_QO] = np.where((i >= 64) | (i < 32), half_pi, 0)
    angle[ROPE_C], phase[ROPE_C] = pair, half_pi
    angle[ROPE_S] = sign * pair
    sees = np.stack([i >= CMP_STRIDE * 2 - 1, i >= 0])
    return m, buckets, {"angle": angle, "phase": phase, "sees_a_block": sees, "eps": np.full((1, P), EPS)}


def plan_psum(proj, attn, long):
    where, used = {}, [0] * 8
    for names, banks in ((proj, [0, 1, 2]), (attn, [3, 4, 5, 6]), (long, [7])):
        for n, name in enumerate(names):
            b = banks[n % len(banks)]
            assert name not in where, name
            where[name] = (b, used[b])
            used[b] += 1
    return where


def proj_names():
    out = ["mem_ss", "mem_k0", "mem_k1", "x_ss", "mem_k2", "mem_k3", "bias", "mem_v0", "mem_v1"]
    out += ["ada0a", "ada0b", "ada1a", "ada1b"]
    out += ["vsw0", "vsw1", "vsb0", "vsb1", "ga0", "ga1", "kc", "vc", "ks", "kw"]
    out += [f"qa{b}" for b in range(4)] + [f"kb{b}" for b in range(4)] + [f"qb{b}" for b in range(4)]
    out += ["ada2a", "ada2b", "ada3a", "ada3b", "cmp_hid_k", "cmp_hid_v", "ma0", "cmp_turn_k", "cmp_turn_v"]
    out += ["ma1", "cmp_out_k", "cmp_out_v", "ma2", "ma3", "ma4", "ma5", "ada4a", "ada4b", "ma6", "ma7"]
    out += ["ada5a", "ada5b"] + [f"mb{b}" for b in range(8)]
    for m in range(KD):
        out += [f"up_nsa{m}", f"up_sb{m}"]
    out += [f"mix{m}" for m in range(KD)]
    out += [f"w1_{m}" for m in range(KF)] + [f"w2_{m}" for m in range(KD)]

    def swiglu(p):
        return [f"{p}{w}{m}" for m in range(KF2) for w in "gu"] + [f"{p}d{m}" for m in range(KD)]

    out += swiglu("f1")
    out += [f"cq{b}" for b in range(3)] + [f"ckv{b}" for b in range(2)] + ["kr"] + [f"qm{b}" for b in range(4)]
    out += ["kr_rot"]
    out += [f"uq{h}" for h in range(8)] + [f"uk{b}" for b in range(4)] + ["uv0", "uv1", "sv0", "sv1"]
    out += [f"su{b}" for b in range(4)]
    out += [f"gate{b}" for b in range(24)]
    for m in range(KD):
        out += [f"br_a{m}", f"br_b{m}", f"br_c{m}"]
    out += [f"mix2_{m}" for m in range(KD)]
    out += swiglu("f2")
    return out


def attn_names():
    out = [f"ss_mem_k{b}" for b in range(4)]
    out += [f"ss_{n}" for n in ("ks", "kw", "qa0", "qa1", "qa2", "qa3")]
    out += ["sbz0", "sbz1", "sbz2", "ss_cmp"] + [f"sbz{h}" for h in range(3, 8)]
    out += ["nsa0a", "nsa0b", "nsa0c"]
    for i in range(8):
        if i < 7:
            out += [f"nsa{i + 1}{c}" for c in "abc"]
        out += [f"nsat{i}{c}" for c in "swc"]
    out += ["ss_cq", "ss_ckv"] + [f"ss_qm{b}" for b in range(4)]
    out += [f"ss_uq{h}" for h in range(8)] + [f"ss_uk{h}" for h in range(8)]
    out += ["mla0"]
    for h in range(8):
        out += [f"mla{h + 1}" if h < 7 else "mem0", f"mlat{h}"]
    for h in range(4):
        out += [f"mem{h + 1}"] * (h < 3) + [f"memt{h}"]
    out += [f"sg{b}{c}" for b in range(4) for c in range(TT)]
    return out


def long_names():
    out = [f"sbo{b}" for b in range(4)] + [f"nsao{b}" for b in range(4)] + ["x1_ss", "x2_ss", "x3_ss"]
    out += [f"mlao{b}" for b in range(4)] + [f"memo{b}" for b in range(4)] + ["x4_ss"]
    return out


ROW_MEM, ROW_X, ROW_1, ROW_2, ROW_3, ROW_4 = range(6)


def build(nc, stream, ada, x_t, mem_t, cols_d, mats_d, buckets_d, table_d, pos_d, gates_w_d, cmp_w2_d,
          cmp_pos_d, sg_w_d, sg_b_d, sg_ln_d, out_t, taps=None):
    n_slots = stream.shape[0]
    where = plan_psum(proj_names(), attn_names(), long_names())

    with ExitStack() as ctx:
        def sb(name, shape, dt=F32):
            return ctx.enter_context(nc.sbuf_tensor(name, shape, dt))

        def sem(name):
            return ctx.enter_context(nc.semaphore(name))

        psum = [ctx.enter_context(nc.psum_tensor(f"bank{b}", [P, 512], F32)) for b in range(8)]

        def flat(t):
            return t.rearrange("p a b -> p (a b)")

        def flat4(t):
            return t.rearrange("p a b c d -> p (a b c d)")

        ring = sb("ring", [P, RING * SLOT * P])
        ada_ring = sb("ada_ring", [P, ADA_RING, D])
        ada_acc = sb("ada_acc", [P, 2, D])
        mod = sb("mod", [P, 48])
        mats = sb("mats", [P, len(MATRICES), P])
        cols = sb("cols", [P, N_COLS])
        half_bias = sb("half_bias", [P, 24])
        c_act = sb("c_act", [P, 2, 8])
        x = sb("x", [P, KD, T])
        u = sb("u", [P, KD, T])
        wide = sb("wide", [P, 32, T])
        gates, merged, hidden = wide[:, 0:24, :], wide[:, 24:32, :], wide
        mem_n = wide[:, 0:8, :]
        bias_steps = wide[0:8, 8:23, :].rearrange("h a b -> h (a b)").rearrange("h (t c) -> h t c", c=N_CMP)
        squares = sb("squares", [P, SQ, T])
        log_ms = sb("log_ms", [P, T])
        rinv = sb("rinv", [P, 2, T])
        row_rinv = sb("row_rinv", [P, T])
        part = sb("part", [P, 2, T])
        mem_k = sb("mem_k", [P, 4, T])
        mem_v = sb("mem_v", [P, TT, 512])
        qa = sb("qa", [P, 4, T])
        kcat = sb("kcat", [P, 2, 528])
        vcat = sb("vcat", [P, TT, 2, 2, P])
        kc_ext = sb("kc_ext", [P, 2, 288])
        cmp_sb = sb("cmp_sb", [32, 2, P])
        cmp_tanh = sb("cmp_tanh", [P, 2, 16])
        cmp_turned = sb("cmp_turned", [P, 2, 16])
        cmp_w2 = sb("cmp_w2", [P, 2, P])
        cmp_k = sb("cmp_k", [P, 4, 16])
        vcmp = sb("vcmp", [16, 2, P])
        pair_k = sb("pair_k", [P, 8, T])
        pair_q = sb("pair_q", [P, 8, T])
        pair_v = sb("pair_v", [P, TT, 8, P])
        attn_a = sb("attn_a", [P, 4, T])
        attn_b = sb("attn_b", [P, 4, T])
        bias = sb("bias", [P, 8, T])
        attn_c = bias[:, 0:4, :]
        k_squares = bias[:, 4:8, :]
        bias_cmp = sb("bias_cmp", [P, 8, TT, N_CMP])
        bias_line = sb("bias_line", [8, 512])
        buckets = sb("buckets", [33, 512])
        table = sb("table", [33, 8])
        gates_w = sb("gates_w", [P, KD, 24])
        gate_raw = sb("gate_raw", [P, TT, 24])
        gate_tanh = sb("gate_tanh", [P, TT, 24])
        gate_t = sb("gate_t", [P, 8, 6])
        sbw = flat(wide[:, 16:28, :]).rearrange("p (a b c) -> p a b c", a=2, b=4)
        logit = flat(wide[:, 24:32, :])[:, 0:1600].rearrange("p (a b) -> p a b", a=2)
        ada_flat = flat(ada_acc[:, :, :])
        latent = ada_flat[:, 0:1280].rearrange("p (b t) -> p b t", t=T)
        kr = ada_flat[:, 1280:1792].rearrange("p (b t) -> p b t", t=T)
        pos = ada_flat[:, 1792:2048]
        sg_v = flat4(vcat[:, :, :, :, :])[:, 0:1024].rearrange("p (t c) -> p t c", t=TT)
        stats = sb("stats", [P, 2, 4, 6])
        turned = sb("turned", [P, 2, 2, 512])
        turned_c = sb("turned_c", [16, 2, T])
        row_squares = turned[:, :, :, :].rearrange("p a b c -> p (a b c)").rearrange("p (k t) -> p k t", t=T)
        pos_i = sb("pos_i", [P, T], I32)
        rope_n = row_squares[:, 0:4, :]
        rope = ada_ring[:, 0, :].rearrange("p (b t) -> p b t", t=T)
        sg_w = ada_ring[:, 1, :].rearrange("p (g t) -> p g t", t=P)
        sg_ln = ada_ring[:, 2, :].rearrange("p (w f) -> p w f", w=2)
        sg_b = ada_ring[0:1, 3, :]
        sg_stat = sb("sg_stat", [P, TT, 12])

        slot_full = [sem(f"slot_full{i}") for i in range(RING)]
        slot_used = sem("slot_used")
        ada_full = [sem(f"ada_full{i}") for i in range(ADA_RING)]
        ada_used = sem("ada_used")
        bank_full = [sem(f"bank_full{b}") for b in range(8)]
        bank_free = [sem(f"bank_free{b}") for b in range(8)]
        loaded = {n: sem(f"loaded_{n}") for n in ("x", "mem", "cols", "mats", "bias_in", "small", "pos", "sg", "bias")}
        stored = sem("stored")
        c_tanh_ready, c_ready = sem("c_tanh_ready"), sem("c_ready")
        zeros_ready, lines_ready, sg_w_ready = sem("zeros_ready"), sem("lines_ready"), sem("sg_w_ready")
        squares_ready, k_squares_ready = sem("squares_ready"), sem("k_squares_ready")
        row_squares_ready, row_rinv_ready = sem("row_squares_ready"), sem("row_rinv_ready")
        rinv_ready, log_ready, normed = sem("rinv_ready"), sem("log_ready"), sem("normed")
        u_normed, u_modulated, u_ready = sem("u_normed"), sem("u_modulated"), sem("u_ready")
        ada_summed, mod_ready, half_bias_ready = sem("ada_summed"), sem("mod_ready"), sem("half_bias_ready")
        gates_tanh_ready, gate_t_ready, tanh_ready = sem("gates_tanh_ready"), sem("gate_t_ready"), sem("tanh_ready")
        cmp_tanh_ready, cmp_rinv_ready, cmp_k_ready = sem("cmp_tanh_ready"), sem("cmp_rinv_ready"), sem("cmp_k_ready")
        sb_log_ready, softplus_ready, sb_logits_ready = sem("sb_log_ready"), sem("softplus_ready"), sem("sb_logits_ready")
        logits_ready, weights_raw, weights_ready = sem("logits_ready"), sem("weights_raw"), sem("weights_ready")
        merged_ready, relu_ready, hidden_ready, silu_ready = (
            sem("merged_ready"), sem("relu_ready"), sem("hidden_ready"), sem("silu_ready"))
        latent_ready, k_pe_ready = sem("latent_ready"), sem("k_pe_ready")
        rope_angle_ready, rope_ready = sem("rope_angle_ready"), sem("rope_ready")
        sg_var_ready, sg_dev_ready, sg_ln_ready = sem("sg_var_ready"), sem("sg_dev_ready"), sem("sg_ln_ready")
        act_step, dve_step = sem("act_step"), sem("dve_step")

        def full(eng, name):
            b, k = where[name]
            eng.wait_ge(bank_full[b], k + 1)

        def evacuated(eng, name):
            b, k = where[name]
            eng.wait_ge(bank_free[b], k + 1)

        def bank(name):
            return psum[where[name][0]]

        def free(ins, name):
            ins.then_inc(bank_free[where[name][0]], 1)

        def mat(name):
            return mats[:, MAT[name], :]

        def col(name, i=0, rows=slice(0, P)):
            return cols[rows, AT[name] + i:AT[name] + i + 1]

        def chain(eng, s):
            n = [0]

            def step(ins):
                n[0] += 1
                ins.then_inc(s, 1)
                eng.wait_ge(s, n[0])
            return step

        LO, HI = slice(0, 64), slice(64, P)
        block = ctx.enter_context(nc.Block())

        @block.sync
        def _(sp):
            def load(r, i):
                sp.dma_start(ring[:, r * SLOT * P:(r + 1) * SLOT * P], stream[i]).then_inc(slot_full[r], 16)

            sp.dma_start(cols[:, :], cols_d).then_inc(loaded["cols"], 16)
            sp.dma_start(mem_n, mem_t).then_inc(loaded["mem"], 16)
            sp.dma_start(mats[:, :, :], mats_d).then_inc(loaded["mats"], 16)
            for r in range(RING):
                load(r, r)
                if r == 1:
                    sp.dma_start(x[:, :, :], x_t).then_inc(loaded["x"], 16)
                if r == 3:
                    sp.dma_start(buckets[:, :], buckets_d).then_inc(loaded["bias_in"], 16)
                    sp.dma_start(table[:, :], table_d).then_inc(loaded["bias_in"], 16)
            sp.dma_start(gates_w[:, :, :], gates_w_d).then_inc(loaded["small"], 16)
            sp.dma_start(cmp_w2[:, :, :], cmp_w2_d).then_inc(loaded["small"], 16)
            for w in range(2):
                sp.dma_start(kc_ext[:, w, T:T + 32], cmp_pos_d).then_inc(loaded["small"], 16)
            sp.dma_start(pos_i[:, :], pos_d).then_inc(loaded["pos"], 16)
            rounds = n_slots // RING
            with sp.Fori(1, rounds) as i:
                for r in range(RING):
                    sp.wait_ge(slot_used, i * RING + (r + 1 - RING))
                    load(r, i * RING + r)
            for n in range(rounds * RING, n_slots):
                sp.wait_ge(slot_used, n + 1 - RING)
                load(n % RING, n)
            for m in range(KD):
                evacuated(sp, f"f2d{m}")
                sp.dma_start(out_t[:, m, :], x[:, m, :]).then_inc(stored, 16)
            sp.wait_ge(stored, 16 * KD)

        @block.gpsimd
        def _(pool):
            def load_ada(n):
                if n >= ADA_RING:
                    pool.wait_ge(ada_used, n - ADA_RING + 1)
                pool.dma_start(ada_ring[:, n % ADA_RING, :], ada[n]).then_inc(ada_full[n % ADA_RING], 16)

            for n in range(ADA_RING):
                load_ada(n)
            for t in (kcat, vcat, pair_k, pair_v, vcmp, kc_ext[:, :, 0:T]):
                pool.memset(t[:], 0.0).then_inc(zeros_ready, 1)
            for n in range(ADA_RING, 16):
                load_ada(n)
            evacuated(pool, "bias")
            for c in range(N_CMP):
                first = 2 * CMP_STRIDE - 1 + CMP_STRIDE * c
                last = pool.tensor_copy(bias_steps[:, :, c], bias_line[:, first:first + T])
            last.then_inc(lines_ready, 1)
            pool.wait_ge(lines_ready, 1)
            for h in range(8):
                line = bias_line[h:h + 1, :]
                pool.dma_start(bias[:, h, :], bass.AP(line.tensor, line.offset + P - 1, [[line.ap[0][0], 1], [-1, P], [1, T]])
                               ).then_inc(loaded["bias"], 16)
                step = bias_steps[h:h + 1, :, :]
                for t in range(TT):
                    pool.dma_start(bias_cmp[:, h, t, :],
                                   bass.AP(step.tensor, step.offset + (T - 1 - t * P) * N_CMP,
                                           [[step.ap[0][0], 1], [-N_CMP, P], [1, N_CMP]])).then_inc(loaded["bias"], 16)
            for n in range(16, 48):
                load_ada(n)
            pool.wait_ge(ada_used, 48)
            pool.dma_start(sg_w[:, :, :], sg_w_d).then_inc(loaded["sg"], 16)
            pool.dma_start(sg_b[:, :], sg_b_d).then_inc(loaded["sg"], 16)
            pool.dma_start(sg_ln[:, :, :], sg_ln_d).then_inc(loaded["sg"], 16)
            pool.wait_ge(loaded["sg"], 48)
            pool.affine_select(out=sg_w[:, :, :], in_=sg_w[:, :, :], compare_op=ALU.is_ge, fill=0.0, base=0,
                               pattern=[[0, 8], [1, P]], channel_multiplier=-1).then_inc(sg_w_ready, 1)

        @block.tensor
        def _(pe):
            at = {"chunk": 0, "owed": 0, "squares": 0}

            def mm(out, lhs, rhs, start=False, stop=False):
                return nc.tensor.matmul(out, lhs, rhs, start=start, stop=stop, skip_group_check=True)

            def claim(name):
                b, k = where[name]
                if k:
                    pe.wait_ge(bank_free[b], k)
                return psum[b]

            def done(ins, name):
                ins.then_inc(bank_full[where[name][0]], 1)

            def take(n=1):
                c = at["chunk"]
                if c % SLOT == 0:
                    i = c // SLOT
                    pe.wait_ge(slot_full[i % RING], 16 * (i // RING + 1))
                at["chunk"] = c + n
                c %= RING * SLOT
                return ring[:, c * P:(c + n) * P]

            def give_back(ins, chunk):
                n = chunk // SLOT - at["owed"]
                if n:
                    ins.then_inc(slot_used, n)
                    at["owed"] += n

            def project(name, k, rhs, ready=None):
                ps = claim(name)
                for i in range(k):
                    chunk = at["chunk"]
                    w = take()
                    if ready:
                        ready(i)
                    ins = mm(ps[:, 0:T], w, rhs[:, i, :], i == 0, i == k - 1)
                    if i < k - 1:
                        give_back(ins, chunk)
                done(ins, name)

            def project_tokens(names, k, lhs, width):
                ps = [claim(n) for n in names]
                for i in range(k):
                    chunk = at["chunk"]
                    w = take(width // P)
                    for t in range(TT):
                        ins = mm(ps[t][:, 0:width], lhs[:, i, t * P:(t + 1) * P], w, i == 0, i == k - 1)
                        if i < k - 1 and t == 0:
                            give_back(ins, chunk)
                        if i == k - 1:
                            done(ins, names[t])

            def sum_squares(name, matrix, n=1):
                ps = claim("ss_" + name)
                for i in range(n):
                    q = at["squares"]
                    at["squares"] += 1
                    pe.wait_ge(squares_ready, q + 1)
                    ins = mm(ps[:, 0:T], mat(matrix), squares[:, q % SQ, :], i == 0, i == n - 1)
                done(ins, "ss_" + name)

            def sum_row(name, row, src):
                ps = claim(name)
                for i in range(KD):
                    pe.wait_ge(row_squares_ready, row * KD + i + 1)
                    ins = mm(ps[:, 0:T], mat("ones"), src[:, i, :], i == 0, i == KD - 1)
                done(ins, name)

            def ada_part(j):
                pe.wait_ge(ada_summed, j + 1)
                for half in range(2):
                    name = f"ada{j}{'ab'[half]}"
                    ps = claim(name)
                    for i in range(4):
                        c = (half * 4 + i) * P
                        ins = nc.tensor.transpose(ps[:, i * P:(i + 1) * P], ada_acc[:, j % 2, c:c + P], mat("ident"))
                    done(ins, name)

            pe.wait_ge(loaded["mats"], 16)
            sum_row("mem_ss", ROW_MEM, row_squares)
            project("mem_k0", KD, mem_n, lambda i: pe.wait_ge(u_ready, i + 1))
            project("mem_k1", KD, mem_n)
            sum_squares("mem_k0", "ones")
            sum_row("x_ss", ROW_X, merged)
            project("mem_k2", KD, mem_n)
            sum_squares("mem_k1", "ones")
            project("mem_k3", KD, mem_n)
            sum_squares("mem_k2", "ones")
            pe.wait_ge(loaded["bias_in"], 32)
            done(mm(claim("bias")[0:8, 0:512], table[:, :], buckets[:, :], True, True), "bias")
            sum_squares("mem_k3", "ones")
            project_tokens(["mem_v0", "mem_v1"], KD, mem_n, 512)
            ada_part(0)
            ada_part(1)

            pe.wait_ge(u_modulated, KD)
            project_tokens(["vsw0", "vsw1"], KD, u, 256)
            project_tokens(["vsb0", "vsb1"], KD, u, 512)
            pe.wait_ge(loaded["small"], 64)
            for t in range(TT):
                ps = claim(f"ga{t}")
                for k in range(KD):
                    ins = mm(ps[:, 0:24], u[:, k, t * P:(t + 1) * P], gates_w[:, k, :], k == 0, k == KD - 1)
                done(ins, f"ga{t}")
            for n in ("kc", "vc", "ks", "kw"):
                project(n, KD, u)
            sum_squares("ks", "halves")
            for b in range(4):
                project(f"qa{b}", KD, u)
                sum_squares(f"qa{b - 1}" if b else "kw", "halves")
            for b in range(4):
                project(f"kb{b}", KD, u)
                if b == 0:
                    sum_squares("qa3", "halves")
            for b in range(4):
                project(f"qb{b}", KD, u)
            ada_part(2)
            ada_part(3)

            for w, n in enumerate("kv"):
                evacuated(pe, n + "c" if n == "v" else "kc")
                name = f"cmp_hid_{n}"
                ps = claim(name)
                for j in range(32):
                    chunk = at["chunk"]
                    ins = mm(ps[0:N_CMP + 2, 0:P], kc_ext[:, w, j:j + 257:CMP_STRIDE], take(), j == 0, j == 31)
                    if j < 31:
                        give_back(ins, chunk)
                done(ins, name)

            def cmp_turn():
                for w, n in enumerate("kv"):
                    evacuated(pe, f"cmp_hid_{n}")
                    ps = claim(f"cmp_turn_{n}")
                    done(mm(ps[:, 0:N_CMP], cmp_sb[0:N_CMP + 2, w, :], mats[0:N_CMP + 2, MAT["spread"], 0:N_CMP],
                            True, True), f"cmp_turn_{n}")

            def cmp_out():
                evacuated(pe, "cmp_turn_k")
                ps = claim("cmp_out_k")
                done(mm(ps[:, 0:N_CMP], cmp_w2[:, 0, :], cmp_turned[:, 0, 0:N_CMP], True, True), "cmp_out_k")
                evacuated(pe, "cmp_turn_v")
                ps = claim("cmp_out_v")
                done(mm(ps[0:N_CMP, 0:P], cmp_turned[:, 1, 0:N_CMP], cmp_w2[:, 1, :], True, True), "cmp_out_v")

            def cmp_sum():
                evacuated(pe, "cmp_out_k")
                done(mm(claim("ss_cmp")[:, 0:N_CMP], mat("halves"), cmp_k[:, 1, 0:N_CMP], True, True), "ss_cmp")

            def sb_scores(h):
                evacuated(pe, f"kb{h // 2}")
                evacuated(pe, f"qb{h // 2}")
                ps = claim(f"sbz{h}")
                mm(ps[:, 0:T], pair_k[:, h, 0:P], pair_q[:, h // 2, :], True)
                done(mm(ps[:, T:T + P], pair_k[:, h, P:T], pair_q[:, h // 2, P:T], stop=True), f"sbz{h}")

            def sb_logits(h):
                pe.wait_ge(softplus_ready, h + 1)
                ps = bank(f"sbz{h}")
                soft = sbw[:, h % 2, 2, :]
                mm(ps[:, 0:T], mat("neg_suffix"), soft[:, 0:T])
                mm(ps[:, P:T], mat("neg_ones"), soft[:, T:T + P])
                mm(ps[:, T:T + P], mat("neg_suffix"), soft[:, T:T + P])
                mm(ps[:, 0:P], mat("ident"), mat("not_before"))
                mm(ps[:, T:T + P], mat("ident"), mat("not_before"), stop=True).then_inc(sb_logits_ready, 1)

            def sb_values(h):
                evacuated(pe, f"sbz{h}")
                name = f"sbo{h // 2}"
                ps = claim(name) if h % 2 == 0 else bank(name)
                w = sbw[:, h % 2, 3, :]
                mm(ps[:, 0:T], pair_v[:, 0, h, :], w[:, 0:T], h % 2 == 0)
                ins = mm(ps[:, P:T], pair_v[:, 1, h, :], w[:, T:T + P], stop=h % 2 == 1)
                if h % 2 == 1:
                    done(ins, name)

            evacuated(pe, "vsb0")
            evacuated(pe, "vsb1")
            sb_scores(0)
            for h in range(8):
                project(f"ma{h}", KD, u)
                if h == 0:
                    cmp_turn()
                if h == 1:
                    cmp_out()
                if h == 2:
                    cmp_sum()
                if h == 5:
                    ada_part(4)
                if h < 7:
                    sb_scores(h + 1)
                sb_logits(h)
                if h:
                    sb_values(h - 1)
            sb_values(7)
            ada_part(5)

            def nsa_scores(i):
                b, s = i // 2, i % 2
                for c, q, k in (("a", slice(0, P), slice(0, 272)), ("b", slice(P, T), slice(0, 272)),
                                ("c", slice(P, T), slice(272, 528))):
                    ps = claim(f"nsa{i}{c}")
                    done(mm(ps[:, 0:k.stop - k.start], qa[:, b, q], kcat[:, s, k], True, True), f"nsa{i}{c}")

            def turn_block(ps, at_col, src):
                return nc.tensor.transpose(ps[:, at_col:at_col + P], src, mat("ident"))

            def nsa_turn(i):
                pe.wait_ge(weights_ready, i + 1)
                w = logit[:, i % 2, :]
                for br, c in enumerate("sw"):
                    ps = claim(f"nsat{i}{c}")
                    late = T + br * T
                    turn_block(ps, 0, w[:, br * P:(br + 1) * P])
                    turn_block(ps, P, w[:, late:late + P])
                    done(turn_block(ps, T, w[:, late + P:late + T]), f"nsat{i}{c}")
                ps = claim(f"nsat{i}c")
                turn_block(ps[0:N_CMP], 0, w[:, 768:768 + N_CMP])
                done(turn_block(ps[0:N_CMP], P, w[:, 784:784 + N_CMP]), f"nsat{i}c")

            def nsa_values(i):
                b, s = i // 2, i % 2
                name = f"nsao{b}"
                ps = claim(name) if s == 0 else bank(name)
                for br, c in enumerate("sw"):
                    evacuated(pe, f"nsat{i}{c}")
                    w = turned[:, i % 2, br, :]
                    mm(ps[:, 0:T], vcat[:, 0, br, s, :], w[:, 0:T], s == 0 and br == 0)
                    mm(ps[:, P:T], vcat[:, 1, br, s, :], w[:, T:T + P])
                evacuated(pe, f"nsat{i}c")
                ins = mm(ps[:, 0:T], vcmp[0:N_CMP, s, :], turned_c[0:N_CMP, i % 2, :], stop=s == 1)
                if s == 1:
                    done(ins, name)

            for n in ("vsw0", "vsw1", "ks", "kw", "qa0", "qa1", "qa2", "qa3", "cmp_out_v"):
                evacuated(pe, n)
            pe.wait_ge(cmp_k_ready, 1)
            nsa_scores(0)
            for i in range(8):
                project(f"mb{i}", KD, u)
                if i < 7:
                    nsa_scores(i + 1)
                if i:
                    nsa_values(i - 1)
                nsa_turn(i)
            nsa_values(7)

            for m in range(KD):
                project(f"up_nsa{m}", 4, attn_a, (lambda i: evacuated(pe, f"nsao{i}")) if m == 0 else None)
                project(f"up_sb{m}", 4, attn_b, (lambda i: evacuated(pe, f"sbo{i}")) if m == 0 else None)
            for m in range(KD):
                project(f"mix{m}", KD, merged, (lambda i: pe.wait_ge(merged_ready, i + 1)) if m == 0 else None)

            sum_row("x1_ss", ROW_1, row_squares)
            for m in range(KF):
                project(f"w1_{m}", KD, u, (lambda i: pe.wait_ge(u_modulated, KD + i + 1)) if m == 0 else None)
            for m in range(KD):
                project(f"w2_{m}", KF, hidden, (lambda i: pe.wait_ge(hidden_ready, i + 1)) if m == 0 else None)

            def swiglu(p, stage):
                for m in range(KF2):
                    for w in "gu":
                        first = m == 0 and w == "g"
                        project(f"{p}{w}{m}", KD, u, (lambda i: pe.wait_ge(u_ready, stage * KD + i + 1)) if first else None)
                for m in range(KD):
                    project(f"{p}d{m}", KF2, hidden, (lambda i: evacuated(pe, f"{p}u{i}")) if m == 0 else None)

            sum_row("x2_ss", ROW_2, row_squares)
            swiglu("f1", 1)

            sum_row("x3_ss", ROW_3, row_squares)
            for b in range(3):
                project(f"cq{b}", KD, u, (lambda i: pe.wait_ge(u_ready, 2 * KD + i + 1)) if b == 0 else None)
            for b in range(2):
                project(f"ckv{b}", KD, u)
            sum_squares("cq", "ones", 3)
            project("kr", KD, u)
            sum_squares("ckv", "ones", 2)
            project("qm0", KD, u)
            project("qm1", KD, u)
            sum_squares("qm0", "ones")
            project("qm2", KD, u)
            sum_squares("qm1", "ones")
            project("qm3", KD, u)
            sum_squares("qm2", "ones")
            evacuated(pe, "kr")
            done(mm(claim("kr_rot")[:, 0:T], mat("rotate"), kr[:, 0, :], True, True), "kr_rot")
            for h in range(8):
                project(f"uq{h}", 3, latent, (lambda i: pe.wait_ge(latent_ready, i + 1)) if h == 0 else None)
                if h == 0:
                    sum_squares("qm3", "ones")
                else:
                    sum_squares(f"uq{h - 1}", "q_odd" if (h - 1) % 2 else "q_even")

            def sum_k_squares(b):
                for h in (2 * b, 2 * b + 1):
                    pe.wait_ge(k_squares_ready, h + 1)
                    done(mm(claim(f"ss_uk{h}")[:, 0:T], mat("ones"), k_squares[:, 2 * (h % 2) + b % 2, :], True, True),
                         f"ss_uk{h}")

            for b in range(4):
                project(f"uk{b}", 2, latent[:, 3:5, :], (lambda i: pe.wait_ge(latent_ready, 4 + i)) if b == 0 else None)
                if b == 0:
                    sum_squares("uq7", "q_odd")
                else:
                    sum_k_squares(b - 1)
            sum_k_squares(3)
            project_tokens(["uv0", "uv1"], 2, latent[:, 3:5, :], 512)
            project_tokens(["sv0", "sv1"], KD, u, 512)
            for b in range(4):
                project(f"su{b}", KD, u)

            def scores(i):
                if i < 8:
                    ps = claim(f"mla{i}")
                    mm(ps[:, 0:P], pair_q[:, i, 0:P], pair_k[:, i, 0:P], True)
                    done(mm(ps[:, P:384], pair_q[:, i, P:T], pair_k[:, i, :], stop=True), f"mla{i}")
                else:
                    h = i - 8
                    evacuated(pe, f"qm{h}")
                    evacuated(pe, f"mem_k{h}")
                    ps = claim(f"mem{h}")
                    mm(ps[:, 0:T], qa[:, h, 0:P], mem_k[:, h, :], True)
                    done(mm(ps[:, T:2 * T], qa[:, h, P:T], mem_k[:, h, :], stop=True), f"mem{h}")

            def turn(i):
                pe.wait_ge(weights_ready, 8 + i + 1)
                w = logit[:, i % 2, :]
                if i < 8:
                    ps = claim(f"mlat{i}")
                    for j in range(3):
                        ins = turn_block(ps, j * P, w[:, j * P:(j + 1) * P])
                    done(ins, f"mlat{i}")
                else:
                    ps = claim(f"memt{i - 8}")
                    for kt in range(2):
                        for qt in range(2):
                            j = qt * 2 + kt
                            ins = turn_block(ps, (kt * 2 + qt) * P, w[:, j * P:(j + 1) * P])
                    done(ins, f"memt{i - 8}")

            def values(i):
                w = turned[:, i % 2, 0, :]
                if i < 8:
                    evacuated(pe, f"mlat{i}")
                    name = f"mlao{i // 2}"
                    ps = claim(name) if i % 2 == 0 else bank(name)
                    mm(ps[:, 0:T], pair_v[:, 0, i, :], w[:, 0:T], i % 2 == 0)
                    ins = mm(ps[:, P:T], pair_v[:, 1, i, :], w[:, T:T + P], stop=i % 2 == 1)
                    if i % 2:
                        done(ins, name)
                else:
                    h = i - 8
                    evacuated(pe, f"memt{h}")
                    ps = claim(f"memo{h}")
                    mm(ps[:, 0:T], mem_v[:, 0, h * P:(h + 1) * P], w[:, 0:T], True)
                    done(mm(ps[:, 0:T], mem_v[:, 1, h * P:(h + 1) * P], w[:, T:2 * T], stop=True), f"memo{h}")

            for n in ("uv0", "uv1", "mem_v0", "mem_v1"):
                evacuated(pe, n)
            pe.wait_ge(normed, 16)
            scores(0)
            for i in range(12):
                project(f"gate{2 * i}", KD, u)
                project(f"gate{2 * i + 1}", KD, u)
                if i < 11:
                    scores(i + 1)
                if i:
                    values(i - 1)
                turn(i)
            pe.wait_ge(sg_ln_ready, TT)
            pe.wait_ge(sg_w_ready, 1)
            for b in range(4):
                for c in range(TT):
                    name = f"sg{b}{c}"
                    ps = claim(name)
                    mm(ps[:, 0:T], sg_v[:, c, b * P:(b + 1) * P], sg_w[:, 2 * b:2 * b + 2, :], True)
                    done(mm(ps[:, 0:T], mats[0:1, MAT["ones"], :], sg_b[0:1, b * T:(b + 1) * T], stop=True), name)
            values(11)

            for b in range(4):
                for c in range(TT):
                    evacuated(pe, f"sg{b}{c}")
            for m in range(KD):
                project(f"br_a{m}", 4, attn_a)
                project(f"br_b{m}", 4, attn_b, (lambda i: evacuated(pe, f"mlao{i}")) if m == 0 else None)
                project(f"br_c{m}", 4, attn_c, (lambda i: evacuated(pe, f"memo{i}")) if m == 0 else None)
            for m in range(KD):
                project(f"mix2_{m}", KD, merged, (lambda i: pe.wait_ge(merged_ready, KD + i + 1)) if m == 0 else None)
            sum_row("x4_ss", ROW_4, row_squares)
            swiglu("f2", 3)

        @block.scalar
        def _(act):
            n_squares, n_rinv, n_row = [0], [0], [0]
            step = chain(act, act_step)
            a = nc.scalar.activation

            def square(name):
                n = n_squares[0]
                n_squares[0] += 1
                full(act, name)
                a(squares[:, n % SQ, :], bank(name)[:, 0:T], ACT.Square).then_inc(squares_ready, 1)

            def inv_rms(name, width, last_reader):
                n = n_rinv[0]
                n_rinv[0] += 1
                full(act, "ss_" + name)
                free(a(log_ms[:, :], bank("ss_" + name)[:, 0:T], ACT.Ln, scale=1.0 / width, bias=col("eps")), "ss_" + name)
                evacuated(act, "ss_" + name)
                if last_reader:
                    last_reader()
                a(rinv[:, n % 2, :], log_ms[:, :], ACT.Exp, scale=-0.5).then_inc(rinv_ready, 1)
                act.wait_ge(rinv_ready, n + 1)

            def row_square(dst, src, ready=None):
                for i in range(KD):
                    if ready:
                        ready(i)
                    a(dst[:, i, :], src[:, i, :], ACT.Square).then_inc(row_squares_ready, 1)

            def row_inv(name):
                n_row[0] += 1
                full(act, name)
                free(a(log_ms[:, :], bank(name)[:, 0:T], ACT.Ln, scale=1.0 / D, bias=col("eps")), name)
                evacuated(act, name)
                a(row_rinv[:, :], log_ms[:, :], ACT.Exp, scale=-0.5).then_inc(row_rinv_ready, 1)
                act.wait_ge(row_rinv_ready, n_row[0])

            def modulate(first, scale, shift):
                for i in range(KD):
                    act.wait_ge(u_normed, first + i + 1)
                    a(u[:, i, :], u[:, i, :], ACT.Identity, scale=mod[:, scale * 8 + i:scale * 8 + i + 1],
                      bias=mod[:, shift * 8 + i:shift * 8 + i + 1]).then_inc(u_modulated, 1)

            def copy(dst, name, src=None, **kw):
                full(act, name)
                free(a(dst, bank(name)[:, 0:T] if src is None else src, ACT.Copy, **kw), name)

            def spread_heads(dst, name):
                full(act, name)
                src = bank(name)[:, :].rearrange("p (b s d) -> p b s d", s=2, d=HD)
                dst = dst.rearrange("p (b s) c -> p b s c", s=2)
                a(dst[:, :, 0, 0:HD], src[:, :, 0, :], ACT.Copy)
                free(a(dst[:, :, 1, HD:P], src[:, :, 1, :], ACT.Copy), name)

            nc.scalar.preload_act_table_set("exp_and_others")
            act.wait_ge(loaded["cols"], 16)
            a(c_act[:, 0, :], cols[:, AT["c"]:AT["c"] + 8], ACT.Tanh, scale=0.5).then_inc(c_tanh_ready, 1)
            nc.scalar.preload_act_table_set("natural_log_exp_and_others")
            act.wait_ge(loaded["mem"], 16)
            row_square(row_squares, mem_n)
            row_inv("mem_ss")
            square("mem_k0")
            act.wait_ge(loaded["x"], 16)
            row_square(merged, x)
            square("mem_k1")
            inv_rms("mem_k0", P, None)
            act.wait_ge(u_ready, KD)
            row_inv("x_ss")
            square("mem_k2")
            inv_rms("mem_k1", P, None)
            square("mem_k3")
            inv_rms("mem_k2", P, lambda: evacuated(act, "mem_k0"))
            inv_rms("mem_k3", P, lambda: evacuated(act, "mem_k1"))
            for t in range(TT):
                copy(mem_v[:, t, :], f"mem_v{t}", bank(f"mem_v{t}")[:, :])
            act.wait_ge(mod_ready, 2)
            modulate(0, 1, 0)

            act.wait_ge(zeros_ready, 6)
            for t in range(TT):
                full(act, f"vsw{t}")
                src = bank(f"vsw{t}")[:, 0:256].rearrange("p (r s d) -> p r s d", r=2, d=HD)
                a(vcat[:, t, :, 0, 0:HD], src[:, :, 0, :], ACT.Copy)
                free(a(vcat[:, t, :, 1, HD:P], src[:, :, 1, :], ACT.Copy), f"vsw{t}")
            for t in range(TT):
                spread_heads(pair_v[:, t, :, :], f"vsb{t}")
            for t in range(TT):
                copy(gate_raw[:, t, :], f"ga{t}", bank(f"ga{t}")[:, 0:24])
            for w, n in enumerate(("kc", "vc")):
                copy(kc_ext[:, w, 0:T], n)
            square("ks")
            square("kw")
            inv_rms("ks", HD, lambda: evacuated(act, "mem_k2"))
            for b in range(4):
                square(f"qa{b}")
                inv_rms(f"qa{b - 1}" if b else "kw", HD, lambda: evacuated(act, ("mem_k3", "ks", "kw", "qa0")[b]))
            inv_rms("qa3", HD, lambda: evacuated(act, "qa1"))
            for b in range(4):
                copy(pair_q[:, b, :], f"qb{b}", scale=HD ** -0.5)
            for w, n in enumerate("kv"):
                copy(cmp_sb[0:N_CMP + 2, w, :], f"cmp_hid_{n}", bank(f"cmp_hid_{n}")[0:N_CMP + 2, 0:P])

            def sb_log(h):
                full(act, f"sbz{h}")
                w = sbw[:, h % 2, :, :]
                step(a(w[:, 0, :], bank(f"sbz{h}")[:, 0:384], ACT.Abs))
                step(a(w[:, 0, :], w[:, 0, :], ACT.Exp, scale=-1.0))
                a(w[:, 1, :], w[:, 0, :], ACT.Ln, bias=1.0).then_inc(sb_log_ready, 1)

            def sb_exp(h):
                act.wait_ge(sb_logits_ready, h + 1)
                free(a(sbw[:, h % 2, 3, :], bank(f"sbz{h}")[:, 0:384], ACT.Exp), f"sbz{h}")

            sb_log(0)
            act.wait_ge(loaded["bias"], 16 * 24)
            for h in range(8):
                copy(gates[:, h, :], f"ma{h}")
                if h == 0:
                    nc.scalar.preload_act_table_set("exp_and_others")
                    for w, n in enumerate("kv"):
                        full(act, f"cmp_turn_{n}")
                        a(cmp_tanh[:, w, 0:N_CMP], bank(f"cmp_turn_{n}")[:, 0:N_CMP], ACT.Tanh, scale=0.5).then_inc(cmp_tanh_ready, 1)
                    evacuated(act, "ga1")
                    a(gate_tanh[:, :, :], gate_raw[:, :, :], ACT.Tanh, scale=0.5).then_inc(gates_tanh_ready, 1)
                    nc.scalar.preload_act_table_set("natural_log_exp_and_others")
                if h == 1:
                    full(act, "cmp_out_k")
                    a(cmp_k[:, 0, 0:N_CMP], bank("cmp_out_k")[:, 0:N_CMP], ACT.Copy)
                    free(a(cmp_k[:, 1, 0:N_CMP], bank("cmp_out_k")[:, 0:N_CMP], ACT.Square), "cmp_out_k")
                    full(act, "cmp_out_v")
                    ps = bank("cmp_out_v")
                    a(vcmp[0:N_CMP, 0, 0:HD], ps[0:N_CMP, 0:HD], ACT.Copy)
                    free(a(vcmp[0:N_CMP, 1, HD:P], ps[0:N_CMP, HD:P], ACT.Copy), "cmp_out_v")
                if h == 2:
                    full(act, "ss_cmp")
                    free(a(cmp_k[:, 2, 0:N_CMP], bank("ss_cmp")[:, 0:N_CMP], ACT.Ln, scale=1.0 / HD, bias=col("eps")), "ss_cmp")
                    evacuated(act, "ss_cmp")
                    a(cmp_k[:, 3, 0:N_CMP], cmp_k[:, 2, 0:N_CMP], ACT.Exp, scale=-0.5).then_inc(cmp_rinv_ready, 1)
                if h < 7:
                    sb_log(h + 1)
                sb_exp(h)
                if h and h % 2 == 0:
                    copy(attn_b[:, h // 2 - 1, :], f"sbo{h // 2 - 1}")
            copy(attn_b[:, 3, :], "sbo3")

            def exps(i, parts):
                act.wait_ge(logits_ready, i + 1)
                for k, (src, dst) in parts.items():
                    ins = a(dst, src, ACT.Exp, bias=stats[:, i % 2, 0, k:k + 1], accum_out=stats[:, i % 2, 1, k:k + 1])
                ins.then_inc(weights_raw, 1)

            def nsa_exp(i):
                w = logit[:, i % 2, :]
                at = [w[:, 0:128], w[:, 128:256], w[:, 256:512], w[:, 512:768], w[:, 768:768 + N_CMP], w[:, 784:784 + N_CMP]]
                exps(i, {k: (s, s) for k, s in enumerate(at)})

            nc.scalar.preload_act_table_set("exp_and_others")
            nsa_exp(0)
            for i in range(8):
                full(act, f"mb{i}")
                free(a(gates[:, 8 + i, :], bank(f"mb{i}")[:, 0:T], ACT.Tanh, scale=0.5), f"mb{i}")
                if i % 2 == 0:
                    k = i
                    evacuated(act, f"ma{k + 1}")
                    a(gates[:, k:k + 2, :], gates[:, k:k + 2, :], ACT.Tanh, scale=0.5).then_inc(tanh_ready, 1)
                if i < 7:
                    nsa_exp(i + 1)
                if i and i % 2 == 0:
                    copy(attn_a[:, i // 2 - 1, :], f"nsao{i // 2 - 1}")
                copy(turned[:, i % 2, 0, 0:384], f"nsat{i}s", bank(f"nsat{i}s")[:, 0:384])
                copy(turned_c[0:N_CMP, i % 2, :], f"nsat{i}c", bank(f"nsat{i}c")[0:N_CMP, 0:T])
            copy(attn_a[:, 3, :], "nsao3")

            nc.scalar.preload_act_table_set("natural_log_exp_and_others")
            row_square(row_squares, x, lambda i: evacuated(act, f"mix{i}"))
            row_inv("x1_ss")
            act.wait_ge(mod_ready, 6)
            modulate(KD, 4, 3)
            for m in range(KF):
                if m >= 2:
                    act.wait_ge(hidden_ready, m - 1)
                full(act, f"w1_{m}")
                free(a(part[:, m % 2, :], bank(f"w1_{m}")[:, 0:T], ACT.Relu), f"w1_{m}")
            row_square(row_squares, x, lambda i: evacuated(act, f"w2_{i}"))
            row_inv("x2_ss")

            act.wait_ge(rope_angle_ready, 1)
            a(rope[:, :, :], rope[:, :, :], ACT.Sin).then_inc(rope_ready, 1)

            def swiglu(p):
                for m in range(KF2):
                    if m >= 2:
                        evacuated(act, f"{p}u{m - 2}")
                    full(act, f"{p}g{m}")
                    free(a(part[:, m % 2, :], bank(f"{p}g{m}")[:, 0:T], ACT.Silu), f"{p}g{m}")

            swiglu("f1")

            nc.scalar.preload_act_table_set("natural_log_exp_and_others")
            row_square(row_squares, x, lambda i: evacuated(act, f"f1d{i}"))
            row_inv("x3_ss")

            def latent_block(i, name, gain, k):
                square(name)
                free(a(latent[:, i, :], bank(name)[:, 0:T], ACT.Copy, scale=col(gain, k)), name)

            for b in range(3):
                latent_block(b, f"cq{b}", "mla_cq_norm_2", b)
            latent_block(3, "ckv0", "mla_ckv_norm_2", 0)
            inv_rms("cq", 384, lambda: evacuated(act, "qa2"))
            latent_block(4, "ckv1", "mla_ckv_norm_2", 1)
            full(act, "kr")
            ps = bank("kr")
            for s in range(2):
                a(k_squares[HI, s, :], ps[HI, 0:T], ACT.Square, scale=0.5 ** 0.5)
                a(k_squares[LO, 2 + s, :], ps[LO, 0:T], ACT.Square, scale=0.5 ** 0.5)
            free(a(kr[:, 0, :], ps[:, 0:T], ACT.Copy, scale=col("mla_k_rope")), "kr")
            inv_rms("ckv", 256, lambda: evacuated(act, "qa3"))
            square("qm0")
            square("qm1")
            inv_rms("qm0", P, lambda: act.wait_ge(latent_ready, 3))
            square("qm2")
            inv_rms("qm1", P, lambda: act.wait_ge(latent_ready, 5))
            square("qm3")
            inv_rms("qm2", P, lambda: evacuated(act, "qm0"))
            square("uq0")
            inv_rms("qm3", P, lambda: evacuated(act, "qm1"))
            for h in range(1, 8):
                square(f"uq{h}")
                inv_rms(f"uq{h - 1}", 96, lambda: evacuated(act, f"qm{h + 1}") if h < 3 else act.wait_ge(normed, h - 2))

            def k_square(b):
                full(act, f"uk{b}")
                ps = bank(f"uk{b}")
                a(k_squares[LO, b % 2, :], ps[LO, 0:T], ACT.Square).then_inc(k_squares_ready, 1)
                a(k_squares[HI, 2 + b % 2, :], ps[HI, 0:T], ACT.Square).then_inc(k_squares_ready, 1)

            k_square(0)
            inv_rms("uq7", 96, lambda: act.wait_ge(normed, 6))
            for b in range(4):
                if b < 3:
                    k_square(b + 1)
                for h in (2 * b, 2 * b + 1):
                    inv_rms(f"uk{h}", 96, lambda: act.wait_ge(normed, 7 + h))
            for t in range(TT):
                spread_heads(pair_v[:, t, :, :], f"uv{t}")
            nc.scalar.preload_act_table_set("gelu_and_others")
            for t in range(TT):
                full(act, f"sv{t}")
                free(a(sg_v[:, t, :], bank(f"sv{t}")[:, :], ACT.Gelu), f"sv{t}")
            for b in range(4):
                full(act, f"su{b}")
                free(a(attn_a[:, b, :], bank(f"su{b}")[:, 0:T], ACT.Gelu), f"su{b}")
            nc.scalar.preload_act_table_set("natural_log_exp_and_others")
            act.wait_ge(sg_var_ready, 1)
            step(a(sg_stat[:, :, 8], sg_stat[:, :, 7], ACT.Ln, bias=col("eps")))
            a(sg_stat[:, :, 9], sg_stat[:, :, 8], ACT.Exp, scale=-0.5).then_inc(sg_dev_ready, 1)

            nc.scalar.preload_act_table_set("exp_and_others")

            def attend(i):
                w = logit[:, i % 2, :]
                if i < 8:
                    exps(8 + i, {0: (w[:, 0:P],) * 2, 1: (w[:, P:384],) * 2})
                else:
                    ps = bank(f"mem{i - 8}")
                    act.wait_ge(logits_ready, 8 + i + 1)
                    a(w[:, 0:T], ps[:, 0:T], ACT.Exp, scale=P ** -0.5, bias=stats[:, i % 2, 0, 0:1],
                      accum_out=stats[:, i % 2, 1, 0:1])
                    a(w[:, T:2 * T], ps[:, T:2 * T], ACT.Exp, scale=P ** -0.5, bias=stats[:, i % 2, 0, 1:2],
                      accum_out=stats[:, i % 2, 1, 1:2]).then_inc(weights_raw, 1)
                    act.wait_ge(weights_raw, 8 + i + 1)
                    free(a(stats[:, i % 2, 3, 5:6], stats[:, i % 2, 1, 1:2], ACT.Copy), f"mem{i - 8}")

            act.wait_ge(half_bias_ready, 1)
            attend(0)
            for i in range(12):
                for g in (2 * i, 2 * i + 1):
                    full(act, f"gate{g}")
                    free(a(gates[:, g, :], bank(f"gate{g}")[:, 0:T], ACT.Tanh, scale=0.5, bias=half_bias[:, g:g + 1]), f"gate{g}")
                if i < 11:
                    attend(i + 1)
                if i and i % 2 == 0 and i <= 8:
                    copy(attn_b[:, i // 2 - 1, :], f"mlao{i // 2 - 1}")
                if i >= 9:
                    copy(attn_c[:, i - 9, :], f"memo{i - 9}")
                if i < 8:
                    copy(turned[:, i % 2, 0, 0:384], f"mlat{i}", bank(f"mlat{i}")[:, 0:384])
                else:
                    copy(turned[:, i % 2, 0, :], f"memt{i - 8}", bank(f"memt{i - 8}")[:, :])
            copy(attn_c[:, 3, :], "memo3")

            nc.scalar.preload_act_table_set("natural_log_exp_and_others")
            row_square(row_squares, x, lambda i: evacuated(act, f"mix2_{i}"))
            row_inv("x4_ss")
            swiglu("f2")

        @block.vector
        def _(dve):
            v = nc.vector
            step = chain(dve, dve_step)
            n_rinv, n_ada = [0], [0]

            def take_rinv():
                n = n_rinv[0]
                n_rinv[0] += 1
                dve.wait_ge(rinv_ready, n + 1)
                return rinv[:, n % 2, :]

            def normalise(name, outs, gain, rows=(slice(0, P),)):
                r = take_rinv()
                for out, rr in zip(outs, rows):
                    ins = v.scalar_tensor_tensor(out=out, in0=bank(name)[rr, 0:T], scalar=col(gain, 0, rr), in1=r[rr, :],
                                                 op0=ALU.mult, op1=ALU.mult)
                free(ins, name)

            def norm_row(dst, src, gain, row, sem_):
                dve.wait_ge(row_rinv_ready, row + 1)
                for i in range(KD):
                    v.scalar_tensor_tensor(out=dst[:, i, :], in0=src[:, i, :], scalar=col(gain, i), in1=row_rinv[:, :],
                                           op0=ALU.mult, op1=ALU.mult).then_inc(sem_, 1)

            def ada_step():
                n = n_ada[0]
                n_ada[0] += 1
                j, k = n // KD, n % KD
                acc = ada_acc[:, j % 2, :]
                dve.wait_ge(ada_full[n % ADA_RING], 16 * (n // ADA_RING + 1))
                w = ada_ring[:, n % ADA_RING, :]
                c = c_act[:, 1, k:k + 1]
                if k == 0:
                    if j >= 2:
                        full(dve, f"ada{j - 2}b")
                    v.tensor_scalar(acc, w, c, None, ALU.mult).then_inc(ada_used, 1)
                else:
                    dve.wait_ge(ada_used, n)
                    v.scalar_tensor_tensor(out=acc, in0=w, scalar=c, in1=acc, op0=ALU.mult, op1=ALU.add).then_inc(ada_used, 1)
                if k == KD - 1:
                    dve.wait_ge(ada_used, n + 1)
                    v.tensor_copy(c_act[:, 0, 0:1], c_act[:, 1, 0:1]).then_inc(ada_summed, 1)

            def ada_reduce(j):
                at = mod[:, j * 8:(j + 1) * 8]
                for half in range(2):
                    name = f"ada{j}{'ab'[half]}"
                    full(dve, name)
                    free(v.tensor_reduce(out=at[:, half * 4:half * 4 + 4], in_=bank(name)[:, :].rearrange("p (k i) -> p k i", i=P),
                                         axis=AX.X, op=ALU.add), name)
                evacuated(dve, f"ada{j}a")
                evacuated(dve, f"ada{j}b")
                b = cols[:, AT["ada_b"] + j * 8:AT["ada_b"] + (j + 1) * 8]
                if j in (1, 4):
                    v.scalar_tensor_tensor(out=at, in0=at, scalar=1.0, in1=b, op0=ALU.add, op1=ALU.add).then_inc(mod_ready, 1)
                elif j == 2:
                    step(v.tensor_tensor(at, at, b, ALU.add))
                    v.tensor_scalar(at, at, 0.5, None, ALU.mult).then_inc(mod_ready, 1)
                else:
                    v.tensor_tensor(at, at, b, ALU.add).then_inc(mod_ready, 1)

            dve.wait_ge(c_tanh_ready, 1)
            step(v.tensor_scalar(c_act[:, 0, :], c_act[:, 0, :], 0.5, 0.5, ALU.mult, ALU.add))
            step(v.tensor_tensor(c_act[:, 1, :], c_act[:, 0, :], cols[:, AT["c"]:AT["c"] + 8], ALU.mult))
            norm_row(mem_n, mem_n, "mem_norm_2", ROW_MEM, u_ready)
            for b in range(4):
                normalise(f"mem_k{b}", [mem_k[:, b, :]], "mem_k_norm_2")
                for _ in range(4):
                    ada_step()
                if b == 2:
                    full(dve, "bias")
                    free(v.tensor_copy(bias_line[:, :], bank("bias")[0:8, :]), "bias")
                if b == 1:
                    norm_row(u, x, "norm1_g", ROW_X, u_normed)
            v.tensor_scalar(half_bias[:, :], cols[:, AT["b_gate_2"]:AT["b_gate_2"] + 24], 0.5, None, ALU.mult).then_inc(half_bias_ready, 1)
            ada_reduce(0)
            ada_reduce(1)

            for _ in range(16):
                ada_step()
            dve.wait_ge(zeros_ready, 6)
            for n, off in (("ks", 0), ("kw", P)):
                r = take_rinv()
                late = 272 + off
                for s, rr in enumerate((LO, HI)):
                    for first, dst in ((0, off), (P, late)):
                        ins = v.scalar_tensor_tensor(out=kcat[rr, s, dst:dst + P], in0=bank(n)[rr, first:first + P],
                                                     scalar=col("k_slc_norm" if n == "ks" else "k_win_norm", 0, rr),
                                                     in1=r[rr, first:first + P], op0=ALU.mult, op1=ALU.mult)
                free(ins, n)
            for b in range(4):
                normalise(f"qa{b}", [qa[:, b, :]], "q_norm")
            for b in range(4):
                full(dve, f"kb{b}")
                ps = bank(f"kb{b}")
                v.tensor_copy(pair_k[LO, 2 * b, :], ps[LO, 0:T])
                free(v.tensor_copy(pair_k[HI, 2 * b + 1, :], ps[HI, 0:T]), f"kb{b}")
            ada_reduce(2)
            ada_reduce(3)

            before = mat("before")

            def softplus(h):
                dve.wait_ge(sb_log_ready, h + 1)
                w = sbw[:, h % 2, :, :]
                step(v.scalar_tensor_tensor(out=w[:, 2, :], in0=bank(f"sbz{h}")[:, 0:384], scalar=0.0, in1=w[:, 1, :],
                                            op0=ALU.max, op1=ALU.add))
                v.tensor_tensor(w[:, 2, 0:P], w[:, 2, 0:P], before, ALU.mult)
                v.tensor_tensor(w[:, 2, T:T + P], w[:, 2, T:T + P], before, ALU.mult).then_inc(softplus_ready, 1)

            softplus(0)
            for h in range(8):
                if h == 0:
                    for w, n in enumerate("kv"):
                        dve.wait_ge(cmp_tanh_ready, w + 1)
                        th = cmp_tanh[:, w, 0:N_CMP]
                        step(v.tensor_scalar(th, th, 0.5, 0.5, ALU.mult, ALU.add))
                        free(v.tensor_tensor(cmp_turned[:, w, 0:N_CMP], th, bank(f"cmp_turn_{n}")[:, 0:N_CMP], ALU.mult), f"cmp_turn_{n}")
                    dve.wait_ge(gates_tanh_ready, 1)
                    step(v.tensor_scalar(gate_tanh[:, :, :], gate_tanh[:, :, :], 0.5, 0.5, ALU.mult, ALU.add))
                    for t in range(TT):
                        g = gate_tanh[:, t, :].rearrange("p (h r) -> p h r", r=3)
                        v.tensor_copy(gate_t[:, :, 2 * t:2 * t + 2], g[:, :, 1:3])
                        v.tensor_scalar(gate_t[:, :, 4 + t], g[:, :, 0], col("sees_a_block", t), None, ALU.mult).then_inc(gate_t_ready, 1)
                if h == 2:
                    dve.wait_ge(cmp_rinv_ready, 1)
                    for s, rr in enumerate((LO, HI)):
                        ins = v.scalar_tensor_tensor(out=kcat[rr, s, T:T + N_CMP], in0=cmp_k[rr, 0, 0:N_CMP],
                                                     scalar=col("k_cmp_norm", 0, rr), in1=cmp_k[rr, 3, 0:N_CMP],
                                                     op0=ALU.mult, op1=ALU.mult)
                    ins.then_inc(cmp_k_ready, 1)
                if h < 7:
                    softplus(h + 1)
                ada_step()
                ada_step()
                if h == 5:
                    ada_reduce(4)
            ada_reduce(5)

            def nsa_logits(i):
                h = i // 2 + 4 * (i % 2)
                w, st = logit[:, i % 2, :], stats[:, i % 2, :, :]
                if i >= 2:
                    full(dve, f"nsat{i - 2}c")
                early = w[:, 0:256].rearrange("p (r k) -> p r k", r=2)
                late = w[:, 256:768].rearrange("p (r k) -> p r k", r=2)

                def add(out, ps, b):
                    return v.scalar_tensor_tensor(out=out, in0=ps, scalar=HD ** -0.5, in1=b, op0=ALU.mult, op1=ALU.add)

                def both(b):
                    return b.unsqueeze(1).to_broadcast([P, 2, P])

                for c, t, dst, b in (("a", 0, early, bias[:, h, P:T]), ("b", 1, late[:, :, 0:P], bias[:, h, 0:P])):
                    full(dve, f"nsa{i}{c}")
                    ps = bank(f"nsa{i}{c}")
                    add(dst, ps[:, 0:256].rearrange("p (r k) -> p r k", r=2), both(b))
                    free(add(w[:, 768 + 16 * t:768 + 16 * t + N_CMP], ps[:, T:T + N_CMP], bias_cmp[:, h, t, :]), f"nsa{i}{c}")
                full(dve, f"nsa{i}c")
                free(add(late[:, :, P:T], bank(f"nsa{i}c")[:, 0:256].rearrange("p (r k) -> p r k", r=2), both(bias[:, h, P:T])), f"nsa{i}c")
                for c in "abc":
                    evacuated(dve, f"nsa{i}{c}")
                v.tensor_reduce(out=st[:, 0, 0:2], in_=early, axis=AX.X, op=ALU.max, negate=True)
                v.tensor_reduce(out=st[:, 0, 4:6], in_=w[:, 768:800].rearrange("p (t k) -> p t k", t=2)[:, :, 0:N_CMP],
                                axis=AX.X, op=ALU.max, negate=True)
                v.tensor_reduce(out=st[:, 0, 2:4], in_=late, axis=AX.X, op=ALU.max, negate=True).then_inc(logits_ready, 1)

            def scale_weights(i, n, parts, gate=None):
                dve.wait_ge(weights_raw, i + 1)
                st = stats[:, i % 2, :, :]
                step(v.tensor_scalar(st[:, 2, 0:n], st[:, 1, 0:n], 1e-30, None, ALU.max))
                step(v.reciprocal(st[:, 3 if gate is None else 2, 0:n], st[:, 2, 0:n]))
                if gate is not None:
                    step(v.tensor_tensor(st[:, 3, 0:n], st[:, 2, 0:n], gate, ALU.mult))
                for k, p in enumerate(parts):
                    ins = v.tensor_scalar(p, p, st[:, 3, k:k + 1], None, ALU.mult)
                ins.then_inc(weights_ready, 1)

            def nsa_scale(i):
                w = logit[:, i % 2, :]
                scale_weights(i, 6, [w[:, 0:128], w[:, 128:256], w[:, 256:512], w[:, 512:768], w[:, 768:768 + N_CMP],
                                     w[:, 784:784 + N_CMP]], gate_t[:, i // 2 + 4 * (i % 2), :])

            dve.wait_ge(gate_t_ready, TT)
            dve.wait_ge(loaded["bias"], 16 * 24)
            nsa_logits(0)
            nsa_scale(0)
            for i in range(8):
                if i < 7:
                    nsa_logits(i + 1)
                full(dve, f"nsat{i}w")
                free(v.tensor_copy(turned[:, i % 2, 1, 0:384], bank(f"nsat{i}w")[:, 0:384]), f"nsat{i}w")
                if i < 7:
                    nsa_scale(i + 1)

            for m in range(KD):
                dve.wait_ge(tanh_ready, m // 2 + 1)
                evacuated(dve, f"mb{m}")
                for n, g, dst in ((f"up_nsa{m}", m, merged[:, m, :]), (f"up_sb{m}", 8 + m, part[:, m % 2, :])):
                    full(dve, n)
                    free(v.scalar_tensor_tensor(out=dst, in0=gates[:, g, :], scalar=1.0, in1=bank(n)[:, 0:T],
                                                op0=ALU.add, op1=ALU.mult), n)
                evacuated(dve, f"up_nsa{m}")
                evacuated(dve, f"up_sb{m}")
                v.tensor_tensor(merged[:, m, :], merged[:, m, :], part[:, m % 2, :], ALU.add).then_inc(merged_ready, 1)

            def add_residual(name, m, gate):
                full(dve, name)
                free(v.scalar_tensor_tensor(out=x[:, m, :], in0=bank(name)[:, 0:T], scalar=gate, in1=x[:, m, :],
                                            op0=ALU.mult, op1=ALU.add), name)

            dve.wait_ge(mod_ready, 6)
            for m in range(KD):
                add_residual(f"mix{m}", m, mod[:, 16 + m:17 + m])

            for i in range(KD):
                evacuated(dve, f"mix{i}")
            norm_row(u, x, "norm2_g", ROW_1, u_normed)

            def rope_steps():
                dve.wait_ge(loaded["pos"], 16)
                step(v.tensor_copy(pos[:, :], pos_i[:, :]))
                yield
                for r in range(4):
                    step(v.tensor_scalar(rope[:, r, :], pos[:, :], col("angle", r), None, ALU.mult))
                    yield
                step(v.tensor_scalar(rope_n, rope[:, :, :], 1.0 / TWO_PI, BIG, ALU.mult, ALU.add))
                yield
                step(v.tensor_scalar(rope_n, rope_n, -BIG, None, ALU.add))
                yield
                for c in (PI_1, PI_2, PI_3):
                    step(v.scalar_tensor_tensor(out=rope[:, :, :], in0=rope_n, scalar=-c, in1=rope[:, :, :], op0=ALU.mult, op1=ALU.add))
                    yield
                for r in range(4):
                    step(v.tensor_scalar(rope[:, r, :], rope[:, r, :], col("phase", r), None, ALU.add))
                    yield
                step(v.tensor_scalar(rope_n, rope[:, :, :], PI_LIMIT, -TWO_PI, ALU.is_gt, ALU.mult))
                yield
                step(v.tensor_tensor(rope[:, :, :], rope[:, :, :], rope_n, ALU.add))
                yield
                v.tensor_scalar(rope[:, :, :], rope[:, :, :], PI_LIMIT, -PI_LIMIT, ALU.min, ALU.max).then_inc(rope_angle_ready, 1)
                yield

            steps = rope_steps()
            for m in range(KF):
                evacuated(dve, f"w1_{m}")
                v.tensor_tensor(hidden[:, m, :], part[:, m % 2, :], part[:, m % 2, :], ALU.mult).then_inc(hidden_ready, 1)
                next(steps, None)
            for m in range(KD):
                add_residual(f"w2_{m}", m, mod[:, 40 + m:41 + m])
            for i in range(KD):
                evacuated(dve, f"w2_{i}")

            def swiglu(p):
                for m in range(KF2):
                    evacuated(dve, f"{p}g{m}")
                    full(dve, f"{p}u{m}")
                    free(v.tensor_tensor(hidden[:, m, :], part[:, m % 2, :], bank(f"{p}u{m}")[:, 0:T], ALU.mult), f"{p}u{m}")
                for m in range(KD):
                    add_residual(f"{p}d{m}", m, 0.5)
                for m in range(KD):
                    evacuated(dve, f"{p}d{m}")

            norm_row(u, x, "ffn1_norm_2", ROW_2, u_ready)
            swiglu("f1")

            norm_row(u, x, "mix_norm_2", ROW_3, u_ready)
            for first, n, last in ((0, 3, "cq2"), (3, 2, "ckv1")):
                r = take_rinv()
                evacuated(dve, last)
                for i in range(first, first + n):
                    v.tensor_tensor(latent[:, i, :], latent[:, i, :], r, ALU.mult).then_inc(latent_ready, 1)
            for b in range(3):
                normalise(f"qm{b}", [qa[:, b, :]], "mem_q_norm_2")
            dve.wait_ge(rope_ready, 1)
            full(dve, "kr_rot")
            evacuated(dve, "kr")
            step(v.tensor_tensor(kr[:, 1, :], kr[:, 0, :], rope[:, ROPE_C, :], ALU.mult))
            free(v.tensor_tensor(part[:, 0, :], bank("kr_rot")[:, 0:T], rope[:, ROPE_S, :], ALU.mult), "kr_rot")
            evacuated(dve, "kr_rot")
            v.tensor_tensor(kr[:, 1, :], kr[:, 1, :], part[:, 0, :], ALU.add).then_inc(k_pe_ready, 1)
            dve.wait_ge(k_pe_ready, 1)

            def mla_q_gain(h):
                dve.wait_ge(squares_ready, 19 + h + 1)
                odd = h % 2
                if h >= 2:
                    dve.wait_ge(normed, h - 1)
                free(v.scalar_tensor_tensor(out=part[:, h % 2, :], in0=bank(f"uq{h}")[:, 0:T],
                                            scalar=col("mla_q_odd" if odd else "mla_q_even"), in1=rope[:, ROPE_QO if odd else ROPE_QE, :],
                                            op0=ALU.mult, op1=ALU.mult), f"uq{h}")

            def mla_q_norm(h):
                r = take_rinv()
                evacuated(dve, f"uq{h}")
                v.tensor_tensor(pair_q[:, h, :], part[:, h % 2, :], r, ALU.mult).then_inc(normed, 1)

            mla_q_gain(0)
            normalise("qm3", [qa[:, 3, :]], "mem_q_norm_2")
            for h in range(8):
                if h < 7:
                    mla_q_gain(h + 1)
                mla_q_norm(h)
            for h in range(8):
                name, (own, pe_rows) = f"uk{h // 2}", ((LO, HI), (HI, LO))[h % 2]
                r = take_rinv()
                ins = v.scalar_tensor_tensor(out=pair_k[own, h, :], in0=bank(name)[own, 0:T], scalar=col("mla_k_nope", 0, own),
                                             in1=r[own, :], op0=ALU.mult, op1=ALU.mult)
                if h % 2:
                    free(ins, name)
                v.tensor_tensor(pair_k[pe_rows, h, :], kr[pe_rows, 1, :], r[pe_rows, :], ALU.mult).then_inc(normed, 1)

            for t in range(TT):
                evacuated(dve, f"sv{t}")
                step(v.bn_stats(sg_stat[:, t, 0:6], sg_v[:, t, :]))
                ins = v.bn_aggr(sg_stat[:, t, 6:8], sg_stat[:, t, 0:6])
            ins.then_inc(sg_var_ready, 1)
            dve.wait_ge(sg_dev_ready, 1)
            dve.wait_ge(loaded["sg"], 48)
            for t in range(TT):
                s = sg_v[:, t, :]
                step(v.tensor_scalar(s, s, sg_stat[:, t, 6:7], sg_stat[:, t, 9:10], ALU.subtract, ALU.mult))
                step(v.tensor_tensor(s, s, sg_ln[:, 0, :], ALU.mult))
                v.tensor_tensor(s, s, sg_ln[:, 1, :], ALU.add).then_inc(sg_ln_ready, 1)

            def logits(i):
                w, st = logit[:, i % 2, :], stats[:, i % 2, :, :]
                if i >= 2:
                    full(dve, f"mlat{i - 2}" if i < 10 else f"memt{i - 10}")
                if i < 8:
                    name = f"mla{i}"
                    full(dve, name)
                    ps = bank(name)
                    scale = 96 ** -0.5
                    v.scalar_tensor_tensor(out=w[:, 0:P], in0=ps[:, 0:P], scalar=scale, in1=mat("not_after"), op0=ALU.mult, op1=ALU.add)
                    v.tensor_scalar(w[:, P:T], ps[:, P:T], scale, None, ALU.mult)
                    free(v.scalar_tensor_tensor(out=w[:, T:384], in0=ps[:, T:384], scalar=scale, in1=mat("not_after"),
                                                op0=ALU.mult, op1=ALU.add), name)
                    evacuated(dve, name)
                    v.tensor_reduce(out=st[:, 0, 0:1], in_=w[:, 0:P], axis=AX.X, op=ALU.max, negate=True)
                    v.tensor_reduce(out=st[:, 0, 1:2], in_=w[:, P:384], axis=AX.X, op=ALU.max, negate=True).then_inc(logits_ready, 1)
                else:
                    name = f"mem{i - 8}"
                    full(dve, name)
                    step(v.tensor_reduce(out=st[:, 0, 2:4], in_=bank(name)[:, :].rearrange("p (t k) -> p t k", t=2),
                                         axis=AX.X, op=ALU.max, negate=True))
                    v.tensor_scalar(st[:, 0, 0:2], st[:, 0, 2:4], P ** -0.5, None, ALU.mult).then_inc(logits_ready, 1)

            def attend_scale(i):
                w = logit[:, i % 2, :]
                scale_weights(8 + i, 2, [w[:, 0:P], w[:, P:384]] if i < 8 else [w[:, 0:T], w[:, T:2 * T]])

            logits(0)
            attend_scale(0)
            for i in range(12):
                if i < 11:
                    logits(i + 1)
                    attend_scale(i + 1)
            for b in range(4):
                evacuated(dve, f"su{b}")
                for c in range(TT):
                    name = f"sg{b}{c}"
                    full(dve, name)
                    for s, rr in enumerate((LO, HI)):
                        dst = attn_a[rr, b, c * P:(c + 1) * P]
                        ins = v.tensor_tensor(dst, dst, bank(name)[rr, s * P:(s + 1) * P], ALU.mult)
                    free(ins, name)

            for m in range(KD):
                for k, c in enumerate("abc"):
                    evacuated(dve, f"gate{8 * k + m}")
                    n = f"br_{c}{m}"
                    full(dve, n)
                    dst = merged[:, m, :] if k == 0 else part[:, k - 1, :]
                    free(v.scalar_tensor_tensor(out=dst, in0=gates[:, 8 * k + m, :], scalar=1.0, in1=bank(n)[:, 0:T],
                                                op0=ALU.add, op1=ALU.mult), n)
                for c in "abc":
                    evacuated(dve, f"br_{c}{m}")
                step(v.tensor_tensor(merged[:, m, :], merged[:, m, :], part[:, 0, :], ALU.add))
                v.tensor_tensor(merged[:, m, :], merged[:, m, :], part[:, 1, :], ALU.add).then_inc(merged_ready, 1)
                dve.wait_ge(merged_ready, KD + m + 1)
            for m in range(KD):
                add_residual(f"mix2_{m}", m, 0.5)
            for m in range(KD):
                evacuated(dve, f"mix2_{m}")
            norm_row(u, x, "ffn2_norm_2", ROW_4, u_ready)
            swiglu("f2")


def lay_out(a):
    a = {k: np.asarray(v) for k, v in a.items()}
    sq = {k: (v[0] if k not in ("x", "c", "rel_bias", "mem_2", "positions_2") else v) for k, v in a.items()}

    def block_diagonal(w):
        out = np.zeros(w.shape[:-2] + (P, P), w.dtype)
        out[..., 0:64, 0:64] = w
        out[..., 64:, 64:] = w
        return out

    src = dict(sq)
    for n in ("cmp_k_w1", "cmp_v_w1"):
        src[n] = block_diagonal(sq[n].reshape(32, HD, HD))
    chunks = stream_chunks()
    n_slots = -(-len(chunks) // SLOT)
    stream = np.zeros((n_slots, P, SLOT, P), np.float32)
    for i, (name, rows, cols) in enumerate(chunks):
        w = src[name]
        stream[i // SLOT, :, i % SLOT, :] = w[rows] if cols is None else w[np.ix_(rows, cols)]
    ada = sq["ada_w"].reshape(KD, P, 6, D).transpose(2, 0, 1, 3).reshape(48, P, D)
    mats, buckets, consts = shape_constants()
    q, k = sq["mla_q_norm_2"], sq["mla_k_norm_2"]
    pe = np.concatenate([q[64:96], q[80:96], q[64:80]])
    twice = lambda v: np.concatenate([v, v])
    vec = {n: sq[n] for n in ("norm1_g", "norm2_g", "ffn1_norm_2", "mix_norm_2", "ffn2_norm_2", "mem_norm_2", "ada_b",
                              "b_gate_2", "mla_cq_norm_2", "mla_ckv_norm_2", "mem_q_norm_2", "mem_k_norm_2")}
    vec["c"] = a["c"]
    vec["q_norm"] = twice(sq["q_norm_g"])
    for i, n in enumerate(("k_cmp_norm", "k_slc_norm", "k_win_norm")):
        vec[n] = twice(sq["k_norm_g"][i])
    vec["mla_q_even"] = np.concatenate([q[0:64], pe])
    vec["mla_q_odd"] = np.concatenate([pe, q[0:64]])
    vec["mla_k_nope"] = twice(k[0:64])
    vec["mla_k_rope"] = np.concatenate([k[64:96]] * 4)
    vec.update(consts)
    cols = np.concatenate([np.asarray(vec[n], np.float32).reshape(c, P) for n, c in VECTORS]).T

    def feature_major(v):
        return np.ascontiguousarray(v.reshape(T, KD, P).transpose(2, 1, 0))

    table = np.concatenate([a["rel_bias"], np.ones((1, 8), np.float32)])
    pos_rows = sq["cmp_pos"].T
    out = {
        "stream": stream.reshape(n_slots, P, SLOT * P), "ada": ada, "x_t": feature_major(a["x"]),
        "mem_t": feature_major(a["mem_2"]), "cols": cols, "mats": mats.transpose(1, 0, 2), "buckets": buckets,
        "table": table, "pos": np.broadcast_to(a["positions_2"], (P, T)),
        "gates_w": sq["w_in"][:, C_GA:C_GA + 24].reshape(KD, P, 24).transpose(1, 0, 2),
        "cmp_w2": np.stack([block_diagonal(sq["cmp_k_w2"]), block_diagonal(sq["cmp_v_w2"])], 1),
        "cmp_pos": np.concatenate([pos_rows, pos_rows]),
        "sg_w": sq["sg_w_2"].transpose(2, 0, 1), "sg_b": sq["sg_b_2"].reshape(1, 8 * P),
        "sg_ln": np.broadcast_to(np.stack([sq["sg_ln_g_2"], sq["sg_ln_b_2"]])[None], (P, 2, 512)),
    }
    return {n: np.ascontiguousarray(v) for n, v in out.items()}


def kernel(**inputs):
    import concourse.bacc as bacc
    from concourse.bass_utils import run_bass_kernel_spmd

    arrays = lay_out(inputs)
    nc = bacc.Bacc("TRN2", target_bir_lowering=False, num_devices=1)
    args = [nc.dram_tensor(f"in_{n}", v.shape, mybir.dt.from_np(v.dtype), kind="ExternalInput").ap() for n, v in arrays.items()]
    out = nc.dram_tensor("out_t", (P, KD, T), F32, kind="ExternalOutput").ap()
    build(nc, *args, out)
    r = run_bass_kernel_spmd(nc, [{f"in_{n}": v for n, v in arrays.items()}], core_ids=[0])
    got = np.asarray(r.results[0]["out_t"])
    return np.ascontiguousarray(got.transpose(2, 1, 0)).reshape(1, T, D)
```

```python
from contextlib import ExitStack

import numpy as np

import concourse.bass as bass
from concourse import mybir

F32 = mybir.dt.float32
F32R = mybir.dt.float32r
I32 = mybir.dt.int32
ACT = mybir.ActivationFunctionType
ALU = mybir.AluOpType
AX = mybir.AxisListType

P = 128
T = 256
TT = T // P
D = 1024
KD = D // P
HD = 64
DFF, DFF2 = 4096, 2816
KF, KF2 = DFF // P, DFF2 // P
NEG = -1e30
EPS = 1e-6
N_CMP = 15
CMP_STRIDE = 16
SLOT = 8
SQ = 3
RING = 6
HALVES = 3
ADA_RING = 3
BIG = 12582912.0
TWO_PI = 6.283185307179586
PI_1 = 6.28125
PI_2 = 0.0019350051879882812
PI_3 = float(np.float32(TWO_PI - PI_1 - PI_2))
PI_LIMIT = 3.1415925

C_QA, C_KC, C_VC, C_KS, C_VS, C_KW, C_VW, C_GA, C_QB, C_KB, C_VB, C_MA, C_MB = (
    0, 512, 640, 768, 896, 1024, 1152, 1280, 1304, 1816, 2328, 2840, 3864)
D_U, D_V, D_CQ, D_CKV, D_KR, D_QM, D_GATE = 0, 512, 1024, 1408, 1664, 1696, 2208


def span(first, n=P):
    return list(range(first, first + n))


def rot(cols):
    half = len(cols) // 2
    return cols[half:] + cols[:half]


def mla_q_cols(h):
    nope, rope = span(h * 96, 64), span(h * 96 + 64, 32)
    pe = rope + rot(rope)
    return nope + pe if h % 2 == 0 else pe + nope


def stream_chunks():
    out = []

    def stationary(name, cols, rows):
        for r in rows:
            out.append((name, r, cols))

    def moving(name, first, n, k):
        for kk in range(k):
            for j in range(n // P):
                out.append((name, span(kk * P), span(first + j * P)))

    full = [span(k * P) for k in range(KD)]
    half = [span(k * P) for k in range(4)]
    for b in range(4):
        stationary("mem_w_kv_2", span(b * P), full)
    moving("mem_w_kv_2", 512, 512, KD)
    for k in range(KD):
        out.append(("w_in", span(k * P), span(C_VS)))
        out.append(("w_in", span(k * P), span(C_VW)))
    moving("w_in", C_VB, 512, KD)
    stationary("w_in", span(C_GA), full)
    for c in (C_KC, C_VC, C_KS, C_KW):
        stationary("w_in", span(c), full)
    for b in range(4):
        stationary("w_in", span(b * HD, HD) + span((4 + b) * HD, HD), full)
    for c in (C_KB, C_QB):
        for b in range(4):
            stationary("w_in", span(c + b * P), full)
    for name in ("cmp_k_w1", "cmp_v_w1"):
        for j in range(32):
            out.append((name, j, None))
    for c in (C_MA, C_MB):
        for b in range(KD):
            stationary("w_in", span(c + b * P), full)
    for m in range(KD):
        stationary("w_up_nsa", span(m * P), [span(b * HD, HD) + span((4 + b) * HD, HD) for b in range(4)])
        stationary("w_up_sb", span(m * P), half)
    for m in range(KD):
        stationary("w_out", span(m * P), full)
    for m in range(KF):
        stationary("mlp_w1", span(m * P), full)
    for m in range(KD):
        stationary("mlp_w2", span(m * P), [span(k * P) for k in range(KF)])

    def swiglu(gu, down):
        for m in range(KF2):
            stationary(gu, span(m * P), full)
            stationary(gu, span(DFF2 + m * P), full)
        for m in range(KD):
            stationary(down, span(m * P), [span(k * P) for k in range(KF2)])

    swiglu("ffn1_w_gu_2", "ffn1_w_down_2")
    for b in range(3):
        stationary("w_in_2", span(D_CQ + b * P), full)
    for b in range(2):
        stationary("w_in_2", span(D_CKV + b * P), full)
    stationary("w_in_2", 4 * span(D_KR, 32), full)
    for b in range(4):
        stationary("w_in_2", span(D_QM + b * P), full)
    for h in range(8):
        stationary("mla_w_uq_2", mla_q_cols(h), [span(k * P) for k in range(3)])
    for b in range(4):
        stationary("mla_w_ukv_2", span(2 * b * P, HD) + span((2 * b + 1) * P, HD), [span(0), span(P)])
    for k in range(2):
        for j in range(4):
            out.append(("mla_w_ukv_2", span(k * P), span(2 * j * P + HD, HD) + span((2 * j + 1) * P + HD, HD)))
    moving("w_in_2", D_V, 512, KD)
    for b in range(4):
        stationary("w_in_2", span(D_U + b * P), full)
    for b in range(24):
        stationary("w_in_2", span(D_GATE + b * P), full)
    for m in range(KD):
        for name in ("w_branch_a_2", "w_branch_b_2", "w_branch_c_2"):
            stationary(name, span(m * P), half)
    for m in range(KD):
        stationary("w_out_2", span(m * P), full)
    swiglu("ffn2_w_gu_2", "ffn2_w_down_2")
    return out


VECTORS = [("norm1_g", 8), ("norm2_g", 8), ("ffn1_norm_2", 8), ("mix_norm_2", 8), ("ffn2_norm_2", 8),
           ("mem_norm_2", 8), ("c", 8), ("ada_b", 48), ("b_gate_2", 24), ("mla_cq_norm_2", 3),
           ("mla_ckv_norm_2", 2), ("q_norm", 1), ("k_cmp_norm", 1), ("k_slc_norm", 1), ("k_win_norm", 1),
           ("mla_q_even", 1), ("mla_q_odd", 1), ("mla_k_nope", 1), ("mla_k_rope", 1), ("mem_q_norm_2", 1),
           ("mem_k_norm_2", 1), ("angle", 4), ("phase", 4), ("sees_a_block", 2), ("eps", 1)]
AT = {}
_n = 0
for _name, _k in VECTORS:
    AT[_name] = _n
    _n += _k
N_COLS = _n
ROPE_QE, ROPE_QO, ROPE_C, ROPE_S = range(4)

MATRICES = ["ident", "ones", "halves", "q_even", "q_odd", "rotate", "neg_suffix",
            "neg_ones", "before", "not_before", "not_after", "spread"]
MAT = {n: i for i, n in enumerate(MATRICES)}


def shape_constants():
    i = np.arange(P)
    k, q = i[:, None], i[None, :]
    m = np.zeros((len(MATRICES), P, P), np.float32)
    m[MAT["ident"]] = np.eye(P)
    m[MAT["ones"]] = 1
    m[MAT["halves"]] = (k // 64) == (q // 64)
    m[MAT["q_even"]] = (k < 96) + 0 * q
    m[MAT["q_odd"]] = ((k < 32) | (k >= 64)) + 0 * q
    m[MAT["rotate"]] = (k // 32 == q // 32) & ((k % 32) == (q % 32 + 16) % 32)
    m[MAT["neg_suffix"]] = -1.0 * (k >= q)
    m[MAT["neg_ones"]] = -1
    m[MAT["before"]] = k < q
    m[MAT["not_before"]] = np.where(k < q, 0, NEG)
    m[MAT["not_after"]] = np.where(q <= k, 0, NEG)
    m[MAT["spread"]] = ((k == q) | (k == N_CMP + 1)) & (q < N_CMP)
    dist = 255 - np.arange(512)
    n = np.maximum(dist, 0)
    nf = np.maximum(n, 1).astype(np.float32)
    large = 16 + (np.log(nf / np.float32(16)) / np.float32(np.log(128 / 16)) * 16).astype(np.int32)
    bucket = np.where(n < 16, n, np.minimum(large, 31))
    buckets = np.zeros((33, 512), np.float32)
    buckets[bucket, np.arange(512)] = dist >= 0
    buckets[32] = np.where(dist >= 0, 0, NEG)
    inv = (np.float32(10000.0) ** (-np.arange(16, dtype=np.float32) / np.float32(16))).astype(np.float32)
    pair = inv[i % 16]
    sign = np.where(i % 32 < 16, -1, 1)
    angle, phase = np.zeros((4, P)), np.zeros((4, P))
    half_pi = np.pi / 2
    angle[ROPE_QE] = np.where(i < 64, 0, np.where(i < 96, pair, sign * pair))
    phase[ROPE_QE] = np.where(i < 96, half_pi, 0)
    angle[ROPE_QO] = np.where(i >= 64, 0, np.where(i < 32, pair, sign * pair))
    phase[ROPE_QO] = np.where((i >= 64) | (i < 32), half_pi, 0)
    angle[ROPE_C], phase[ROPE_C] = pair, half_pi
    angle[ROPE_S] = sign * pair
    sees = np.stack([i >= CMP_STRIDE * 2 - 1, i >= 0])
    return m, buckets, {"angle": angle, "phase": phase, "sees_a_block": sees, "eps": np.full((1, P), EPS)}


def plan_psum(proj, attn, long):
    where, used = {}, [0] * 8
    for names, banks in ((proj, [0, 1, 2]), (attn, [3, 4, 5, 6]), (long, [7])):
        for n, name in enumerate(names):
            b = banks[n % len(banks)]
            assert name not in where, name
            where[name] = (b, used[b])
            used[b] += 1
    return where


def proj_names():
    out = ["mem_ss", "mem_k0", "mem_k1", "x_ss", "mem_k2", "mem_k3", "bias", "mem_v0", "mem_v1"]
    out += ["ada0a", "ada0b", "ada1a", "ada1b"]
    out += ["vsw0", "vsw1", "vsb0", "vsb1", "ga", "kc", "vc", "ks", "kw"]
    out += [f"qa{b}" for b in range(4)] + [f"kb{b}" for b in range(4)] + [f"qb{b}" for b in range(4)]
    out += ["ada2a", "ada2b", "ada3a", "ada3b", "cmp_hid_k", "cmp_hid_v", "ma0", "cmp_turn_k", "cmp_turn_v"]
    out += ["ga_turn", "ma1", "cmp_out_k", "cmp_out_v", "ma2", "ma3", "ma4", "ma5", "ada4a", "ada4b", "ma6", "ma7"]
    out += ["ada5a", "ada5b"] + [f"mb{b}" for b in range(8)]
    for m in range(KD):
        out += [f"up_nsa{m}", f"up_sb{m}"]
    out += [f"mix{m}" for m in range(KD)]
    out += [f"w1_{m}" for m in range(KF)] + [f"w2_{m}" for m in range(KD)]

    def swiglu(p):
        return [f"{p}{w}{m}" for m in range(KF2) for w in "gu"] + [f"{p}d{m}" for m in range(KD)]

    out += swiglu("f1")
    out += [f"cq{b}" for b in range(3)] + [f"ckv{b}" for b in range(2)] + ["kr"] + [f"qm{b}" for b in range(4)]
    out += ["kr_rot"]
    out += [f"uq{h}" for h in range(8)] + [f"uk{b}" for b in range(4)] + ["uv0", "uv1", "sv0", "sv1"]
    out += [f"su{b}" for b in range(4)]
    out += [f"gate{b}" for b in range(24)]
    for m in range(KD):
        out += [f"br_a{m}", f"br_b{m}", f"br_c{m}"]
    out += [f"mix2_{m}" for m in range(KD)]
    out += swiglu("f2")
    return out


def attn_names():
    out = [f"ss_mem_k{b}" for b in range(4)]
    out += [f"ss_{n}" for n in ("ks", "kw", "qa0", "qa1", "qa2", "qa3")]
    out += ["sbz0", "sbz1", "sbz2", "ss_cmp"] + [f"sbz{h}" for h in range(3, 8)]
    out += ["nsa0a", "nsa0b", "nsa0c"]
    for i in range(8):
        if i < 7:
            out += [f"nsa{i + 1}{c}" for c in "abc"]
        out += [f"nsat{i}{c}" for c in "swc"]
    out += ["ss_cq", "ss_ckv"] + [f"ss_qm{b}" for b in range(4)]
    out += [f"ss_uq{h}" for h in range(8)] + [f"ss_uk{h}" for h in range(8)]
    out += ["mla0"]
    for h in range(8):
        out += [f"mla{h + 1}" if h < 7 else "mem0", f"mlat{h}"]
    for h in range(4):
        out += [f"mem{h + 1}"] * (h < 3) + [f"memt{h}"]
    out += [f"sg{b}{c}" for b in range(4) for c in range(TT)]
    return out


def long_names():
    out = [f"sbo{b}" for b in range(4)] + [f"nsao{b}" for b in range(4)] + ["x1_ss", "x2_ss", "x3_ss"]
    out += [f"mlao{b}" for b in range(4)] + [f"memo{b}" for b in range(4)] + ["x4_ss"]
    return out


ROW_MEM, ROW_X, ROW_1, ROW_2, ROW_3, ROW_4 = range(6)


def build(nc, stream, ada, x_t, mem_t, cols_d, mats_d, buckets_d, table_d, pos_d, cmp_w2_d,
          cmp_pos_d, sg_w_d, sg_b_d, sg_ln_d, out_t, taps=None):
    n_slots = stream.shape[0]
    where = plan_psum(proj_names(), attn_names(), long_names())

    with ExitStack() as ctx:
        def sb(name, shape, dt=F32):
            return ctx.enter_context(nc.sbuf_tensor(name, shape, dt))

        def sem(name):
            return ctx.enter_context(nc.semaphore(name))

        psum = [ctx.enter_context(nc.psum_tensor(f"bank{b}", [P, 512], F32)) for b in range(8)]

        rounded_view = {}

        def sb_split(name, shape):
            first = -(-nc.sbuf_base // 32) * 32
            t = sb(name, shape)
            rounded_view[t.name] = nc.alloc_sbuf_tensor_at(name + "_rounded", shape, F32R, offset=first)
            return t

        def R(ap):
            return bass.AP(rounded_view[ap.tensor.name], ap.offset, ap.ap)

        def flat(t):
            return t.rearrange("p a b -> p (a b)")

        def flat4(t):
            return t.rearrange("p a b c d -> p (a b c d)")

        ring = sb_split("ring", [P, RING * SLOT * P])
        rounded = sb_split("rounded", [P, HALVES * SLOT * P])
        ada_ring = sb("ada_ring", [P, ADA_RING, D])
        ada_acc = sb_split("ada_acc", [P, 2, D])
        mod = sb("mod", [P, 48])
        mats = sb("mats", [P, len(MATRICES), P])
        cols = sb("cols", [P, N_COLS])
        half_bias = sb("half_bias", [P, 24])
        c_act = sb("c_act", [P, 2, 8])
        x = sb("x", [P, KD, T])
        u = sb_split("u", [P, KD, T])
        u_lo = sb_split("u_lo", [P, KD, T])
        shared = sb_split("shared", [P, 32, T])
        hidden_lo = shared
        pair_k = shared[:, 0:8, :]
        pair_q = shared[:, 8:16, :]
        bias = shared[:, 16:24, :]
        attn_a, attn_b = shared[:, 24:28, :], shared[:, 28:32, :]
        attn_c = bias[:, 0:4, :]
        k_squares = bias[:, 4:8, :]
        mem_n_lo = pair_q
        attn_a_lo1, attn_b_lo1 = pair_k[:, 0:4, :], pair_q[:, 4:8, :]
        attn_a_lo2, attn_c_lo2 = pair_q[:, 0:4, :], bias[:, 4:8, :]
        cmp_sb = attn_a[0:32, 0, :].rearrange("p (w c) -> p w c", w=2)
        cmp_w2 = attn_a[:, 1, :].rearrange("p (w c) -> p w c", w=2)
        wide = sb_split("wide", [P, 32, T])
        gates, merged, hidden = wide[:, 0:24, :], wide[:, 24:32, :], wide
        merged_lo1, merged_lo2 = wide[:, 16:24, :], pair_k
        mem_n = wide[:, 0:8, :]
        bias_steps = wide[0:8, 8:23, :].rearrange("h a b -> h (a b)").rearrange("h (t c) -> h t c", c=N_CMP)
        squares = sb("squares", [P, SQ, T])
        log_ms = sb("log_ms", [P, T])
        rinv = sb("rinv", [P, 2, T])
        row_rinv = sb("row_rinv", [P, T])
        part = sb("part", [P, 2, T])
        mem_k = sb("mem_k", [P, 4, T])
        mem_v = sb("mem_v", [P, TT, 512])
        qa = sb("qa", [P, 4, T])
        kcat = sb_split("kcat", [P, 2, 528])
        attn_b_lo2 = flat(kcat[:, :, :])[:, 0:1024].rearrange("p (b t) -> p b t", t=T)
        vcat = sb("vcat", [P, TT, 2, 2, P])
        kc_ext = sb("kc_ext", [P, 2, 288])
        cmp_tanh = sb("cmp_tanh", [P, 2, 16])
        cmp_turned = sb("cmp_turned", [P, 2, 16])
        cmp_k = sb("cmp_k", [P, 4, 16])
        vcmp = sb("vcmp", [16, 2, P])
        pair_v = sb("pair_v", [P, TT, 8, P])
        bias_cmp = sb("bias_cmp", [P, 8, TT, N_CMP])
        lines = sb("lines", [33, 1024])
        buckets, bias_line, sg_b = lines[:, 0:512], lines[0:8, 512:1024], lines[0:1, :]
        table = sb("table", [33, 8])
        gate_raw = sb("gate_raw", [24, T])
        gate_tanh = sb("gate_tanh", [P, TT, 24])
        gate_t = sb("gate_t", [P, 8, 6])
        sbw = flat(wide[:, 16:28, :]).rearrange("p (a b c) -> p a b c", a=2, b=4)
        logit = flat(wide[:, 24:32, :])[:, 0:1600].rearrange("p (a b) -> p a b", a=2)
        ada_flat = flat(ada_acc[:, :, :])
        latent_lo = wide[:, 24:29, :]
        latent = ada_flat[:, 0:1280].rearrange("p (b t) -> p b t", t=T)
        kr = ada_flat[:, 1280:1792].rearrange("p (b t) -> p b t", t=T)
        pos = ada_flat[:, 1792:2048]
        sg_v = flat4(vcat[:, :, :, :, :])[:, 0:1024].rearrange("p (t c) -> p t c", t=TT)
        stats = sb("stats", [P, 2, 4, 6])
        turned = sb("turned", [P, 2, 2, 512])
        turned_c = turned[0:16, :, :, 384:512]
        row_squares = turned[:, :, :, :].rearrange("p a b c -> p (a b c)").rearrange("p (k t) -> p k t", t=T)
        pos_i = sb("pos_i", [P, T], I32)
        rope_n = row_squares[:, 0:4, :]
        rope = ada_ring[:, 0, :].rearrange("p (b t) -> p b t", t=T)
        sg_w = ada_ring[:, 1, :].rearrange("p (g t) -> p g t", t=P)
        sg_ln = ada_ring[:, 2, :].rearrange("p (w f) -> p w f", w=2)
        sg_stat = sb("sg_stat", [P, TT, 12])

        slot_full = [sem(f"slot_full{i}") for i in range(RING)]
        slot_used, slot_rounded, slot_split = sem("slot_used"), sem("slot_rounded"), sem("slot_split")
        ada_full = [sem(f"ada_full{i}") for i in range(ADA_RING)]
        ada_used = sem("ada_used")
        bank_full = [sem(f"bank_full{b}") for b in range(8)]
        bank_free = [sem(f"bank_free{b}") for b in range(8)]
        loaded = {n: sem(f"loaded_{n}") for n in ("x", "mem", "cols", "mats", "bias_in", "small", "pos", "sg", "bias")}
        stored = sem("stored")
        c_tanh_ready, c_ready = sem("c_tanh_ready"), sem("c_ready")
        zeros_ready, lines_ready, sg_w_ready = sem("zeros_ready"), sem("lines_ready"), sem("sg_w_ready")
        squares_ready, k_squares_ready = sem("squares_ready"), sem("k_squares_ready")
        row_squares_ready, row_rinv_ready = sem("row_squares_ready"), sem("row_rinv_ready")
        rinv_ready, log_ready, normed = sem("rinv_ready"), sem("log_ready"), sem("normed")
        u_normed, u_modulated, u_rounded, u_ready = sem("u_normed"), sem("u_modulated"), sem("u_rounded"), sem("u_ready")
        ada_summed, mod_ready, half_bias_ready = sem("ada_summed"), sem("mod_ready"), sem("half_bias_ready")
        gates_tanh_ready, gate_t_ready, tanh_ready = sem("gates_tanh_ready"), sem("gate_t_ready"), sem("tanh_ready")
        cmp_tanh_ready, cmp_rinv_ready, cmp_k_ready = sem("cmp_tanh_ready"), sem("cmp_rinv_ready"), sem("cmp_k_ready")
        sb_log_ready, softplus_ready, sb_logits_ready = sem("sb_log_ready"), sem("softplus_ready"), sem("sb_logits_ready")
        logits_ready, weights_raw, weights_ready = sem("logits_ready"), sem("weights_raw"), sem("weights_ready")
        merged_raw, merged_rounded, merged_ready = sem("merged_raw"), sem("merged_rounded"), sem("merged_ready")
        hidden_raw, hidden_rounded, hidden_ready = sem("hidden_raw"), sem("hidden_rounded"), sem("hidden_ready")
        latent_ready, k_pe_ready = sem("latent_ready"), sem("k_pe_ready")
        rope_angle_ready, rope_ready = sem("rope_angle_ready"), sem("rope_ready")
        sg_var_ready, sg_dev_ready, sg_ln_ready = sem("sg_var_ready"), sem("sg_dev_ready"), sem("sg_ln_ready")
        sg_ready = sem("sg_ready")
        act_step, dve_step = sem("act_step"), sem("dve_step")

        def full(eng, name):
            b, k = where[name]
            eng.wait_ge(bank_full[b], k + 1)

        def evacuated(eng, name):
            b, k = where[name]
            eng.wait_ge(bank_free[b], k + 1)

        first_plain = [c[0] for c in stream_chunks()].index("cmp_k_w1") // SLOT
        split_slots = [n for n in range(n_slots) if not first_plain <= n < first_plain + 64 // SLOT]
        nth_split = {n: q for q, n in enumerate(split_slots)}
        slot_at = {}

        def slot_weights(n):
            return ring[:, n % RING * SLOT * P:(n % RING + 1) * SLOT * P]

        def slot_round(q):
            return rounded[:, q % HALVES * SLOT * P:(q % HALVES + 1) * SLOT * P]

        def splitter(split):
            at = {"next": 0}

            def ahead(name):
                while at["next"] < len(split_slots) and split_slots[at["next"]] < slot_at[name] + HALVES:
                    split(at["next"], split_slots[at["next"]])
                    at["next"] += 1
            return ahead

        def bank(name):
            return psum[where[name][0]]

        def free(ins, name):
            ins.then_inc(bank_free[where[name][0]], 1)

        def mat(name):
            return mats[:, MAT[name], :]

        def col(name, i=0, rows=slice(0, P)):
            return cols[rows, AT[name] + i:AT[name] + i + 1]

        def chain(eng, s):
            n = [0]

            def step(ins):
                n[0] += 1
                ins.then_inc(s, 1)
                eng.wait_ge(s, n[0])
            return step

        LO, HI = slice(0, 64), slice(64, P)
        block = ctx.enter_context(nc.Block())

        @block.sync
        def _(sp):
            def load(r, i):
                sp.dma_start(ring[:, r * SLOT * P:(r + 1) * SLOT * P], stream[i]).then_inc(slot_full[r], 16)

            sp.dma_start(cols[:, :], cols_d).then_inc(loaded["cols"], 16)
            sp.dma_start(mem_n, mem_t).then_inc(loaded["mem"], 16)
            sp.dma_start(mats[:, :, :], mats_d).then_inc(loaded["mats"], 16)
            for r in range(RING):
                load(r, r)
                if r == 1:
                    sp.dma_start(x[:, :, :], x_t).then_inc(loaded["x"], 16)
                if r == 3:
                    sp.dma_start(buckets, buckets_d).then_inc(loaded["bias_in"], 16)
                    sp.dma_start(table[:, :], table_d).then_inc(loaded["bias_in"], 16)
            sp.dma_start(cmp_w2, cmp_w2_d).then_inc(loaded["small"], 16)
            for w in range(2):
                sp.dma_start(kc_ext[:, w, T:T + 32], cmp_pos_d).then_inc(loaded["small"], 16)
            sp.dma_start(pos_i[:, :], pos_d).then_inc(loaded["pos"], 16)
            rounds = n_slots // RING
            with sp.Fori(1, rounds) as i:
                for r in range(RING):
                    sp.wait_ge(slot_used, i * RING + (r + 1 - RING))
                    load(r, i * RING + r)
            for n in range(rounds * RING, n_slots):
                sp.wait_ge(slot_used, n + 1 - RING)
                load(n % RING, n)
            for m in range(KD):
                evacuated(sp, f"f2d{m}")
                sp.dma_start(out_t[:, m, :], x[:, m, :]).then_inc(stored, 16)
            sp.wait_ge(stored, 16 * KD)

        @block.gpsimd
        def _(pool):
            def load_ada(n):
                if n >= ADA_RING:
                    pool.wait_ge(ada_used, n - ADA_RING + 1)
                pool.dma_start(ada_ring[:, n % ADA_RING, :], ada[n]).then_inc(ada_full[n % ADA_RING], 16)

            for n in range(ADA_RING):
                load_ada(n)
            for t in (kcat[:], vcat[:], pair_k, pair_v[:], vcmp[:], kc_ext[:, :, 0:T]):
                pool.memset(t, 0.0).then_inc(zeros_ready, 1)
            for n in range(ADA_RING, 16):
                load_ada(n)
            evacuated(pool, "bias")
            for c in range(N_CMP):
                first = 2 * CMP_STRIDE - 1 + CMP_STRIDE * c
                last = pool.tensor_copy(bias_steps[:, :, c], bias_line[:, first:first + T])
            last.then_inc(lines_ready, 1)
            pool.wait_ge(lines_ready, 1)
            for h in range(8):
                line = bias_line[h:h + 1, :]
                pool.dma_start(bias[:, h, :], bass.AP(line.tensor, line.offset + P - 1, [[line.ap[0][0], 1], [-1, P], [1, T]])
                               ).then_inc(loaded["bias"], 16)
                step = bias_steps[h:h + 1, :, :]
                for t in range(TT):
                    pool.dma_start(bias_cmp[:, h, t, :],
                                   bass.AP(step.tensor, step.offset + (T - 1 - t * P) * N_CMP,
                                           [[step.ap[0][0], 1], [-N_CMP, P], [1, N_CMP]])).then_inc(loaded["bias"], 16)
            for n in range(16, 48):
                load_ada(n)
            pool.wait_ge(ada_used, 48)
            pool.dma_start(sg_w[:, :, :], sg_w_d).then_inc(loaded["sg"], 16)
            pool.wait_ge(loaded["bias"], 16 * 24)
            pool.dma_start(sg_b, sg_b_d).then_inc(loaded["sg"], 16)
            pool.dma_start(sg_ln[:, :, :], sg_ln_d).then_inc(loaded["sg"], 16)
            pool.wait_ge(loaded["sg"], 48)
            pool.affine_select(out=sg_w[:, :, :], in_=sg_w[:, :, :], compare_op=ALU.is_ge, fill=0.0, base=0,
                               pattern=[[0, 8], [1, P]], channel_multiplier=-1).then_inc(sg_w_ready, 1)

        @block.tensor
        def _(pe):
            at = {"chunk": 0, "owed": 0, "squares": 0}

            def mm(out, lhs, rhs, start=False, stop=False):
                return nc.tensor.matmul(out, lhs, rhs, start=start, stop=stop, skip_group_check=True)

            def claim(name):
                b, k = where[name]
                if k:
                    pe.wait_ge(bank_free[b], k)
                return psum[b]

            def done(ins, name):
                ins.then_inc(bank_full[where[name][0]], 1)
                slot_at[name] = max(at["chunk"] - 1, 0) // SLOT

            def take_plain():
                c = at["chunk"]
                if c % SLOT == 0:
                    i = c // SLOT
                    pe.wait_ge(slot_full[i % RING], 16 * (i // RING + 1))
                at["chunk"] = c + 1
                c %= RING * SLOT
                return ring[:, c * P:(c + 1) * P]

            def take(n=1):
                c = at["chunk"]
                slot, first = c // SLOT, c % SLOT * P
                if first == 0:
                    pe.wait_ge(slot_split, nth_split[slot] + 1)
                at["chunk"] = c + n
                return (R(slot_round(nth_split[slot])[:, first:first + n * P]),
                        R(slot_weights(slot)[:, first:first + n * P]))

            def give_back(ins, chunk):
                n = chunk // SLOT - at["owed"]
                if n > 0:
                    ins.then_inc(slot_used, n)
                    at["owed"] += n

            def project(name, k, rhs, ready=None):
                ps = claim(name)
                hi, lo = rhs
                for i in range(k):
                    chunk = at["chunk"]
                    w_hi, w_lo = take()
                    if ready:
                        ready(i)
                    give_back(mm(ps[:, 0:T], w_hi, R(hi[:, i, :]), i == 0), chunk)
                    mm(ps[:, 0:T], w_hi, R(lo[:, i, :]))
                    ins = mm(ps[:, 0:T], w_lo, R(hi[:, i, :]), stop=i == k - 1)
                done(ins, name)

            def project_tokens(names, k, lhs, width):
                ps = [claim(n) for n in names]
                hi, lo = lhs
                for i in range(k):
                    chunk = at["chunk"]
                    w_hi, w_lo = take(width // P)
                    for t in range(TT):
                        at_t = slice(t * P, (t + 1) * P)
                        ins = mm(ps[t][:, 0:width], R(hi[:, i, at_t]), w_hi, i == 0)
                        if t == 0:
                            give_back(ins, chunk)
                        mm(ps[t][:, 0:width], R(hi[:, i, at_t]), w_lo)
                        ins = mm(ps[t][:, 0:width], R(lo[:, i, at_t]), w_hi, stop=i == k - 1)
                        if i == k - 1:
                            done(ins, names[t])

            def sum_squares(name, matrix, n=1):
                ps = claim("ss_" + name)
                for i in range(n):
                    q = at["squares"]
                    at["squares"] += 1
                    pe.wait_ge(squares_ready, q + 1)
                    ins = mm(ps[:, 0:T], mat(matrix), squares[:, q % SQ, :], i == 0, i == n - 1)
                done(ins, "ss_" + name)

            def sum_row(name, row, src):
                ps = claim(name)
                for i in range(KD):
                    pe.wait_ge(row_squares_ready, row * KD + i + 1)
                    ins = mm(ps[:, 0:T], mat("ones"), src[:, i, :], i == 0, i == KD - 1)
                done(ins, name)

            def ada_part(j):
                pe.wait_ge(ada_summed, j + 1)
                for half in range(2):
                    name = f"ada{j}{'ab'[half]}"
                    ps = claim(name)
                    for i in range(4):
                        c = (half * 4 + i) * P
                        ins = nc.tensor.transpose(ps[:, i * P:(i + 1) * P], ada_acc[:, j % 2, c:c + P], mat("ident"))
                    done(ins, name)

            pe.wait_ge(loaded["mats"], 16)
            sum_row("mem_ss", ROW_MEM, row_squares)
            mem_parts, u_parts, hidden_parts = (mem_n, mem_n_lo), (u, u_lo), (hidden, hidden_lo)
            project("mem_k0", KD, mem_parts, lambda i: pe.wait_ge(u_ready, i + 1))
            project("mem_k1", KD, mem_parts)
            sum_squares("mem_k0", "ones")
            sum_row("x_ss", ROW_X, merged)
            project("mem_k2", KD, mem_parts)
            sum_squares("mem_k1", "ones")
            project("mem_k3", KD, mem_parts)
            sum_squares("mem_k2", "ones")
            pe.wait_ge(loaded["bias_in"], 32)
            done(mm(claim("bias")[0:8, 0:512], table[:, :], buckets[:, :], True, True), "bias")
            sum_squares("mem_k3", "ones")
            project_tokens(["mem_v0", "mem_v1"], KD, mem_parts, 512)
            ada_part(0)
            ada_part(1)

            pe.wait_ge(u_ready, (ROW_X + 1) * KD)
            project_tokens(["vsw0", "vsw1"], KD, u_parts, 256)
            project_tokens(["vsb0", "vsb1"], KD, u_parts, 512)
            project("ga", KD, u_parts)
            pe.wait_ge(loaded["small"], 48)
            for n in ("kc", "vc", "ks", "kw"):
                project(n, KD, u_parts)
            sum_squares("ks", "halves")
            for b in range(4):
                project(f"qa{b}", KD, u_parts)
                sum_squares(f"qa{b - 1}" if b else "kw", "halves")
            for b in range(4):
                project(f"kb{b}", KD, u_parts)
                if b == 0:
                    sum_squares("qa3", "halves")
            for b in range(4):
                project(f"qb{b}", KD, u_parts)
            ada_part(2)
            ada_part(3)

            for w, n in enumerate("kv"):
                evacuated(pe, n + "c" if n == "v" else "kc")
                name = f"cmp_hid_{n}"
                ps = claim(name)
                for j in range(32):
                    chunk = at["chunk"]
                    ins = mm(ps[0:N_CMP + 2, 0:P], kc_ext[:, w, j:j + 257:CMP_STRIDE], take_plain(), j == 0, j == 31)
                    if j < 31:
                        give_back(ins, chunk)
                done(ins, name)

            def cmp_turn():
                for w, n in enumerate("kv"):
                    evacuated(pe, f"cmp_hid_{n}")
                    ps = claim(f"cmp_turn_{n}")
                    done(mm(ps[:, 0:N_CMP], cmp_sb[0:N_CMP + 2, w, :], mats[0:N_CMP + 2, MAT["spread"], 0:N_CMP],
                            True, True), f"cmp_turn_{n}")
                evacuated(pe, "ga")
                ps = claim("ga_turn")
                for t in range(TT):
                    ins = mm(ps[:, t * 24:(t + 1) * 24], gate_raw[:, t * P:(t + 1) * P], mats[0:24, MAT["ident"], 0:24], t == 0, t == TT - 1)
                done(ins, "ga_turn")

            def cmp_out():
                evacuated(pe, "cmp_turn_k")
                ps = claim("cmp_out_k")
                done(mm(ps[:, 0:N_CMP], cmp_w2[:, 0, :], cmp_turned[:, 0, 0:N_CMP], True, True), "cmp_out_k")
                evacuated(pe, "cmp_turn_v")
                ps = claim("cmp_out_v")
                done(mm(ps[0:N_CMP, 0:P], cmp_turned[:, 1, 0:N_CMP], cmp_w2[:, 1, :], True, True), "cmp_out_v")

            def cmp_sum():
                evacuated(pe, "cmp_out_k")
                done(mm(claim("ss_cmp")[:, 0:N_CMP], mat("halves"), cmp_k[:, 1, 0:N_CMP], True, True), "ss_cmp")

            def sb_scores(h):
                evacuated(pe, f"kb{h // 2}")
                evacuated(pe, f"qb{h // 2}")
                ps = claim(f"sbz{h}")
                mm(ps[:, 0:T], pair_k[:, h, 0:P], pair_q[:, h // 2, :], True)
                done(mm(ps[:, T:T + P], pair_k[:, h, P:T], pair_q[:, h // 2, P:T], stop=True), f"sbz{h}")

            def sb_logits(h):
                pe.wait_ge(softplus_ready, h + 1)
                ps = bank(f"sbz{h}")
                soft = sbw[:, h % 2, 2, :]
                mm(ps[:, 0:T], mat("neg_suffix"), soft[:, 0:T])
                mm(ps[:, P:T], mat("neg_ones"), soft[:, T:T + P])
                mm(ps[:, T:T + P], mat("neg_suffix"), soft[:, T:T + P])
                mm(ps[:, 0:P], mat("ident"), mat("not_before"))
                mm(ps[:, T:T + P], mat("ident"), mat("not_before"), stop=True).then_inc(sb_logits_ready, 1)

            def sb_values(h):
                evacuated(pe, f"sbz{h}")
                name = f"sbo{h // 2}"
                ps = claim(name) if h % 2 == 0 else bank(name)
                w = sbw[:, h % 2, 3, :]
                mm(ps[:, 0:T], pair_v[:, 0, h, :], w[:, 0:T], h % 2 == 0)
                ins = mm(ps[:, P:T], pair_v[:, 1, h, :], w[:, T:T + P], stop=h % 2 == 1)
                if h % 2 == 1:
                    done(ins, name)

            evacuated(pe, "vsb0")
            evacuated(pe, "vsb1")
            sb_scores(0)
            for h in range(8):
                project(f"ma{h}", KD, u_parts)
                if h == 0:
                    cmp_turn()
                if h == 1:
                    cmp_out()
                if h == 2:
                    cmp_sum()
                if h == 5:
                    ada_part(4)
                if h < 7:
                    sb_scores(h + 1)
                sb_logits(h)
                if h:
                    sb_values(h - 1)
            sb_values(7)
            ada_part(5)

            def nsa_scores(i):
                b, s = i // 2, i % 2
                for c, q, k in (("a", slice(0, P), slice(0, 272)), ("b", slice(P, T), slice(0, 272)),
                                ("c", slice(P, T), slice(272, 528))):
                    ps = claim(f"nsa{i}{c}")
                    done(mm(ps[:, 0:k.stop - k.start], qa[:, b, q], kcat[:, s, k], True, True), f"nsa{i}{c}")

            def turn_block(ps, at_col, src):
                return nc.tensor.transpose(ps[:, at_col:at_col + P], src, mat("ident"))

            def nsa_turn(i):
                pe.wait_ge(weights_ready, i + 1)
                w = logit[:, i % 2, :]
                for br, c in enumerate("sw"):
                    ps = claim(f"nsat{i}{c}")
                    late = T + br * T
                    turn_block(ps, 0, w[:, br * P:(br + 1) * P])
                    turn_block(ps, P, w[:, late:late + P])
                    done(turn_block(ps, T, w[:, late + P:late + T]), f"nsat{i}{c}")
                ps = claim(f"nsat{i}c")
                turn_block(ps[0:N_CMP], 0, w[:, 768:768 + N_CMP])
                done(turn_block(ps[0:N_CMP], P, w[:, 784:784 + N_CMP]), f"nsat{i}c")

            def nsa_values(i):
                b, s = i // 2, i % 2
                name = f"nsao{b}"
                ps = claim(name) if s == 0 else bank(name)
                for br, c in enumerate("sw"):
                    evacuated(pe, f"nsat{i}{c}")
                    w = turned[:, i % 2, br, :]
                    mm(ps[:, 0:T], vcat[:, 0, br, s, :], w[:, 0:T], s == 0 and br == 0)
                    mm(ps[:, P:T], vcat[:, 1, br, s, :], w[:, T:T + P])
                evacuated(pe, f"nsat{i}c")
                ins = mm(ps[:, 0:T], vcmp[0:N_CMP, s, :], turned_c[0:N_CMP, i % 2, :, :], stop=s == 1)
                if s == 1:
                    done(ins, name)

            for n in ("vsw0", "vsw1", "ks", "kw", "qa0", "qa1", "qa2", "qa3", "cmp_out_v"):
                evacuated(pe, n)
            pe.wait_ge(cmp_k_ready, 1)
            nsa_scores(0)
            for i in range(8):
                project(f"mb{i}", KD, u_parts)
                if i < 7:
                    nsa_scores(i + 1)
                if i:
                    nsa_values(i - 1)
                nsa_turn(i)
            nsa_values(7)

            for m in range(KD):
                project(f"up_nsa{m}", 4, (attn_a, attn_a_lo1), (lambda i: evacuated(pe, f"nsao{i}")) if m == 0 else None)
                project(f"up_sb{m}", 4, (attn_b, attn_b_lo1), (lambda i: evacuated(pe, f"sbo{i}")) if m == 0 else None)
            for m in range(KD):
                project(f"mix{m}", KD, (merged, merged_lo1), (lambda i: pe.wait_ge(merged_ready, i + 1)) if m == 0 else None)

            sum_row("x1_ss", ROW_1, row_squares)
            for m in range(KF):
                project(f"w1_{m}", KD, u_parts, (lambda i: pe.wait_ge(u_ready, ROW_1 * KD + i + 1)) if m == 0 else None)
            for m in range(KD):
                project(f"w2_{m}", KF, hidden_parts, (lambda i: pe.wait_ge(hidden_ready, i + 1)) if m == 0 else None)

            def swiglu(p, row, before):
                for m in range(KF2):
                    for w in "gu":
                        first = m == 0 and w == "g"
                        project(f"{p}{w}{m}", KD, u_parts, (lambda i: pe.wait_ge(u_ready, row * KD + i + 1)) if first else None)
                for m in range(KD):
                    project(f"{p}d{m}", KF2, hidden_parts, (lambda i: pe.wait_ge(hidden_ready, before + i + 1)) if m == 0 else None)

            sum_row("x2_ss", ROW_2, row_squares)
            swiglu("f1", ROW_2, KF)

            sum_row("x3_ss", ROW_3, row_squares)
            for b in range(3):
                project(f"cq{b}", KD, u_parts, (lambda i: pe.wait_ge(u_ready, ROW_3 * KD + i + 1)) if b == 0 else None)
            project("ckv0", KD, u_parts)
            sum_squares("cq", "ones", 3)
            project("ckv1", KD, u_parts)
            project("kr", KD, u_parts)
            sum_squares("ckv", "ones", 2)
            project("qm0", KD, u_parts)
            project("qm1", KD, u_parts)
            sum_squares("qm0", "ones")
            project("qm2", KD, u_parts)
            sum_squares("qm1", "ones")
            project("qm3", KD, u_parts)
            sum_squares("qm2", "ones")
            evacuated(pe, "kr")
            done(mm(claim("kr_rot")[:, 0:T], mat("rotate"), kr[:, 0, :], True, True), "kr_rot")
            for h in range(8):
                project(f"uq{h}", 3, (latent, latent_lo), (lambda i: pe.wait_ge(latent_ready, i + 1)) if h == 0 else None)
                if h == 0:
                    sum_squares("qm3", "ones")
                else:
                    sum_squares(f"uq{h - 1}", "q_odd" if (h - 1) % 2 else "q_even")

            def sum_k_squares(b):
                for h in (2 * b, 2 * b + 1):
                    pe.wait_ge(k_squares_ready, h + 1)
                    done(mm(claim(f"ss_uk{h}")[:, 0:T], mat("ones"), k_squares[:, 2 * (h % 2) + b % 2, :], True, True),
                         f"ss_uk{h}")

            kv_latent = (latent[:, 3:5, :], latent_lo[:, 3:5, :])
            for b in range(4):
                project(f"uk{b}", 2, kv_latent, (lambda i: pe.wait_ge(latent_ready, 4 + i)) if b == 0 else None)
                if b == 0:
                    sum_squares("uq7", "q_odd")
                else:
                    sum_k_squares(b - 1)
            sum_k_squares(3)
            project_tokens(["uv0", "uv1"], 2, kv_latent, 512)
            project_tokens(["sv0", "sv1"], KD, u_parts, 512)
            for b in range(4):
                project(f"su{b}", KD, u_parts)

            def scores(i):
                if i < 8:
                    ps = claim(f"mla{i}")
                    mm(ps[:, 0:P], pair_q[:, i, 0:P], pair_k[:, i, 0:P], True)
                    done(mm(ps[:, P:384], pair_q[:, i, P:T], pair_k[:, i, :], stop=True), f"mla{i}")
                else:
                    h = i - 8
                    evacuated(pe, f"qm{h}")
                    evacuated(pe, f"mem_k{h}")
                    ps = claim(f"mem{h}")
                    mm(ps[:, 0:T], qa[:, h, 0:P], mem_k[:, h, :], True)
                    done(mm(ps[:, T:2 * T], qa[:, h, P:T], mem_k[:, h, :], stop=True), f"mem{h}")

            def turn(i):
                pe.wait_ge(weights_ready, 8 + i + 1)
                w = logit[:, i % 2, :]
                if i < 8:
                    ps = claim(f"mlat{i}")
                    for j in range(3):
                        ins = turn_block(ps, j * P, w[:, j * P:(j + 1) * P])
                    done(ins, f"mlat{i}")
                else:
                    ps = claim(f"memt{i - 8}")
                    for kt in range(2):
                        for qt in range(2):
                            j = qt * 2 + kt
                            ins = turn_block(ps, (kt * 2 + qt) * P, w[:, j * P:(j + 1) * P])
                    done(ins, f"memt{i - 8}")

            def values(i):
                w = turned[:, i % 2, 0, :]
                if i < 8:
                    evacuated(pe, f"mlat{i}")
                    name = f"mlao{i // 2}"
                    ps = claim(name) if i % 2 == 0 else bank(name)
                    mm(ps[:, 0:T], pair_v[:, 0, i, :], w[:, 0:T], i % 2 == 0)
                    ins = mm(ps[:, P:T], pair_v[:, 1, i, :], w[:, T:T + P], stop=i % 2 == 1)
                    if i % 2:
                        done(ins, name)
                else:
                    h = i - 8
                    evacuated(pe, f"memt{h}")
                    ps = claim(f"memo{h}")
                    mm(ps[:, 0:T], mem_v[:, 0, h * P:(h + 1) * P], w[:, 0:T], True)
                    done(mm(ps[:, 0:T], mem_v[:, 1, h * P:(h + 1) * P], w[:, T:2 * T], stop=True), f"memo{h}")

            for n in ("uv0", "uv1", "mem_v0", "mem_v1"):
                evacuated(pe, n)
            pe.wait_ge(normed, 16)
            scores(0)
            for i in range(12):
                project(f"gate{2 * i}", KD, u_parts)
                project(f"gate{2 * i + 1}", KD, u_parts)
                if i < 11:
                    scores(i + 1)
                if i:
                    values(i - 1)
                turn(i)
            pe.wait_ge(sg_ln_ready, TT)
            pe.wait_ge(sg_w_ready, 1)
            for b in range(4):
                for c in range(TT):
                    name = f"sg{b}{c}"
                    ps = claim(name)
                    mm(ps[:, 0:T], sg_v[:, c, b * P:(b + 1) * P], sg_w[:, 2 * b:2 * b + 2, :], True)
                    done(mm(ps[:, 0:T], mats[0:1, MAT["ones"], :], sg_b[:, b * T:(b + 1) * T], stop=True), name)
            values(11)

            pe.wait_ge(sg_ready, 4)
            for m in range(KD):
                project(f"br_a{m}", 4, (attn_a, attn_a_lo2))
                project(f"br_b{m}", 4, (attn_b, attn_b_lo2), (lambda i: evacuated(pe, f"mlao{i}")) if m == 0 else None)
                project(f"br_c{m}", 4, (attn_c, attn_c_lo2), (lambda i: evacuated(pe, f"memo{i}")) if m == 0 else None)
            for m in range(KD):
                project(f"mix2_{m}", KD, (merged, merged_lo2), (lambda i: pe.wait_ge(merged_ready, KD + i + 1)) if m == 0 else None)
            sum_row("x4_ss", ROW_4, row_squares)
            swiglu("f2", ROW_4, KF + KF2)

        @block.scalar
        def _(act):
            n_squares, n_rinv, n_row = [0], [0], [0]
            step = chain(act, act_step)
            a = nc.scalar.activation

            def round_slot(q, n):
                act.wait_ge(slot_full[n % RING], 16 * (n // RING + 1))
                if q >= HALVES:
                    act.wait_ge(slot_used, split_slots[q - HALVES] + 1)
                a(R(slot_round(q)), slot_weights(n), ACT.Copy).then_inc(slot_rounded, 1)

            ahead = splitter(round_slot)

            def output(name):
                ahead(name)
                full(act, name)

            def taken(name):
                ahead(name)
                evacuated(act, name)

            def square(name):
                n = n_squares[0]
                n_squares[0] += 1
                output(name)
                a(squares[:, n % SQ, :], bank(name)[:, 0:T], ACT.Square).then_inc(squares_ready, 1)

            def inv_rms(name, width, last_reader):
                n = n_rinv[0]
                n_rinv[0] += 1
                output("ss_" + name)
                free(a(log_ms[:, :], bank("ss_" + name)[:, 0:T], ACT.Ln, scale=1.0 / width, bias=col("eps")), "ss_" + name)
                taken("ss_" + name)
                if last_reader:
                    last_reader()
                a(rinv[:, n % 2, :], log_ms[:, :], ACT.Exp, scale=-0.5).then_inc(rinv_ready, 1)
                act.wait_ge(rinv_ready, n + 1)

            def row_square(dst, src, ready=None):
                for i in range(KD):
                    if ready:
                        ready(i)
                    a(dst[:, i, :], src[:, i, :], ACT.Square).then_inc(row_squares_ready, 1)

            def row_inv(name):
                n_row[0] += 1
                output(name)
                free(a(log_ms[:, :], bank(name)[:, 0:T], ACT.Ln, scale=1.0 / D, bias=col("eps")), name)
                taken(name)
                a(row_rinv[:, :], log_ms[:, :], ACT.Exp, scale=-0.5).then_inc(row_rinv_ready, 1)
                act.wait_ge(row_rinv_ready, n_row[0])

            def modulate(row, first, scale, shift):
                for i in range(KD + 1):
                    if i < KD:
                        act.wait_ge(u_normed, row * KD + i + 1)
                        a(u_lo[:, i, :], u_lo[:, i, :], ACT.Identity, scale=mod[:, scale * 8 + i:scale * 8 + i + 1],
                          bias=mod[:, shift * 8 + i:shift * 8 + i + 1]).then_inc(u_modulated, 1)
                    if i:
                        act.wait_ge(u_modulated, first + i)
                        a(R(u[:, i - 1, :]), u_lo[:, i - 1, :], ACT.Copy).then_inc(u_rounded, 1)

            def round_row(row, hi, lo):
                for i in range(KD):
                    act.wait_ge(u_normed, row * KD + i + 1)
                    a(R(hi[:, i, :]), lo[:, i, :], ACT.Copy).then_inc(u_rounded, 1)

            def copy(dst, name, src=None, **kw):
                output(name)
                free(a(dst, bank(name)[:, 0:T] if src is None else src, ACT.Copy, **kw), name)

            def spread_heads(dst, name):
                output(name)
                src = bank(name)[:, :].rearrange("p (b s d) -> p b s d", s=2, d=HD)
                dst = dst.rearrange("p (b s) c -> p b s c", s=2)
                a(dst[:, :, 0, 0:HD], src[:, :, 0, :], ACT.Copy)
                free(a(dst[:, :, 1, HD:P], src[:, :, 1, :], ACT.Copy), name)

            nc.scalar.preload_act_table_set("exp_and_others")
            act.wait_ge(loaded["cols"], 16)
            a(c_act[:, 0, :], cols[:, AT["c"]:AT["c"] + 8], ACT.Tanh, scale=0.5).then_inc(c_tanh_ready, 1)
            nc.scalar.preload_act_table_set("natural_log_exp_and_others")
            act.wait_ge(loaded["mem"], 16)
            row_square(row_squares, mem_n)
            row_inv("mem_ss")
            round_row(ROW_MEM, mem_n, mem_n_lo)
            square("mem_k0")
            act.wait_ge(loaded["x"], 16)
            row_square(merged, x)
            square("mem_k1")
            inv_rms("mem_k0", P, None)
            act.wait_ge(u_normed, KD)
            row_inv("x_ss")
            square("mem_k2")
            inv_rms("mem_k1", P, None)
            square("mem_k3")
            inv_rms("mem_k2", P, lambda: taken("mem_k0"))
            inv_rms("mem_k3", P, lambda: taken("mem_k1"))
            for t in range(TT):
                copy(mem_v[:, t, :], f"mem_v{t}", bank(f"mem_v{t}")[:, :])
            act.wait_ge(mod_ready, 2)
            modulate(ROW_X, 0, 1, 0)

            act.wait_ge(zeros_ready, 6)
            for t in range(TT):
                output(f"vsw{t}")
                src = bank(f"vsw{t}")[:, 0:256].rearrange("p (r s d) -> p r s d", r=2, d=HD)
                a(vcat[:, t, :, 0, 0:HD], src[:, :, 0, :], ACT.Copy)
                free(a(vcat[:, t, :, 1, HD:P], src[:, :, 1, :], ACT.Copy), f"vsw{t}")
            for t in range(TT):
                spread_heads(pair_v[:, t, :, :], f"vsb{t}")
            copy(gate_raw[:, :], "ga", bank("ga")[0:24, 0:T])
            for w, n in enumerate(("kc", "vc")):
                copy(kc_ext[:, w, 0:T], n)
            square("ks")
            square("kw")
            inv_rms("ks", HD, lambda: taken("mem_k2"))
            for b in range(4):
                square(f"qa{b}")
                inv_rms(f"qa{b - 1}" if b else "kw", HD, lambda: taken(("mem_k3", "ks", "kw", "qa0")[b]))
            inv_rms("qa3", HD, lambda: taken("qa1"))
            for b in range(4):
                copy(pair_q[:, b, :], f"qb{b}", scale=HD ** -0.5)
            for w, n in enumerate("kv"):
                copy(cmp_sb[0:N_CMP + 2, w, :], f"cmp_hid_{n}", bank(f"cmp_hid_{n}")[0:N_CMP + 2, 0:P])

            def sb_log(h):
                output(f"sbz{h}")
                w = sbw[:, h % 2, :, :]
                step(a(w[:, 0, :], bank(f"sbz{h}")[:, 0:384], ACT.Abs))
                step(a(w[:, 0, :], w[:, 0, :], ACT.Exp, scale=-1.0))
                a(w[:, 1, :], w[:, 0, :], ACT.Ln, bias=1.0).then_inc(sb_log_ready, 1)

            def sb_exp(h):
                act.wait_ge(sb_logits_ready, h + 1)
                free(a(sbw[:, h % 2, 3, :], bank(f"sbz{h}")[:, 0:384], ACT.Exp), f"sbz{h}")

            sb_log(0)
            act.wait_ge(loaded["bias"], 16 * 24)
            for h in range(8):
                copy(gates[:, h, :], f"ma{h}")
                if h == 0:
                    nc.scalar.preload_act_table_set("exp_and_others")
                    for w, n in enumerate("kv"):
                        output(f"cmp_turn_{n}")
                        a(cmp_tanh[:, w, 0:N_CMP], bank(f"cmp_turn_{n}")[:, 0:N_CMP], ACT.Tanh, scale=0.5).then_inc(cmp_tanh_ready, 1)
                    output("ga_turn")
                    free(a(gate_tanh[:, :, :], bank("ga_turn")[:, 0:48].rearrange("p (t g) -> p t g", t=TT), ACT.Tanh, scale=0.5), "ga_turn")
                    nc.scalar.preload_act_table_set("natural_log_exp_and_others")
                if h == 1:
                    output("cmp_out_k")
                    a(cmp_k[:, 0, 0:N_CMP], bank("cmp_out_k")[:, 0:N_CMP], ACT.Copy)
                    free(a(cmp_k[:, 1, 0:N_CMP], bank("cmp_out_k")[:, 0:N_CMP], ACT.Square), "cmp_out_k")
                    output("cmp_out_v")
                    ps = bank("cmp_out_v")
                    a(vcmp[0:N_CMP, 0, 0:HD], ps[0:N_CMP, 0:HD], ACT.Copy)
                    free(a(vcmp[0:N_CMP, 1, HD:P], ps[0:N_CMP, HD:P], ACT.Copy), "cmp_out_v")
                if h == 2:
                    output("ss_cmp")
                    free(a(cmp_k[:, 2, 0:N_CMP], bank("ss_cmp")[:, 0:N_CMP], ACT.Ln, scale=1.0 / HD, bias=col("eps")), "ss_cmp")
                    taken("ss_cmp")
                    a(cmp_k[:, 3, 0:N_CMP], cmp_k[:, 2, 0:N_CMP], ACT.Exp, scale=-0.5).then_inc(cmp_rinv_ready, 1)
                if h < 7:
                    sb_log(h + 1)
                sb_exp(h)

            def exps(i, parts):
                act.wait_ge(logits_ready, i + 1)
                for k, (src, dst) in parts.items():
                    ins = a(dst, src, ACT.Exp, bias=stats[:, i % 2, 0, k:k + 1], accum_out=stats[:, i % 2, 1, k:k + 1])
                ins.then_inc(weights_raw, 1)

            def nsa_exp(i):
                w = logit[:, i % 2, :]
                at = [w[:, 0:128], w[:, 128:256], w[:, 256:512], w[:, 512:768], w[:, 768:768 + N_CMP], w[:, 784:784 + N_CMP]]
                exps(i, {k: (s, s) for k, s in enumerate(at)})

            nc.scalar.preload_act_table_set("exp_and_others")
            nsa_exp(0)
            for i in range(8):
                output(f"mb{i}")
                free(a(gates[:, 8 + i, :], bank(f"mb{i}")[:, 0:T], ACT.Tanh, scale=0.5), f"mb{i}")
                if i % 2 == 0:
                    k = i
                    taken(f"ma{k + 1}")
                    a(gates[:, k:k + 2, :], gates[:, k:k + 2, :], ACT.Tanh, scale=0.5).then_inc(tanh_ready, 1)
                if i < 7:
                    nsa_exp(i + 1)
                copy(turned[:, i % 2, 0, 0:384], f"nsat{i}s", bank(f"nsat{i}s")[:, 0:384])
                copy(turned_c[0:N_CMP, i % 2, :, :], f"nsat{i}c",
                     bank(f"nsat{i}c")[0:N_CMP, 0:T].rearrange("p (t q) -> p t q", t=TT))

            def round_merged(before, lo):
                for m in range(KD):
                    ahead(f"{'up_sb' if before == 0 else 'br_c'}{m}")
                    act.wait_ge(merged_raw, before + m + 1)
                    a(R(merged[:, m, :]), lo[:, m, :], ACT.Copy).then_inc(merged_rounded, 1)

            def round_hidden(i):
                a(R(hidden[:, i, :]), hidden_lo[:, i, :], ACT.Copy).then_inc(hidden_rounded, 1)

            round_merged(0, merged_lo1)

            nc.scalar.preload_act_table_set("natural_log_exp_and_others")
            row_square(row_squares, x, lambda i: taken(f"mix{i}"))
            row_inv("x1_ss")
            act.wait_ge(mod_ready, 6)
            modulate(ROW_1, KD, 4, 3)
            for m in range(KF):
                output(f"w1_{m}")
                if m >= 2:
                    act.wait_ge(hidden_raw, m - 1)
                free(a(part[:, m % 2, :], bank(f"w1_{m}")[:, 0:T], ACT.Relu), f"w1_{m}")
                if m:
                    act.wait_ge(hidden_raw, m)
                    round_hidden(m - 1)
            act.wait_ge(hidden_raw, KF)
            round_hidden(KF - 1)
            row_square(row_squares, x, lambda i: taken(f"w2_{i}"))
            row_inv("x2_ss")
            round_row(ROW_2, u, u_lo)

            act.wait_ge(rope_angle_ready, 1)
            a(rope[:, :, :], rope[:, :, :], ACT.Sin).then_inc(rope_ready, 1)

            def swiglu(p):
                for m in range(KF2):
                    output(f"{p}g{m}")
                    if m >= 2:
                        taken(f"{p}u{m - 2}")
                    free(a(part[:, m % 2, :], bank(f"{p}g{m}")[:, 0:T], ACT.Silu), f"{p}g{m}")
                    if m:
                        taken(f"{p}u{m - 1}")
                        round_hidden(m - 1)
                taken(f"{p}u{KF2 - 1}")
                round_hidden(KF2 - 1)

            swiglu("f1")

            nc.scalar.preload_act_table_set("natural_log_exp_and_others")
            row_square(row_squares, x, lambda i: taken(f"f1d{i}"))
            row_inv("x3_ss")
            round_row(ROW_3, u, u_lo)

            def latent_block(i, name, gain, k):
                square(name)
                free(a(latent[:, i, :], bank(name)[:, 0:T], ACT.Copy, scale=col(gain, k)), name)

            for b in range(3):
                latent_block(b, f"cq{b}", "mla_cq_norm_2", b)
            inv_rms("cq", 384, lambda: taken("qa2"))
            latent_block(3, "ckv0", "mla_ckv_norm_2", 0)
            latent_block(4, "ckv1", "mla_ckv_norm_2", 1)
            output("kr")
            ps = bank("kr")
            for s in range(2):
                a(k_squares[HI, s, :], ps[HI, 0:T], ACT.Square, scale=0.5 ** 0.5)
                a(k_squares[LO, 2 + s, :], ps[LO, 0:T], ACT.Square, scale=0.5 ** 0.5)
            free(a(kr[:, 0, :], ps[:, 0:T], ACT.Copy, scale=col("mla_k_rope")), "kr")
            inv_rms("ckv", 256, lambda: taken("qa3"))
            square("qm0")
            square("qm1")
            inv_rms("qm0", P, lambda: act.wait_ge(latent_ready, 3))
            square("qm2")
            inv_rms("qm1", P, lambda: act.wait_ge(latent_ready, 5))
            square("qm3")
            inv_rms("qm2", P, lambda: taken("qm0"))
            square("uq0")
            inv_rms("qm3", P, lambda: taken("qm1"))
            for h in range(1, 8):
                square(f"uq{h}")
                inv_rms(f"uq{h - 1}", 96, lambda: taken(f"qm{h + 1}") if h < 3 else act.wait_ge(normed, h - 2))

            def k_square(b):
                output(f"uk{b}")
                ps = bank(f"uk{b}")
                a(k_squares[LO, b % 2, :], ps[LO, 0:T], ACT.Square).then_inc(k_squares_ready, 1)
                a(k_squares[HI, 2 + b % 2, :], ps[HI, 0:T], ACT.Square).then_inc(k_squares_ready, 1)

            k_square(0)
            inv_rms("uq7", 96, lambda: act.wait_ge(normed, 6))
            for b in range(4):
                if b < 3:
                    k_square(b + 1)
                for h in (2 * b, 2 * b + 1):
                    inv_rms(f"uk{h}", 96, lambda: act.wait_ge(normed, 7 + h))
            for t in range(TT):
                spread_heads(pair_v[:, t, :, :], f"uv{t}")
            nc.scalar.preload_act_table_set("gelu_and_others")
            for t in range(TT):
                output(f"sv{t}")
                free(a(sg_v[:, t, :], bank(f"sv{t}")[:, :], ACT.Gelu), f"sv{t}")
            for b in range(4):
                output(f"su{b}")
                free(a(attn_a[:, b, :], bank(f"su{b}")[:, 0:T], ACT.Gelu), f"su{b}")
            nc.scalar.preload_act_table_set("natural_log_exp_and_others")
            act.wait_ge(sg_var_ready, 1)
            step(a(sg_stat[:, :, 8], sg_stat[:, :, 7], ACT.Ln, bias=col("eps")))
            a(sg_stat[:, :, 9], sg_stat[:, :, 8], ACT.Exp, scale=-0.5).then_inc(sg_dev_ready, 1)

            nc.scalar.preload_act_table_set("exp_and_others")

            def attend(i):
                w = logit[:, i % 2, :]
                if i < 8:
                    exps(8 + i, {0: (w[:, 0:P],) * 2, 1: (w[:, P:384],) * 2})
                else:
                    ps = bank(f"mem{i - 8}")
                    act.wait_ge(logits_ready, 8 + i + 1)
                    a(w[:, 0:T], ps[:, 0:T], ACT.Exp, scale=P ** -0.5, bias=stats[:, i % 2, 0, 0:1],
                      accum_out=stats[:, i % 2, 1, 0:1])
                    a(w[:, T:2 * T], ps[:, T:2 * T], ACT.Exp, scale=P ** -0.5, bias=stats[:, i % 2, 0, 1:2],
                      accum_out=stats[:, i % 2, 1, 1:2]).then_inc(weights_raw, 1)
                    act.wait_ge(weights_raw, 8 + i + 1)
                    free(a(stats[:, i % 2, 3, 5:6], stats[:, i % 2, 1, 1:2], ACT.Copy), f"mem{i - 8}")

            act.wait_ge(half_bias_ready, 1)
            attend(0)
            for i in range(12):
                for g in (2 * i, 2 * i + 1):
                    output(f"gate{g}")
                    free(a(gates[:, g, :], bank(f"gate{g}")[:, 0:T], ACT.Tanh, scale=0.5, bias=half_bias[:, g:g + 1]), f"gate{g}")
                if i < 11:
                    attend(i + 1)
                if i < 8:
                    copy(turned[:, i % 2, 0, 0:384], f"mlat{i}", bank(f"mlat{i}")[:, 0:384])
                else:
                    copy(turned[:, i % 2, 0, :], f"memt{i - 8}", bank(f"memt{i - 8}")[:, :])
            round_merged(KD, merged_lo2)

            nc.scalar.preload_act_table_set("natural_log_exp_and_others")
            row_square(row_squares, x, lambda i: taken(f"mix2_{i}"))
            row_inv("x4_ss")
            round_row(ROW_4, u, u_lo)
            swiglu("f2")
            for m in range(KD):
                ahead(f"f2d{m}")

        @block.vector
        def _(dve):
            v = nc.vector
            step = chain(dve, dve_step)
            n_rinv, n_ada = [0], [0]

            def split_slot(q, n):
                dve.wait_ge(slot_rounded, q + 1)
                w = slot_weights(n)
                v.tensor_tensor(R(w), w, R(slot_round(q)), ALU.subtract).then_inc(slot_split, 1)

            ahead = splitter(split_slot)

            def output(name):
                ahead(name)
                full(dve, name)

            def taken(name):
                ahead(name)
                evacuated(dve, name)

            def split_output(hi, lo, name):
                output(name)
                step(v.tensor_copy(R(hi), bank(name)[:, 0:T]))
                free(v.tensor_tensor(R(lo), bank(name)[:, 0:T], R(hi), ALU.subtract), name)

            def take_rinv():
                n = n_rinv[0]
                n_rinv[0] += 1
                dve.wait_ge(rinv_ready, n + 1)
                return rinv[:, n % 2, :]

            def normalise(name, outs, gain, rows=(slice(0, P),)):
                ahead(name)
                r = take_rinv()
                for out, rr in zip(outs, rows):
                    ins = v.scalar_tensor_tensor(out=out, in0=bank(name)[rr, 0:T], scalar=col(gain, 0, rr), in1=r[rr, :],
                                                 op0=ALU.mult, op1=ALU.mult)
                free(ins, name)

            def norm_row(hi, lo, src, gain, row, lag=2):
                dve.wait_ge(row_rinv_ready, row + 1)
                for i in range(KD + lag):
                    if i < KD:
                        v.scalar_tensor_tensor(out=lo[:, i, :], in0=src[:, i, :], scalar=col(gain, i), in1=row_rinv[:, :],
                                               op0=ALU.mult, op1=ALU.mult).then_inc(u_normed, 1)
                    if i >= lag:
                        rest(hi, lo, row, i - lag)

            def rest(hi, lo, row, i):
                dve.wait_ge(u_rounded, row * KD + i + 1)
                v.tensor_tensor(R(lo[:, i, :]), lo[:, i, :], R(hi[:, i, :]), ALU.subtract).then_inc(u_ready, 1)

            def ada_step():
                n = n_ada[0]
                n_ada[0] += 1
                j, k = n // KD, n % KD
                acc = ada_acc[:, j % 2, :]
                dve.wait_ge(ada_full[n % ADA_RING], 16 * (n // ADA_RING + 1))
                w = ada_ring[:, n % ADA_RING, :]
                c = c_act[:, 1, k:k + 1]
                if k == 0:
                    if j >= 2:
                        output(f"ada{j - 2}b")
                    v.tensor_scalar(acc, w, c, None, ALU.mult).then_inc(ada_used, 1)
                else:
                    dve.wait_ge(ada_used, n)
                    v.scalar_tensor_tensor(out=acc, in0=w, scalar=c, in1=acc, op0=ALU.mult, op1=ALU.add).then_inc(ada_used, 1)
                if k == KD - 1:
                    dve.wait_ge(ada_used, n + 1)
                    v.tensor_copy(c_act[:, 0, 0:1], c_act[:, 1, 0:1]).then_inc(ada_summed, 1)

            def ada_reduce(j):
                at = mod[:, j * 8:(j + 1) * 8]
                for half in range(2):
                    name = f"ada{j}{'ab'[half]}"
                    output(name)
                    free(v.tensor_reduce(out=at[:, half * 4:half * 4 + 4], in_=bank(name)[:, :].rearrange("p (k i) -> p k i", i=P),
                                         axis=AX.X, op=ALU.add), name)
                taken(f"ada{j}a")
                taken(f"ada{j}b")
                b = cols[:, AT["ada_b"] + j * 8:AT["ada_b"] + (j + 1) * 8]
                if j in (1, 4):
                    v.scalar_tensor_tensor(out=at, in0=at, scalar=1.0, in1=b, op0=ALU.add, op1=ALU.add).then_inc(mod_ready, 1)
                elif j == 2:
                    step(v.tensor_tensor(at, at, b, ALU.add))
                    v.tensor_scalar(at, at, 0.5, None, ALU.mult).then_inc(mod_ready, 1)
                else:
                    v.tensor_tensor(at, at, b, ALU.add).then_inc(mod_ready, 1)

            dve.wait_ge(c_tanh_ready, 1)
            step(v.tensor_scalar(c_act[:, 0, :], c_act[:, 0, :], 0.5, 0.5, ALU.mult, ALU.add))
            step(v.tensor_tensor(c_act[:, 1, :], c_act[:, 0, :], cols[:, AT["c"]:AT["c"] + 8], ALU.mult))
            ahead("mem_ss")
            norm_row(mem_n, mem_n_lo, mem_n, "mem_norm_2", ROW_MEM)
            for b in range(4):
                normalise(f"mem_k{b}", [mem_k[:, b, :]], "mem_k_norm_2")
                for _ in range(4):
                    ada_step()
                if b == 2:
                    output("bias")
                    free(v.tensor_copy(bias_line, bank("bias")[0:8, :]), "bias")
                if b == 1:
                    dve.wait_ge(row_rinv_ready, ROW_X + 1)
                    for i in range(KD):
                        v.scalar_tensor_tensor(out=u_lo[:, i, :], in0=x[:, i, :], scalar=col("norm1_g", i), in1=row_rinv[:, :],
                                               op0=ALU.mult, op1=ALU.mult).then_inc(u_normed, 1)
            v.tensor_scalar(half_bias[:, :], cols[:, AT["b_gate_2"]:AT["b_gate_2"] + 24], 0.5, None, ALU.mult).then_inc(half_bias_ready, 1)
            ada_reduce(0)
            ada_reduce(1)
            for i in range(KD):
                rest(u, u_lo, ROW_X, i)

            for _ in range(16):
                ada_step()
            dve.wait_ge(zeros_ready, 6)
            for n, off in (("ks", 0), ("kw", P)):
                ahead(n)
                r = take_rinv()
                late = 272 + off
                for s, rr in enumerate((LO, HI)):
                    for first, dst in ((0, off), (P, late)):
                        ins = v.scalar_tensor_tensor(out=kcat[rr, s, dst:dst + P], in0=bank(n)[rr, first:first + P],
                                                     scalar=col("k_slc_norm" if n == "ks" else "k_win_norm", 0, rr),
                                                     in1=r[rr, first:first + P], op0=ALU.mult, op1=ALU.mult)
                free(ins, n)
            for b in range(4):
                normalise(f"qa{b}", [qa[:, b, :]], "q_norm")
            for b in range(4):
                output(f"kb{b}")
                ps = bank(f"kb{b}")
                v.tensor_copy(pair_k[LO, 2 * b, :], ps[LO, 0:T])
                free(v.tensor_copy(pair_k[HI, 2 * b + 1, :], ps[HI, 0:T]), f"kb{b}")
            ada_reduce(2)
            ada_reduce(3)

            before = mat("before")

            def softplus(h):
                ahead(f"sbz{h}")
                dve.wait_ge(sb_log_ready, h + 1)
                w = sbw[:, h % 2, :, :]
                step(v.scalar_tensor_tensor(out=w[:, 2, :], in0=bank(f"sbz{h}")[:, 0:384], scalar=0.0, in1=w[:, 1, :],
                                            op0=ALU.max, op1=ALU.add))
                v.tensor_tensor(w[:, 2, 0:P], w[:, 2, 0:P], before, ALU.mult)
                v.tensor_tensor(w[:, 2, T:T + P], w[:, 2, T:T + P], before, ALU.mult).then_inc(softplus_ready, 1)

            softplus(0)
            for h in range(8):
                if h == 0:
                    for w, n in enumerate("kv"):
                        ahead(f"cmp_turn_{n}")
                        dve.wait_ge(cmp_tanh_ready, w + 1)
                        th = cmp_tanh[:, w, 0:N_CMP]
                        step(v.tensor_scalar(th, th, 0.5, 0.5, ALU.mult, ALU.add))
                        free(v.tensor_tensor(cmp_turned[:, w, 0:N_CMP], th, bank(f"cmp_turn_{n}")[:, 0:N_CMP], ALU.mult), f"cmp_turn_{n}")
                    taken("ga_turn")
                    step(v.tensor_scalar(gate_tanh[:, :, :], gate_tanh[:, :, :], 0.5, 0.5, ALU.mult, ALU.add))
                    for t in range(TT):
                        g = gate_tanh[:, t, :].rearrange("p (h r) -> p h r", r=3)
                        v.tensor_copy(gate_t[:, :, 2 * t:2 * t + 2], g[:, :, 1:3])
                        v.tensor_scalar(gate_t[:, :, 4 + t], g[:, :, 0], col("sees_a_block", t), None, ALU.mult).then_inc(gate_t_ready, 1)
                if h == 2:
                    ahead("ss_cmp")
                    dve.wait_ge(cmp_rinv_ready, 1)
                    for s, rr in enumerate((LO, HI)):
                        ins = v.scalar_tensor_tensor(out=kcat[rr, s, T:T + N_CMP], in0=cmp_k[rr, 0, 0:N_CMP],
                                                     scalar=col("k_cmp_norm", 0, rr), in1=cmp_k[rr, 3, 0:N_CMP],
                                                     op0=ALU.mult, op1=ALU.mult)
                    ins.then_inc(cmp_k_ready, 1)
                if h < 7:
                    softplus(h + 1)
                ada_step()
                ada_step()
                if h and h % 2 == 0:
                    split_output(attn_b[:, h // 2 - 1, :], attn_b_lo1[:, h // 2 - 1, :], f"sbo{h // 2 - 1}")
                if h == 5:
                    ada_reduce(4)
            split_output(attn_b[:, 3, :], attn_b_lo1[:, 3, :], "sbo3")
            ada_reduce(5)

            def nsa_logits(i):
                h = i // 2 + 4 * (i % 2)
                w, st = logit[:, i % 2, :], stats[:, i % 2, :, :]
                if i >= 2:
                    output(f"nsat{i - 2}c")
                early = w[:, 0:256].rearrange("p (r k) -> p r k", r=2)
                late = w[:, 256:768].rearrange("p (r k) -> p r k", r=2)

                def add(out, ps, b):
                    return v.scalar_tensor_tensor(out=out, in0=ps, scalar=HD ** -0.5, in1=b, op0=ALU.mult, op1=ALU.add)

                def both(b):
                    return b.unsqueeze(1).to_broadcast([P, 2, P])

                for c, t, dst, b in (("a", 0, early, bias[:, h, P:T]), ("b", 1, late[:, :, 0:P], bias[:, h, 0:P])):
                    output(f"nsa{i}{c}")
                    ps = bank(f"nsa{i}{c}")
                    add(dst, ps[:, 0:256].rearrange("p (r k) -> p r k", r=2), both(b))
                    free(add(w[:, 768 + 16 * t:768 + 16 * t + N_CMP], ps[:, T:T + N_CMP], bias_cmp[:, h, t, :]), f"nsa{i}{c}")
                output(f"nsa{i}c")
                free(add(late[:, :, P:T], bank(f"nsa{i}c")[:, 0:256].rearrange("p (r k) -> p r k", r=2), both(bias[:, h, P:T])), f"nsa{i}c")
                for c in "abc":
                    taken(f"nsa{i}{c}")
                v.tensor_reduce(out=st[:, 0, 0:2], in_=early, axis=AX.X, op=ALU.max, negate=True)
                v.tensor_reduce(out=st[:, 0, 4:6], in_=w[:, 768:800].rearrange("p (t k) -> p t k", t=2)[:, :, 0:N_CMP],
                                axis=AX.X, op=ALU.max, negate=True)
                v.tensor_reduce(out=st[:, 0, 2:4], in_=late, axis=AX.X, op=ALU.max, negate=True).then_inc(logits_ready, 1)

            def scale_weights(i, n, parts, gate=None):
                dve.wait_ge(weights_raw, i + 1)
                st = stats[:, i % 2, :, :]
                step(v.tensor_scalar(st[:, 2, 0:n], st[:, 1, 0:n], 1e-30, None, ALU.max))
                step(v.reciprocal(st[:, 3 if gate is None else 2, 0:n], st[:, 2, 0:n]))
                if gate is not None:
                    step(v.tensor_tensor(st[:, 3, 0:n], st[:, 2, 0:n], gate, ALU.mult))
                for k, p in enumerate(parts):
                    ins = v.tensor_scalar(p, p, st[:, 3, k:k + 1], None, ALU.mult)
                ins.then_inc(weights_ready, 1)

            def nsa_scale(i):
                w = logit[:, i % 2, :]
                scale_weights(i, 6, [w[:, 0:128], w[:, 128:256], w[:, 256:512], w[:, 512:768], w[:, 768:768 + N_CMP],
                                     w[:, 784:784 + N_CMP]], gate_t[:, i // 2 + 4 * (i % 2), :])

            dve.wait_ge(gate_t_ready, TT)
            dve.wait_ge(loaded["bias"], 16 * 24)
            nsa_logits(0)
            nsa_scale(0)
            for i in range(8):
                if i < 7:
                    nsa_logits(i + 1)
                if i and i % 2 == 0:
                    split_output(attn_a[:, i // 2 - 1, :], attn_a_lo1[:, i // 2 - 1, :], f"nsao{i // 2 - 1}")
                output(f"nsat{i}w")
                free(v.tensor_copy(turned[:, i % 2, 1, 0:384], bank(f"nsat{i}w")[:, 0:384]), f"nsat{i}w")
                if i < 7:
                    nsa_scale(i + 1)
            split_output(attn_a[:, 3, :], attn_a_lo1[:, 3, :], "nsao3")

            def rest_of_merged(n, m, lo):
                dve.wait_ge(merged_rounded, n + 1)
                v.tensor_tensor(R(lo[:, m, :]), lo[:, m, :], R(merged[:, m, :]), ALU.subtract).then_inc(merged_ready, 1)

            def rest_of_hidden(n, i):
                dve.wait_ge(hidden_rounded, n + 1)
                v.tensor_tensor(R(hidden_lo[:, i, :]), hidden_lo[:, i, :], R(hidden[:, i, :]), ALU.subtract).then_inc(hidden_ready, 1)

            for m in range(KD):
                dve.wait_ge(tanh_ready, m // 2 + 1)
                taken(f"mb{m}")
                for n, g, dst in ((f"up_nsa{m}", m, merged_lo1[:, m, :]), (f"up_sb{m}", 8 + m, part[:, m % 2, :])):
                    output(n)
                    free(v.scalar_tensor_tensor(out=dst, in0=gates[:, g, :], scalar=1.0, in1=bank(n)[:, 0:T],
                                                op0=ALU.add, op1=ALU.mult), n)
                taken(f"up_nsa{m}")
                taken(f"up_sb{m}")
                v.tensor_tensor(merged_lo1[:, m, :], merged_lo1[:, m, :], part[:, m % 2, :], ALU.add).then_inc(merged_raw, 1)
                if m:
                    rest_of_merged(m - 1, m - 1, merged_lo1)
                dve.wait_ge(merged_raw, m + 1)
            rest_of_merged(KD - 1, KD - 1, merged_lo1)

            def add_residual(name, m, gate):
                output(name)
                free(v.scalar_tensor_tensor(out=x[:, m, :], in0=bank(name)[:, 0:T], scalar=gate, in1=x[:, m, :],
                                            op0=ALU.mult, op1=ALU.add), name)

            dve.wait_ge(mod_ready, 6)
            for m in range(KD):
                add_residual(f"mix{m}", m, mod[:, 16 + m:17 + m])

            for i in range(KD):
                taken(f"mix{i}")
            norm_row(u, u_lo, x, "norm2_g", ROW_1, 3)

            def rope_steps():
                dve.wait_ge(loaded["pos"], 16)
                step(v.tensor_copy(pos[:, :], pos_i[:, :]))
                yield
                for r in range(4):
                    step(v.tensor_scalar(rope[:, r, :], pos[:, :], col("angle", r), None, ALU.mult))
                    yield
                step(v.tensor_scalar(rope_n, rope[:, :, :], 1.0 / TWO_PI, BIG, ALU.mult, ALU.add))
                yield
                step(v.tensor_scalar(rope_n, rope_n, -BIG, None, ALU.add))
                yield
                for c in (PI_1, PI_2, PI_3):
                    step(v.scalar_tensor_tensor(out=rope[:, :, :], in0=rope_n, scalar=-c, in1=rope[:, :, :], op0=ALU.mult, op1=ALU.add))
                    yield
                for r in range(4):
                    step(v.tensor_scalar(rope[:, r, :], rope[:, r, :], col("phase", r), None, ALU.add))
                    yield
                step(v.tensor_scalar(rope_n, rope[:, :, :], PI_LIMIT, -TWO_PI, ALU.is_gt, ALU.mult))
                yield
                step(v.tensor_tensor(rope[:, :, :], rope[:, :, :], rope_n, ALU.add))
                yield
                v.tensor_scalar(rope[:, :, :], rope[:, :, :], PI_LIMIT, -PI_LIMIT, ALU.min, ALU.max).then_inc(rope_angle_ready, 1)
                yield

            steps = rope_steps()
            for m in range(KF):
                taken(f"w1_{m}")
                v.tensor_tensor(hidden_lo[:, m, :], part[:, m % 2, :], part[:, m % 2, :], ALU.mult).then_inc(hidden_raw, 1)
                if m:
                    rest_of_hidden(m - 1, m - 1)
                next(steps, None)
            rest_of_hidden(KF - 1, KF - 1)
            for m in range(KD):
                add_residual(f"w2_{m}", m, mod[:, 40 + m:41 + m])
            for i in range(KD):
                taken(f"w2_{i}")

            def swiglu(p, before):
                for m in range(KF2):
                    taken(f"{p}g{m}")
                    output(f"{p}u{m}")
                    free(v.tensor_tensor(hidden_lo[:, m, :], part[:, m % 2, :], bank(f"{p}u{m}")[:, 0:T], ALU.mult), f"{p}u{m}")
                    if m:
                        rest_of_hidden(before + m - 1, m - 1)
                rest_of_hidden(before + KF2 - 1, KF2 - 1)
                for m in range(KD):
                    add_residual(f"{p}d{m}", m, 0.5)
                for m in range(KD):
                    taken(f"{p}d{m}")

            norm_row(u, u_lo, x, "ffn1_norm_2", ROW_2)
            swiglu("f1", KF)

            norm_row(u, u_lo, x, "mix_norm_2", ROW_3)
            for first, n, last in ((0, 3, "cq2"), (3, 2, "ckv1")):
                taken(last)
                r = take_rinv()
                for i in range(first, first + n):
                    z, lo = latent[:, i, :], latent_lo[:, i, :]
                    step(v.tensor_tensor(lo, z, r, ALU.mult))
                    step(v.tensor_tensor(R(z), z, r, ALU.mult))
                    v.tensor_tensor(R(lo), lo, R(z), ALU.subtract).then_inc(latent_ready, 1)
            for b in range(3):
                normalise(f"qm{b}", [qa[:, b, :]], "mem_q_norm_2")
            dve.wait_ge(rope_ready, 1)
            output("kr_rot")
            taken("kr")
            step(v.tensor_tensor(kr[:, 1, :], kr[:, 0, :], rope[:, ROPE_C, :], ALU.mult))
            free(v.tensor_tensor(part[:, 0, :], bank("kr_rot")[:, 0:T], rope[:, ROPE_S, :], ALU.mult), "kr_rot")
            taken("kr_rot")
            v.tensor_tensor(kr[:, 1, :], kr[:, 1, :], part[:, 0, :], ALU.add).then_inc(k_pe_ready, 1)
            dve.wait_ge(k_pe_ready, 1)

            def mla_q_gain(h):
                dve.wait_ge(squares_ready, 19 + h + 1)
                odd = h % 2
                if h >= 2:
                    dve.wait_ge(normed, h - 1)
                free(v.scalar_tensor_tensor(out=part[:, h % 2, :], in0=bank(f"uq{h}")[:, 0:T],
                                            scalar=col("mla_q_odd" if odd else "mla_q_even"), in1=rope[:, ROPE_QO if odd else ROPE_QE, :],
                                            op0=ALU.mult, op1=ALU.mult), f"uq{h}")

            def mla_q_norm(h):
                taken(f"uq{h}")
                r = take_rinv()
                v.tensor_tensor(pair_q[:, h, :], part[:, h % 2, :], r, ALU.mult).then_inc(normed, 1)

            mla_q_gain(0)
            normalise("qm3", [qa[:, 3, :]], "mem_q_norm_2")
            for h in range(8):
                if h < 7:
                    mla_q_gain(h + 1)
                mla_q_norm(h)
            for h in range(8):
                name, (own, pe_rows) = f"uk{h // 2}", ((LO, HI), (HI, LO))[h % 2]
                ahead(name)
                r = take_rinv()
                ins = v.scalar_tensor_tensor(out=pair_k[own, h, :], in0=bank(name)[own, 0:T], scalar=col("mla_k_nope", 0, own),
                                             in1=r[own, :], op0=ALU.mult, op1=ALU.mult)
                if h % 2:
                    free(ins, name)
                v.tensor_tensor(pair_k[pe_rows, h, :], kr[pe_rows, 1, :], r[pe_rows, :], ALU.mult).then_inc(normed, 1)

            for t in range(TT):
                taken(f"sv{t}")
                step(v.bn_stats(sg_stat[:, t, 0:6], sg_v[:, t, :]))
                ins = v.bn_aggr(sg_stat[:, t, 6:8], sg_stat[:, t, 0:6])
            ins.then_inc(sg_var_ready, 1)
            ahead("su3")
            dve.wait_ge(sg_dev_ready, 1)
            dve.wait_ge(loaded["sg"], 48)
            for t in range(TT):
                s = sg_v[:, t, :]
                step(v.tensor_scalar(s, s, sg_stat[:, t, 6:7], sg_stat[:, t, 9:10], ALU.subtract, ALU.mult))
                step(v.tensor_tensor(s, s, sg_ln[:, 0, :], ALU.mult))
                v.tensor_tensor(s, s, sg_ln[:, 1, :], ALU.add).then_inc(sg_ln_ready, 1)

            def logits(i):
                w, st = logit[:, i % 2, :], stats[:, i % 2, :, :]
                if i >= 2:
                    output(f"mlat{i - 2}" if i < 10 else f"memt{i - 10}")
                if i < 8:
                    name = f"mla{i}"
                    output(name)
                    ps = bank(name)
                    scale = 96 ** -0.5
                    v.scalar_tensor_tensor(out=w[:, 0:P], in0=ps[:, 0:P], scalar=scale, in1=mat("not_after"), op0=ALU.mult, op1=ALU.add)
                    v.tensor_scalar(w[:, P:T], ps[:, P:T], scale, None, ALU.mult)
                    free(v.scalar_tensor_tensor(out=w[:, T:384], in0=ps[:, T:384], scalar=scale, in1=mat("not_after"),
                                                op0=ALU.mult, op1=ALU.add), name)
                    taken(name)
                    v.tensor_reduce(out=st[:, 0, 0:1], in_=w[:, 0:P], axis=AX.X, op=ALU.max, negate=True)
                    v.tensor_reduce(out=st[:, 0, 1:2], in_=w[:, P:384], axis=AX.X, op=ALU.max, negate=True).then_inc(logits_ready, 1)
                else:
                    name = f"mem{i - 8}"
                    output(name)
                    step(v.tensor_reduce(out=st[:, 0, 2:4], in_=bank(name)[:, :].rearrange("p (t k) -> p t k", t=2),
                                         axis=AX.X, op=ALU.max, negate=True))
                    v.tensor_scalar(st[:, 0, 0:2], st[:, 0, 2:4], P ** -0.5, None, ALU.mult).then_inc(logits_ready, 1)

            def attend_scale(i):
                w = logit[:, i % 2, :]
                scale_weights(8 + i, 2, [w[:, 0:P], w[:, P:384]] if i < 8 else [w[:, 0:T], w[:, T:2 * T]])

            logits(0)
            attend_scale(0)
            for i in range(12):
                if i < 11:
                    logits(i + 1)
                if i and i % 2 == 0 and i <= 8:
                    split_output(attn_b[:, i // 2 - 1, :], attn_b_lo2[:, i // 2 - 1, :], f"mlao{i // 2 - 1}")
                if i >= 9:
                    split_output(attn_c[:, i - 9, :], attn_c_lo2[:, i - 9, :], f"memo{i - 9}")
                if i < 11:
                    attend_scale(i + 1)
            for b in range(4):
                taken(f"su{b}")
                for c in range(TT):
                    name = f"sg{b}{c}"
                    output(name)
                    for s, rr in enumerate((LO, HI)):
                        dst = attn_a[rr, b, c * P:(c + 1) * P]
                        ins = v.tensor_tensor(attn_a_lo2[rr, b, c * P:(c + 1) * P], dst, bank(name)[rr, s * P:(s + 1) * P], ALU.mult)
                    free(ins, name)
                    taken(name)
                step(v.tensor_copy(R(attn_a[:, b, :]), attn_a_lo2[:, b, :]))
                v.tensor_tensor(R(attn_a_lo2[:, b, :]), attn_a_lo2[:, b, :], R(attn_a[:, b, :]), ALU.subtract).then_inc(sg_ready, 1)
            split_output(attn_c[:, 3, :], attn_c_lo2[:, 3, :], "memo3")

            for m in range(KD):
                for k, c in enumerate("abc"):
                    taken(f"gate{8 * k + m}")
                    n = f"br_{c}{m}"
                    output(n)
                    dst = merged_lo2[:, m, :] if k == 0 else part[:, k - 1, :]
                    free(v.scalar_tensor_tensor(out=dst, in0=gates[:, 8 * k + m, :], scalar=1.0, in1=bank(n)[:, 0:T],
                                                op0=ALU.add, op1=ALU.mult), n)
                for c in "abc":
                    taken(f"br_{c}{m}")
                step(v.tensor_tensor(merged_lo2[:, m, :], merged_lo2[:, m, :], part[:, 0, :], ALU.add))
                v.tensor_tensor(merged_lo2[:, m, :], merged_lo2[:, m, :], part[:, 1, :], ALU.add).then_inc(merged_raw, 1)
                dve.wait_ge(merged_raw, KD + m + 1)
                if m:
                    rest_of_merged(KD + m - 1, m - 1, merged_lo2)
            rest_of_merged(2 * KD - 1, KD - 1, merged_lo2)
            for m in range(KD):
                add_residual(f"mix2_{m}", m, 0.5)
            for m in range(KD):
                taken(f"mix2_{m}")
            norm_row(u, u_lo, x, "ffn2_norm_2", ROW_4)
            swiglu("f2", KF + KF2)


def lay_out(a):
    a = {k: np.asarray(v) for k, v in a.items()}
    sq = {k: (v[0] if k not in ("x", "c", "rel_bias", "mem_2", "positions_2") else v) for k, v in a.items()}

    def block_diagonal(w):
        out = np.zeros(w.shape[:-2] + (P, P), w.dtype)
        out[..., 0:64, 0:64] = w
        out[..., 64:, 64:] = w
        return out

    src = dict(sq)
    for n in ("cmp_k_w1", "cmp_v_w1"):
        src[n] = block_diagonal(sq[n].reshape(32, HD, HD))
    chunks = stream_chunks()
    n_slots = -(-len(chunks) // SLOT)
    stream = np.zeros((n_slots, P, SLOT, P), np.float32)
    for i, (name, rows, cols) in enumerate(chunks):
        w = src[name]
        stream[i // SLOT, :, i % SLOT, :] = w[rows] if cols is None else w[np.ix_(rows, cols)]
    ada = sq["ada_w"].reshape(KD, P, 6, D).transpose(2, 0, 1, 3).reshape(48, P, D)
    mats, buckets, consts = shape_constants()
    q, k = sq["mla_q_norm_2"], sq["mla_k_norm_2"]
    pe = np.concatenate([q[64:96], q[80:96], q[64:80]])
    twice = lambda v: np.concatenate([v, v])
    vec = {n: sq[n] for n in ("norm1_g", "norm2_g", "ffn1_norm_2", "mix_norm_2", "ffn2_norm_2", "mem_norm_2", "ada_b",
                              "b_gate_2", "mla_cq_norm_2", "mla_ckv_norm_2", "mem_q_norm_2", "mem_k_norm_2")}
    vec["c"] = a["c"]
    vec["q_norm"] = twice(sq["q_norm_g"])
    for i, n in enumerate(("k_cmp_norm", "k_slc_norm", "k_win_norm")):
        vec[n] = twice(sq["k_norm_g"][i])
    vec["mla_q_even"] = np.concatenate([q[0:64], pe])
    vec["mla_q_odd"] = np.concatenate([pe, q[0:64]])
    vec["mla_k_nope"] = twice(k[0:64])
    vec["mla_k_rope"] = np.concatenate([k[64:96]] * 4)
    vec.update(consts)
    cols = np.concatenate([np.asarray(vec[n], np.float32).reshape(c, P) for n, c in VECTORS]).T

    def feature_major(v):
        return np.ascontiguousarray(v.reshape(T, KD, P).transpose(2, 1, 0))

    table = np.concatenate([a["rel_bias"], np.ones((1, 8), np.float32)])
    pos_rows = sq["cmp_pos"].T
    out = {
        "stream": stream.reshape(n_slots, P, SLOT * P), "ada": ada, "x_t": feature_major(a["x"]),
        "mem_t": feature_major(a["mem_2"]), "cols": cols, "mats": mats.transpose(1, 0, 2), "buckets": buckets,
        "table": table, "pos": np.broadcast_to(a["positions_2"], (P, T)),
        "cmp_w2": np.stack([block_diagonal(sq["cmp_k_w2"]), block_diagonal(sq["cmp_v_w2"])], 1),
        "cmp_pos": np.concatenate([pos_rows, pos_rows]),
        "sg_w": sq["sg_w_2"].transpose(2, 0, 1), "sg_b": sq["sg_b_2"].reshape(1, 8 * P),
        "sg_ln": np.broadcast_to(np.stack([sq["sg_ln_g_2"], sq["sg_ln_b_2"]])[None], (P, 2, 512)),
    }
    return {n: np.ascontiguousarray(v) for n, v in out.items()}


def kernel(**inputs):
    import concourse.bacc as bacc
    from concourse.bass_utils import run_bass_kernel_spmd

    arrays = lay_out(inputs)
    nc = bacc.Bacc("TRN2", target_bir_lowering=False, num_devices=1)
    args = [nc.dram_tensor(f"in_{n}", v.shape, mybir.dt.from_np(v.dtype), kind="ExternalInput").ap() for n, v in arrays.items()]
    out = nc.dram_tensor("out_t", (P, KD, T), F32, kind="ExternalOutput").ap()
    build(nc, *args, out)
    r = run_bass_kernel_spmd(nc, [{f"in_{n}": v for n, v in arrays.items()}], core_ids=[0])
    got = np.asarray(r.results[0]["out_t"])
    return np.ascontiguousarray(got.transpose(2, 1, 0)).reshape(1, T, D)
```

```python
from contextlib import ExitStack

import numpy as np

import concourse.bass as bass
from concourse import mybir

F32 = mybir.dt.float32
F32R = mybir.dt.float32r
I32 = mybir.dt.int32
ACT = mybir.ActivationFunctionType
ALU = mybir.AluOpType
AX = mybir.AxisListType

P = 128
T = 256
TT = T // P
D = 1024
KD = D // P
HD = 64
DFF, DFF2 = 4096, 2816
KF, KF2 = DFF // P, DFF2 // P
NEG = -1e30
EPS = 1e-6
N_CMP = 15
CMP_STRIDE = 16
SLOT = 8
SQ = 3
RING = 6
HALVES = 4
ADA_RING = 3
ADA_EARLY = 16
BIG = 12582912.0
TWO_PI = 6.283185307179586
PI_1 = 6.28125
PI_2 = 0.0019350051879882812
PI_3 = float(np.float32(TWO_PI - PI_1 - PI_2))
PI_LIMIT = 3.1415925

C_QA, C_KC, C_VC, C_KS, C_VS, C_KW, C_VW, C_GA, C_QB, C_KB, C_VB, C_MA, C_MB = (
    0, 512, 640, 768, 896, 1024, 1152, 1280, 1304, 1816, 2328, 2840, 3864)
D_U, D_V, D_CQ, D_CKV, D_KR, D_QM, D_GATE = 0, 512, 1024, 1408, 1664, 1696, 2208


def span(first, n=P):
    return list(range(first, first + n))


def rot(cols):
    half = len(cols) // 2
    return cols[half:] + cols[:half]


def mla_q_cols(h):
    nope, rope = span(h * 96, 64), span(h * 96 + 64, 32)
    pe = rope + rot(rope)
    return nope + pe if h % 2 == 0 else pe + nope


def stream_chunks():
    out = []

    def stationary(name, cols, rows):
        for r in rows:
            out.append((name, r, cols))

    def moving(name, first, n, k):
        for kk in range(k):
            for j in range(n // P):
                out.append((name, span(kk * P), span(first + j * P)))

    full = [span(k * P) for k in range(KD)]
    half = [span(k * P) for k in range(4)]
    for b in range(4):
        stationary("mem_w_kv_2", span(b * P), full)
    moving("mem_w_kv_2", 512, 512, KD)
    for k in range(KD):
        out.append(("w_in", span(k * P), span(C_VS)))
        out.append(("w_in", span(k * P), span(C_VW)))
    moving("w_in", C_VB, 512, KD)
    stationary("w_in", span(C_GA), full)
    for c in (C_KC, C_VC, C_KS, C_KW):
        stationary("w_in", span(c), full)
    for b in range(4):
        stationary("w_in", span(b * HD, HD) + span((4 + b) * HD, HD), full)
    for c in (C_KB, C_QB):
        for b in range(4):
            stationary("w_in", span(c + b * P), full)
    for name in ("cmp_k_w1", "cmp_v_w1"):
        for j in range(32):
            out.append((name, j, None))
    for c in (C_MA, C_MB):
        for b in range(KD):
            stationary("w_in", span(c + b * P), full)
    for m in range(KD):
        stationary("w_up_nsa", span(m * P), [span(b * HD, HD) + span((4 + b) * HD, HD) for b in range(4)])
        stationary("w_up_sb", span(m * P), half)
    for m in range(KD):
        stationary("w_out", span(m * P), full)
    for m in range(KF):
        stationary("mlp_w1", span(m * P), full)
    for m in range(KD):
        stationary("mlp_w2", span(m * P), [span(k * P) for k in range(KF)])

    def swiglu(gu, down):
        for m in range(KF2):
            stationary(gu, span(m * P), full)
            stationary(gu, span(DFF2 + m * P), full)
        for m in range(KD):
            stationary(down, span(m * P), [span(k * P) for k in range(KF2)])

    swiglu("ffn1_w_gu_2", "ffn1_w_down_2")
    for b in range(3):
        stationary("w_in_2", span(D_CQ + b * P), full)
    for b in range(2):
        stationary("w_in_2", span(D_CKV + b * P), full)
    stationary("w_in_2", 4 * span(D_KR, 32), full)
    for b in range(4):
        stationary("w_in_2", span(D_QM + b * P), full)
    for h in range(8):
        stationary("mla_w_uq_2", mla_q_cols(h), [span(k * P) for k in range(3)])
    for b in range(4):
        stationary("mla_w_ukv_2", span(2 * b * P, HD) + span((2 * b + 1) * P, HD), [span(0), span(P)])
    for k in range(2):
        for j in range(4):
            out.append(("mla_w_ukv_2", span(k * P), span(2 * j * P + HD, HD) + span((2 * j + 1) * P + HD, HD)))
    moving("w_in_2", D_V, 512, KD)
    for b in range(4):
        stationary("w_in_2", span(D_U + b * P), full)
    for b in range(24):
        stationary("w_in_2", span(D_GATE + b * P), full)
    for m in range(KD):
        for name in ("w_branch_a_2", "w_branch_b_2", "w_branch_c_2"):
            stationary(name, span(m * P), half)
    for m in range(KD):
        stationary("w_out_2", span(m * P), full)
    swiglu("ffn2_w_gu_2", "ffn2_w_down_2")
    return out


VECTORS = [("norm1_g", 8), ("norm2_g", 8), ("ffn1_norm_2", 8), ("mix_norm_2", 8), ("ffn2_norm_2", 8),
           ("mem_norm_2", 8), ("c", 8), ("ada_b", 48), ("b_gate_2", 24), ("mla_cq_norm_2", 3),
           ("mla_ckv_norm_2", 2), ("q_norm", 1), ("k_cmp_norm", 1), ("k_slc_norm", 1), ("k_win_norm", 1),
           ("mla_q_even", 1), ("mla_q_odd", 1), ("mla_k_nope", 1), ("mla_k_rope", 1), ("mem_q_norm_2", 1),
           ("mem_k_norm_2", 1), ("angle", 4), ("phase", 4), ("sees_a_block", 2), ("eps", 1)]
AT = {}
_n = 0
for _name, _k in VECTORS:
    AT[_name] = _n
    _n += _k
N_COLS = _n
ROPE_QE, ROPE_QO, ROPE_C, ROPE_S = range(4)

MATRICES = ["ones", "ident", "halves", "q_even", "q_odd", "rotate", "neg_suffix",
            "neg_ones", "before", "not_before", "not_after", "spread"]
MAT = {n: i for i, n in enumerate(MATRICES)}


def shape_constants():
    i = np.arange(P)
    k, q = i[:, None], i[None, :]
    m = np.zeros((len(MATRICES), P, P), np.float32)
    m[MAT["ident"]] = np.eye(P)
    m[MAT["ones"]] = 1
    m[MAT["halves"]] = (k // 64) == (q // 64)
    m[MAT["q_even"]] = (k < 96) + 0 * q
    m[MAT["q_odd"]] = ((k < 32) | (k >= 64)) + 0 * q
    m[MAT["rotate"]] = (k // 32 == q // 32) & ((k % 32) == (q % 32 + 16) % 32)
    m[MAT["neg_suffix"]] = -1.0 * (k >= q)
    m[MAT["neg_ones"]] = -1
    m[MAT["before"]] = k < q
    m[MAT["not_before"]] = np.where(k < q, 0, NEG)
    m[MAT["not_after"]] = np.where(q <= k, 0, NEG)
    m[MAT["spread"]] = ((k == q) | (k == N_CMP + 1)) & (q < N_CMP)
    dist = 255 - np.arange(512)
    n = np.maximum(dist, 0)
    nf = np.maximum(n, 1).astype(np.float32)
    large = 16 + (np.log(nf / np.float32(16)) / np.float32(np.log(128 / 16)) * 16).astype(np.int32)
    bucket = np.where(n < 16, n, np.minimum(large, 31))
    buckets = np.zeros((33, 512), np.float32)
    buckets[bucket, np.arange(512)] = dist >= 0
    buckets[32] = np.where(dist >= 0, 0, NEG)
    inv = (np.float32(10000.0) ** (-np.arange(16, dtype=np.float32) / np.float32(16))).astype(np.float32)
    pair = inv[i % 16]
    sign = np.where(i % 32 < 16, -1, 1)
    angle, phase = np.zeros((4, P)), np.zeros((4, P))
    half_pi = np.pi / 2
    angle[ROPE_QE] = np.where(i < 64, 0, np.where(i < 96, pair, sign * pair))
    phase[ROPE_QE] = np.where(i < 96, half_pi, 0)
    angle[ROPE_QO] = np.where(i >= 64, 0, np.where(i < 32, pair, sign * pair))
    phase[ROPE_QO] = np.where((i >= 64) | (i < 32), half_pi, 0)
    angle[ROPE_C], phase[ROPE_C] = pair, half_pi
    angle[ROPE_S] = sign * pair
    sees = np.stack([i >= CMP_STRIDE * 2 - 1, i >= 0])
    return m, buckets, {"angle": angle, "phase": phase, "sees_a_block": sees, "eps": np.full((1, P), EPS)}


def plan_psum(proj, attn, long):
    where, used = {}, [0] * 8
    for names, banks in ((proj, [0, 1, 2]), (attn, [3, 4, 5, 6]), (long, [7])):
        for n, name in enumerate(names):
            b = banks[n % len(banks)]
            assert name not in where, name
            where[name] = (b, used[b])
            used[b] += 1
    return where


def proj_names():
    out = ["mem_ss", "mem_k0", "mem_k1", "x_ss", "mem_k2", "mem_k3", "bias"]
    out += ["ada0a", "ada0b", "ada1a", "ada1b", "mem_v0", "mem_v1"]
    out += ["vsw0", "vsw1", "vsb0", "vsb1", "ga", "kc", "vc", "ks", "kw"]
    out += [f"qa{b}" for b in range(4)] + [f"kb{b}" for b in range(4)] + [f"qb{b}" for b in range(4)]
    out += ["ada2a", "ada2b", "cmp_hid_k", "cmp_hid_v", "ada3a", "ada3b", "ma0", "cmp_turn_k", "cmp_turn_v"]
    out += ["ga_turn", "ma1", "cmp_out_k", "cmp_out_v", "ma2", "ma3", "ma4", "ma5", "ada4a", "ada4b", "ma6", "ma7"]
    out += ["mb0", "ada5a", "ada5b"] + [f"mb{b}" for b in range(1, 8)]
    for m in range(KD):
        out += [f"up_nsa{m}", f"up_sb{m}"]
    out += [f"mix{m}" for m in range(KD)]
    out += [f"w1_{m}" for m in range(KF)] + [f"w2_{m}" for m in range(KD)]

    def swiglu(p):
        return [f"{p}{w}{m}" for m in range(KF2) for w in "gu"] + [f"{p}d{m}" for m in range(KD)]

    out += swiglu("f1")
    out += [f"cq{b}" for b in range(3)] + [f"ckv{b}" for b in range(2)] + ["kr"] + [f"qm{b}" for b in range(4)]
    out += ["kr_rot"]
    out += [f"uq{h}" for h in range(8)] + [f"uk{b}" for b in range(4)] + ["uv0", "uv1", "sv0", "sv1"]
    out += [f"su{b}" for b in range(4)]
    out += [f"gate{b}" for b in range(24)]
    for m in range(KD):
        out += [f"br_a{m}", f"br_b{m}", f"br_c{m}"]
    out += [f"mix2_{m}" for m in range(KD)]
    out += swiglu("f2")
    return out


def attn_names():
    out = [f"ss_mem_k{b}" for b in range(4)]
    out += [f"ss_{n}" for n in ("ks", "kw", "qa0", "qa1", "qa2", "qa3")]
    out += ["sbz0", "sbz1", "sbz2", "ss_cmp"] + [f"sbz{h}" for h in range(3, 8)]
    out += [f"nsa{i}{c}" for i in (0, 1) for c in "abc"]
    for i in range(8):
        out += [f"nsat{i}{c}" for c in "swc"]
        if i < 6:
            out += [f"nsa{i + 2}{c}" for c in "abc"]
    out += ["ss_cq", "ss_ckv"] + [f"ss_qm{b}" for b in range(4)]
    out += [f"ss_uq{h}" for h in range(8)] + [f"ss_uk{h}" for h in range(8)]
    out += ["mla0"]
    for h in range(8):
        out += [f"mla{h + 1}" if h < 7 else "mem0", f"mlat{h}"]
    for h in range(4):
        out += [f"mem{h + 1}"] * (h < 3) + [f"memt{h}"]
    out += [f"sg{b}{c}" for b in range(4) for c in range(TT)]
    return out


def long_names():
    out = [f"sbo{b}" for b in range(4)] + [f"nsao{b}" for b in range(4)] + ["x1_ss", "x2_ss", "x3_ss"]
    out += [f"mlao{b}" for b in range(4)] + [f"memo{b}" for b in range(4)] + ["x4_ss"]
    return out


ROW_MEM, ROW_X, ROW_1, ROW_2, ROW_3, ROW_4 = range(6)


def build(nc, stream, ada, x_t, mem_t, cols_d, mats_d, buckets_d, table_d, pos_d, cmp_w2_d,
          cmp_pos_d, sg_w_d, sg_b_d, sg_ln_d, out_t):
    n_slots = stream.shape[0]
    where = plan_psum(proj_names(), attn_names(), long_names())

    with ExitStack() as ctx:
        def sb(name, shape, dt=F32):
            return ctx.enter_context(nc.sbuf_tensor(name, shape, dt))

        def sem(name):
            return ctx.enter_context(nc.semaphore(name))

        psum = [ctx.enter_context(nc.psum_tensor(f"bank{b}", [P, 512], F32)) for b in range(8)]

        rounded_view = {}

        def sb_split(name, shape):
            first = -(-nc.sbuf_base // 32) * 32
            t = sb(name, shape)
            rounded_view[t.name] = nc.alloc_sbuf_tensor_at(name + "_rounded", shape, F32R, offset=first)
            return t

        def R(ap):
            return bass.AP(rounded_view[ap.tensor.name], ap.offset, ap.ap)

        def flat(t):
            return t.rearrange("p a b -> p (a b)")

        def flat4(t):
            return t.rearrange("p a b c d -> p (a b c d)")

        ring = sb_split("ring", [P, RING * SLOT * P])
        rounded = sb_split("rounded", [P, HALVES * SLOT * P])
        ada_ring = sb("ada_ring", [P, ADA_RING, D])
        ada_acc = sb_split("ada_acc", [P, 2, D])
        mod = sb("mod", [P, 48])
        mats = sb("mats", [P, len(MATRICES), P])
        cols = sb("cols", [P, N_COLS])
        half_bias = sb("half_bias", [P, 24])
        c_act = sb("c_act", [P, 2, 8])
        x = sb("x", [P, KD, T])
        u = sb_split("u", [P, KD, T])
        u_lo = sb_split("u_lo", [P, KD, T])
        shared = sb_split("shared", [P, 32, T])
        hidden_lo = shared
        pair_k = shared[:, 0:8, :]
        pair_q = shared[:, 8:16, :]
        bias = shared[:, 16:24, :]
        attn_a, attn_b = shared[:, 24:28, :], shared[:, 28:32, :]
        attn_c = bias[:, 0:4, :]
        k_squares = bias[:, 4:8, :]
        mem_n_lo = pair_q
        attn_a_lo1, attn_b_lo1 = pair_k[:, 0:4, :], pair_q[:, 4:8, :]
        attn_a_lo2, attn_c_lo2 = pair_q[:, 0:4, :], bias[:, 4:8, :]
        cmp_sb = attn_a[0:32, 0, :].rearrange("p (w c) -> p w c", w=2)
        cmp_w2 = attn_a[:, 1, :].rearrange("p (w c) -> p w c", w=2)
        wide = sb_split("wide", [P, 32, T])
        gates, merged, hidden = wide[:, 0:24, :], wide[:, 24:32, :], wide
        merged_lo1, merged_lo2 = wide[:, 16:24, :], pair_k
        mem_n = wide[:, 0:8, :]
        bias_steps = wide[0:8, 8:23, :].rearrange("h a b -> h (a b)").rearrange("h (t c) -> h t c", c=N_CMP)
        squares = sb("squares", [P, SQ, T])
        log_ms = sb("log_ms", [P, T])
        rinv = sb("rinv", [P, 2, T])
        row_rinv = sb("row_rinv", [P, T])
        part = sb("part", [P, 2, T])
        mem_k = sb("mem_k", [P, 4, T])
        mem_v = sb("mem_v", [P, TT, 512])
        qa = sb("qa", [P, 4, T])
        kcat = sb_split("kcat", [P, 2, 528])
        attn_b_lo2 = flat(kcat[:, :, :])[:, 0:1024].rearrange("p (b t) -> p b t", t=T)
        vcat = sb("vcat", [P, TT, 2, 2, P])
        cmp_tanh = sb("cmp_tanh", [P, 2, 16])
        cmp_turned = sb("cmp_turned", [P, 2, 16])
        cmp_k = sb("cmp_k", [P, 4, 16])
        pair_v = sb("pair_v", [P, TT, 8, P])
        bias_cmp = sb("bias_cmp", [P, 8, TT, N_CMP])
        lines = sb("lines", [33, 1024])
        buckets, bias_line, sg_b = lines[:, 0:512], lines[0:8, 512:1024], lines[0:1, :]
        vcmp = lines[0:16, 0:256].rearrange("p (s c) -> p s c", s=2)
        table = sb("table", [33, 8])
        gate_tanh = sb("gate_tanh", [P, TT, 24])
        gate_t = sb("gate_t", [P, 8, 6])
        sbw = flat(wide[:, 16:28, :]).rearrange("p (a b c) -> p a b c", a=2, b=4)
        logit = flat(wide[:, 24:32, :]).rearrange("p (a b) -> p a b", a=2)
        ada_flat = flat(ada_acc[:, :, :])
        latent_lo = wide[:, 24:29, :]
        latent = ada_flat[:, 0:1280].rearrange("p (b t) -> p b t", t=T)
        kr = ada_flat[:, 1280:1792].rearrange("p (b t) -> p b t", t=T)
        pos = ada_flat[:, 1792:2048]
        sg_v = flat4(vcat[:, :, :, :, :])[:, 0:1024].rearrange("p (t c) -> p t c", t=TT)
        stats = sb("stats", [P, 2, 4, 6])
        turned = sb("turned", [P, 2, 2, 512])
        turned_c = turned[0:16, :, :, 384:512]
        kc_ext = flat(turned[:, 0, :, :])[:, 0:576].rearrange("p (w t) -> p w t", w=2)
        gate_raw = turned[0:24, 1, 0, 0:T]
        row_squares = turned[:, :, :, :].rearrange("p a b c -> p (a b c)").rearrange("p (k t) -> p k t", t=T)
        pos_i = sb("pos_i", [P, T], I32)
        rope_n = row_squares[:, 0:4, :]
        rope = ada_ring[:, 0, :].rearrange("p (b t) -> p b t", t=T)
        sg_w = ada_ring[:, 1, :].rearrange("p (g t) -> p g t", t=P)
        sg_ln = ada_ring[:, 2, :].rearrange("p (w f) -> p w f", w=2)
        ada_early = [ada_ring[:, 0, :], ada_ring[:, 1, :], ada_ring[:, 2, :], flat(bias[:, 0:4, :]), flat(bias[:, 4:8, :]),
                     flat(attn_b), flat(u[:, 0:4, :]), flat(u[:, 4:8, :])]
        sg_stat = sb("sg_stat", [P, TT, 12])

        slot_full = [sem(f"slot_full{i}") for i in range(RING)]
        slot_used, slot_rounded, slot_split = sem("slot_used"), sem("slot_rounded"), sem("slot_split")
        slot_split_by_pool = sem("slot_split_by_pool")
        ada_full = [sem(f"ada_full{i}") for i in range(ADA_RING)]
        ada_early_full = [sem(f"ada_early_full{i}") for i in range(len(ada_early))]
        ada_used = sem("ada_used")
        bank_full = [sem(f"bank_full{b}") for b in range(8)]
        bank_free = [sem(f"bank_free{b}") for b in range(8)]
        loaded = {n: sem(f"loaded_{n}") for n in ("x", "mem", "mem_end", "cols", "mats", "bias_in", "small", "pos", "sg", "bias")}
        stored = sem("stored")
        c_tanh_ready = sem("c_tanh_ready")
        zeros_ready, lines_ready, sg_w_ready = sem("zeros_ready"), sem("lines_ready"), sem("sg_w_ready")
        squares_ready, k_squares_ready = sem("squares_ready"), sem("k_squares_ready")
        row_squares_ready, row_rinv_ready = sem("row_squares_ready"), sem("row_rinv_ready")
        row_gathering, row_gathered = sem("row_gathering"), sem("row_gathered")
        rinv_ready, normed = sem("rinv_ready"), sem("normed")
        u_normed, u_rounded, u_ready = sem("u_normed"), sem("u_rounded"), sem("u_ready")
        ada_summed, mod_ready, half_bias_ready = sem("ada_summed"), sem("mod_ready"), sem("half_bias_ready")
        gate_t_ready, tanh_ready = sem("gate_t_ready"), sem("tanh_ready")
        cmp_tanh_ready, cmp_rinv_ready, cmp_k_ready = sem("cmp_tanh_ready"), sem("cmp_rinv_ready"), sem("cmp_k_ready")
        sb_log_ready, softplus_ready, sb_logits_ready = sem("sb_log_ready"), sem("softplus_ready"), sem("sb_logits_ready")
        logits_ready, weights_raw, weights_ready = sem("logits_ready"), sem("weights_raw"), sem("weights_ready")
        merged_raw, merged_rounded, merged_ready = sem("merged_raw"), sem("merged_rounded"), sem("merged_ready")
        silu_ready = sem("silu_ready")
        hidden_raw, hidden_rounded, hidden_ready = sem("hidden_raw"), sem("hidden_rounded"), sem("hidden_ready")
        latent_ready, k_pe_ready = sem("latent_ready"), sem("k_pe_ready")
        rope_angle_ready, rope_ready = sem("rope_angle_ready"), sem("rope_ready")
        sg_var_ready, sg_dev_ready, sg_ln_ready = sem("sg_var_ready"), sem("sg_dev_ready"), sem("sg_ln_ready")
        sg_ready = sem("sg_ready")
        ones_ready = sem("ones_ready")
        act_step, dve_step = sem("act_step"), sem("dve_step")

        def full(eng, name):
            b, k = where[name]
            eng.wait_ge(bank_full[b], k + 1)

        def evacuated(eng, name):
            b, k = where[name]
            eng.wait_ge(bank_free[b], k + 1)

        first_plain = [c[0] for c in stream_chunks()].index("cmp_k_w1") // SLOT
        split_slots = [n for n in range(n_slots) if not first_plain <= n < first_plain + 64 // SLOT]
        nth_split = {n: q for q, n in enumerate(split_slots)}
        first_of_pool = nth_split[next(i for i, c in enumerate(stream_chunks()) if c[0] == "w_in" and c[2] == span(C_MB)) // SLOT]

        def by_pool(q):
            return q % 2 == 1 and (q < 8 or q >= first_of_pool)

        def splits_before(q, pool):
            return sum(by_pool(i) == pool for i in range(q))

        slot_at = {}

        def slot_weights(n):
            return ring[:, n % RING * SLOT * P:(n % RING + 1) * SLOT * P]

        def slot_round(q):
            return rounded[:, q % HALVES * SLOT * P:(q % HALVES + 1) * SLOT * P]

        def splitter(split):
            at = {"next": 0}

            def ahead(name, reach=HALVES):
                while at["next"] < len(split_slots) and split_slots[at["next"]] < slot_at[name] + reach:
                    split(at["next"], split_slots[at["next"]])
                    at["next"] += 1
            return ahead

        def bank(name):
            return psum[where[name][0]]

        def free(ins, name):
            ins.then_inc(bank_free[where[name][0]], 1)

        def mat(name):
            return mats[:, MAT[name], :]

        def col(name, i=0, rows=slice(0, P)):
            return cols[rows, AT[name] + i:AT[name] + i + 1]

        def chain(eng, s):
            n = [0]

            def step(ins):
                n[0] += 1
                ins.then_inc(s, 1)
                eng.wait_ge(s, n[0])
            return step

        LO, HI = slice(0, 64), slice(64, P)
        block = ctx.enter_context(nc.Block())

        @block.sync
        def _(sp):
            def load(r, i):
                sp.dma_start(ring[:, r * SLOT * P:(r + 1) * SLOT * P], stream[i]).then_inc(slot_full[r], 16)

            sp.dma_start(cols[:, :], cols_d).then_inc(loaded["cols"], 16)
            for half, name in ((slice(0, 4), "mem"), (slice(4, 8), "mem_end")):
                sp.dma_start(mem_n[:, half, :], mem_t[:, half, :]).then_inc(loaded[name], 16)
            for r in range(RING):
                load(r, r)
                if r == 0:
                    sp.dma_start(mats[:, 1:, :], mats_d[:, 1:, :]).then_inc(loaded["mats"], 16)
                if r == 1:
                    sp.dma_start(x[:, :, :], x_t).then_inc(loaded["x"], 16)
                if r == 3:
                    sp.dma_start(buckets, buckets_d).then_inc(loaded["bias_in"], 16)
                    sp.dma_start(table[:, :], table_d).then_inc(loaded["bias_in"], 16)
            sp.dma_start(cmp_w2, cmp_w2_d).then_inc(loaded["small"], 16)
            evacuated(sp, "mem_ss")
            for w in range(2):
                sp.dma_start(kc_ext[:, w, T:T + 32], cmp_pos_d).then_inc(loaded["small"], 16)
            sp.dma_start(pos_i[:, :], pos_d).then_inc(loaded["pos"], 16)
            rounds = n_slots // RING
            with sp.Fori(1, rounds) as i:
                for r in range(RING):
                    sp.wait_ge(slot_used, i * RING + (r + 1 - RING))
                    load(r, i * RING + r)
            for n in range(rounds * RING, n_slots):
                sp.wait_ge(slot_used, n + 1 - RING)
                load(n % RING, n)
            for m in range(KD):
                evacuated(sp, f"f2d{m}")
                sp.dma_start(out_t[:, m, :], x[:, m, :]).then_inc(stored, 16)
            sp.wait_ge(stored, 16 * KD)

        @block.tensor
        def _(pe):
            at = {"chunk": 0, "owed": 0, "squares": 0}

            def mm(out, lhs, rhs, start=False, stop=False):
                return nc.tensor.matmul(out, lhs, rhs, start=start, stop=stop, skip_group_check=True)

            def claim(name):
                b, k = where[name]
                if k:
                    pe.wait_ge(bank_free[b], k)
                return psum[b]

            def done(ins, name):
                ins.then_inc(bank_full[where[name][0]], 1)
                slot_at[name] = max(at["chunk"] - 1, 0) // SLOT

            def take_plain():
                c = at["chunk"]
                if c % SLOT == 0:
                    i = c // SLOT
                    pe.wait_ge(slot_full[i % RING], 16 * (i // RING + 1))
                at["chunk"] = c + 1
                c %= RING * SLOT
                return ring[:, c * P:(c + 1) * P]

            def take(n=1):
                c = at["chunk"]
                slot, first = c // SLOT, c % SLOT * P
                if first == 0:
                    q = nth_split[slot]
                    pe.wait_ge(slot_split_by_pool if by_pool(q) else slot_split, splits_before(q + 1, by_pool(q)))
                at["chunk"] = c + n
                return (R(slot_round(nth_split[slot])[:, first:first + n * P]),
                        R(slot_weights(slot)[:, first:first + n * P]))

            def give_back(ins, chunk):
                n = chunk // SLOT - at["owed"]
                if n > 0:
                    ins.then_inc(slot_used, n)
                    at["owed"] += n

            def project(name, k, rhs, ready=None):
                ps = claim(name)
                hi, lo = rhs
                for i in range(k):
                    chunk = at["chunk"]
                    w_hi, w_lo = take()
                    if ready:
                        ready(i)
                    give_back(mm(ps[:, 0:T], w_hi, R(hi[:, i, :]), i == 0), chunk)
                    mm(ps[:, 0:T], w_hi, R(lo[:, i, :]))
                    ins = mm(ps[:, 0:T], w_lo, R(hi[:, i, :]), stop=i == k - 1)
                done(ins, name)

            def project_first(name, rhs, row):
                ps = claim(name)
                hi, lo = rhs
                chunk = at["chunk"]
                w_hi, w_lo = take(KD)
                for i in range(KD):
                    c = slice(i * P, (i + 1) * P)
                    pe.wait_ge(u_rounded, row * KD + i + 1)
                    ins = mm(ps[:, 0:T], w_hi[:, c], R(hi[:, i, :]), i == 0)
                    if i == 0:
                        give_back(ins, chunk)
                    mm(ps[:, 0:T], w_lo[:, c], R(hi[:, i, :]))
                for i in range(KD):
                    pe.wait_ge(u_ready, row * KD + i + 1)
                    ins = mm(ps[:, 0:T], w_hi[:, i * P:(i + 1) * P], R(lo[:, i, :]), stop=i == KD - 1)
                done(ins, name)

            def project_tokens(names, k, lhs, width):
                ps = [claim(n) for n in names]
                hi, lo = lhs
                for i in range(k):
                    chunk = at["chunk"]
                    w_hi, w_lo = take(width // P)
                    for t in range(TT):
                        at_t = slice(t * P, (t + 1) * P)
                        ins = mm(ps[t][:, 0:width], R(hi[:, i, at_t]), w_hi, i == 0)
                        if t == 0:
                            give_back(ins, chunk)
                        mm(ps[t][:, 0:width], R(hi[:, i, at_t]), w_lo)
                        ins = mm(ps[t][:, 0:width], R(lo[:, i, at_t]), w_hi, stop=i == k - 1)
                        if i == k - 1:
                            done(ins, names[t])

            def sum_squares(name, matrix, n=1):
                ps = claim("ss_" + name)
                for i in range(n):
                    q = at["squares"]
                    at["squares"] += 1
                    pe.wait_ge(squares_ready, q + 1)
                    ins = mm(ps[:, 0:T], mat(matrix), squares[:, q % SQ, :], i == 0, i == n - 1)
                done(ins, "ss_" + name)

            def sum_gathered(name, row):
                ps = claim(name)
                pe.wait_ge(row_gathered, row - ROW_1 + 1)
                mm(ps[:, 0:T], mat("ones"), row_squares[:, KD - 2, :], True)
                pe.wait_ge(row_squares_ready, (row + 1) * KD)
                done(mm(ps[:, 0:T], mat("ones"), row_squares[:, KD - 1, :], stop=True), name)

            def sum_row(name, row, src):
                ps = claim(name)
                for i in range(KD):
                    pe.wait_ge(row_squares_ready, row * KD + i + 1)
                    ins = mm(ps[:, 0:T], mat("ones"), src[:, i, :], i == 0, i == KD - 1)
                done(ins, name)

            def ada_part(j):
                pe.wait_ge(ada_summed, j + 1)
                for half in range(2):
                    name = f"ada{j}{'ab'[half]}"
                    ps = claim(name)
                    for i in range(4):
                        c = (half * 4 + i) * P
                        ins = nc.tensor.transpose(ps[:, i * P:(i + 1) * P], ada_acc[:, j % 2, c:c + P], mat("ident"))
                    done(ins, name)

            pe.wait_ge(ones_ready, 1)
            sum_row("mem_ss", ROW_MEM, row_squares)
            pe.wait_ge(loaded["mats"], 16)
            mem_parts, u_parts, hidden_parts = (mem_n, mem_n_lo), (u, u_lo), (hidden, hidden_lo)
            project_first("mem_k0", mem_parts, ROW_MEM)
            project("mem_k1", KD, mem_parts)
            sum_squares("mem_k0", "ones")
            sum_row("x_ss", ROW_X, merged)
            project("mem_k2", KD, mem_parts)
            sum_squares("mem_k1", "ones")
            project("mem_k3", KD, mem_parts)
            sum_squares("mem_k2", "ones")
            pe.wait_ge(loaded["bias_in"], 32)
            done(mm(claim("bias")[0:8, 0:512], table[:, :], buckets[:, :], True, True), "bias")
            sum_squares("mem_k3", "ones")
            ada_part(0)
            ada_part(1)
            project_tokens(["mem_v0", "mem_v1"], KD, mem_parts, 512)

            pe.wait_ge(u_ready, (ROW_X + 1) * KD)
            project_tokens(["vsw0", "vsw1"], KD, u_parts, 256)
            project_tokens(["vsb0", "vsb1"], KD, u_parts, 512)
            project("ga", KD, u_parts)
            pe.wait_ge(loaded["small"], 48)
            for n in ("kc", "vc", "ks", "kw"):
                project(n, KD, u_parts)
            sum_squares("ks", "halves")
            for b in range(4):
                project(f"qa{b}", KD, u_parts)
                sum_squares(f"qa{b - 1}" if b else "kw", "halves")
            for b in range(4):
                project(f"kb{b}", KD, u_parts)
                if b == 0:
                    sum_squares("qa3", "halves")
            for b in range(4):
                project(f"qb{b}", KD, u_parts)
            ada_part(2)

            for w, n in enumerate("kv"):
                evacuated(pe, n + "c" if n == "v" else "kc")
                name = f"cmp_hid_{n}"
                ps = claim(name)
                for j in range(32):
                    chunk = at["chunk"]
                    ins = mm(ps[0:N_CMP + 2, 0:P], kc_ext[:, w, j:j + 257:CMP_STRIDE], take_plain(), j == 0, j == 31)
                    if j < 31:
                        give_back(ins, chunk)
                done(ins, name)

            def cmp_turn():
                for w, n in enumerate("kv"):
                    evacuated(pe, f"cmp_hid_{n}")
                    ps = claim(f"cmp_turn_{n}")
                    done(mm(ps[:, 0:N_CMP], cmp_sb[0:N_CMP + 2, w, :], mats[0:N_CMP + 2, MAT["spread"], 0:N_CMP],
                            True, True), f"cmp_turn_{n}")
                evacuated(pe, "ga")
                ps = claim("ga_turn")
                for t in range(TT):
                    ins = mm(ps[:, t * 24:(t + 1) * 24], gate_raw[:, t * P:(t + 1) * P], mats[0:24, MAT["ident"], 0:24], t == 0, t == TT - 1)
                done(ins, "ga_turn")

            def cmp_out():
                evacuated(pe, "cmp_turn_k")
                ps = claim("cmp_out_k")
                done(mm(ps[:, 0:N_CMP], cmp_w2[:, 0, :], cmp_turned[:, 0, 0:N_CMP], True, True), "cmp_out_k")
                evacuated(pe, "cmp_turn_v")
                ps = claim("cmp_out_v")
                done(mm(ps[0:N_CMP, 0:P], cmp_turned[:, 1, 0:N_CMP], cmp_w2[:, 1, :], True, True), "cmp_out_v")

            def cmp_sum():
                evacuated(pe, "cmp_out_k")
                done(mm(claim("ss_cmp")[:, 0:N_CMP], mat("halves"), cmp_k[:, 1, 0:N_CMP], True, True), "ss_cmp")

            def sb_scores(h):
                evacuated(pe, f"kb{h // 2}")
                evacuated(pe, f"qb{h // 2}")
                ps = claim(f"sbz{h}")
                mm(ps[:, 0:T], pair_k[:, h, 0:P], pair_q[:, h // 2, :], True)
                done(mm(ps[:, T:T + P], pair_k[:, h, P:T], pair_q[:, h // 2, P:T], stop=True), f"sbz{h}")

            def sb_logits(h):
                pe.wait_ge(softplus_ready, h + 1)
                ps = bank(f"sbz{h}")
                soft = sbw[:, h % 2, 2, :]
                mm(ps[:, 0:T], mat("neg_suffix"), soft[:, 0:T])
                mm(ps[:, P:T], mat("neg_ones"), soft[:, T:T + P])
                mm(ps[:, T:T + P], mat("neg_suffix"), soft[:, T:T + P])
                mm(ps[:, 0:P], mat("ident"), mat("not_before"))
                mm(ps[:, T:T + P], mat("ident"), mat("not_before"), stop=True).then_inc(sb_logits_ready, 1)

            def sb_values(h):
                evacuated(pe, f"sbz{h}")
                name = f"sbo{h // 2}"
                ps = claim(name) if h % 2 == 0 else bank(name)
                w = sbw[:, h % 2, 3, :]
                mm(ps[:, 0:T], pair_v[:, 0, h, :], w[:, 0:T], h % 2 == 0)
                ins = mm(ps[:, P:T], pair_v[:, 1, h, :], w[:, T:T + P], stop=h % 2 == 1)
                if h % 2 == 1:
                    done(ins, name)

            ada_part(3)
            def nsa_scores(i):
                b, s = i // 2, i % 2
                for c, q, k in (("a", slice(0, P), slice(0, 272)), ("b", slice(P, T), slice(0, 272)),
                                ("c", slice(P, T), slice(272, 528))):
                    ps = claim(f"nsa{i}{c}")
                    done(mm(ps[:, 0:k.stop - k.start], qa[:, b, q], kcat[:, s, k], True, True), f"nsa{i}{c}")

            def turn_block(ps, at_col, src):
                return nc.tensor.transpose(ps[:, at_col:at_col + P], src, mat("ident"))

            def nsa_turn(i):
                pe.wait_ge(weights_ready, i + 1)
                w = logit[:, 1 - i % 2, :]
                for br, c in enumerate("sw"):
                    ps = claim(f"nsat{i}{c}")
                    late = T + br * T
                    turn_block(ps, 0, w[:, br * P:(br + 1) * P])
                    turn_block(ps, P, w[:, late:late + P])
                    done(turn_block(ps, T, w[:, late + P:late + T]), f"nsat{i}{c}")
                ps = claim(f"nsat{i}c")
                turn_block(ps[0:N_CMP], 0, w[:, 768:768 + N_CMP])
                done(turn_block(ps[0:N_CMP], P, w[:, 784:784 + N_CMP]), f"nsat{i}c")

            def nsa_values(i):
                b, s = i // 2, i % 2
                name = f"nsao{b}"
                ps = claim(name) if s == 0 else bank(name)
                for br, c in enumerate("sw"):
                    evacuated(pe, f"nsat{i}{c}")
                    w = turned[:, i % 2, br, :]
                    mm(ps[:, 0:T], vcat[:, 0, br, s, :], w[:, 0:T], s == 0 and br == 0)
                    mm(ps[:, P:T], vcat[:, 1, br, s, :], w[:, T:T + P])
                evacuated(pe, f"nsat{i}c")
                ins = mm(ps[:, 0:T], vcmp[0:N_CMP, s, :], turned_c[0:N_CMP, i % 2, :, :], stop=s == 1)
                if s == 1:
                    done(ins, name)

            evacuated(pe, "vsb0")
            evacuated(pe, "vsb1")
            sb_scores(0)
            for h in range(8):
                project(f"ma{h}", KD, u_parts)
                if h == 0:
                    cmp_turn()
                if h == 1:
                    cmp_out()
                if h == 2:
                    cmp_sum()
                if h == 5:
                    ada_part(4)
                if h < 7:
                    sb_scores(h + 1)
                sb_logits(h)
                if h == 7:
                    for n in ("vsw0", "vsw1", "ks", "kw", "qa0", "qa1", "qa2", "qa3", "cmp_out_v"):
                        evacuated(pe, n)
                    pe.wait_ge(cmp_k_ready, 1)
                    nsa_scores(0)
                if h:
                    sb_values(h - 1)
            sb_values(7)
            nsa_scores(1)

            for i in range(8):
                project(f"mb{i}", KD, u_parts)
                if i == 0:
                    ada_part(5)
                if i:
                    nsa_values(i - 1)
                nsa_turn(i)
                if i < 6:
                    nsa_scores(i + 2)
            nsa_values(7)

            for m in range(KD):
                project(f"up_nsa{m}", 4, (attn_a, attn_a_lo1), (lambda i: evacuated(pe, f"nsao{i}")) if m == 0 else None)
                project(f"up_sb{m}", 4, (attn_b, attn_b_lo1), (lambda i: evacuated(pe, f"sbo{i}")) if m == 0 else None)
            for m in range(KD):
                project(f"mix{m}", KD, (merged, merged_lo1), (lambda i: pe.wait_ge(merged_ready, i + 1)) if m == 0 else None)

            sum_gathered("x1_ss", ROW_1)
            project_first("w1_0", u_parts, ROW_1)
            for m in range(1, KF):
                project(f"w1_{m}", KD, u_parts)
            for m in range(KD):
                project(f"w2_{m}", KF, hidden_parts, (lambda i: pe.wait_ge(hidden_ready, i + 1)) if m == 0 else None)

            def swiglu(p, row, before):
                project_first(f"{p}g0", u_parts, row)
                project(f"{p}u0", KD, u_parts)
                for m in range(1, KF2):
                    project(f"{p}g{m}", KD, u_parts)
                    project(f"{p}u{m}", KD, u_parts)
                for m in range(KD):
                    project(f"{p}d{m}", KF2, hidden_parts, (lambda i: pe.wait_ge(hidden_ready, before + i + 1)) if m == 0 else None)

            sum_gathered("x2_ss", ROW_2)
            swiglu("f1", ROW_2, KF)

            sum_gathered("x3_ss", ROW_3)
            project_first("cq0", u_parts, ROW_3)
            project("cq1", KD, u_parts)
            project("cq2", KD, u_parts)
            project("ckv0", KD, u_parts)
            sum_squares("cq", "ones", 3)
            project("ckv1", KD, u_parts)
            project("kr", KD, u_parts)
            sum_squares("ckv", "ones", 2)
            project("qm0", KD, u_parts)
            project("qm1", KD, u_parts)
            sum_squares("qm0", "ones")
            project("qm2", KD, u_parts)
            sum_squares("qm1", "ones")
            project("qm3", KD, u_parts)
            sum_squares("qm2", "ones")
            evacuated(pe, "kr")
            done(mm(claim("kr_rot")[:, 0:T], mat("rotate"), kr[:, 0, :], True, True), "kr_rot")
            for h in range(8):
                project(f"uq{h}", 3, (latent, latent_lo), (lambda i: pe.wait_ge(latent_ready, i + 1)) if h == 0 else None)
                if h == 0:
                    sum_squares("qm3", "ones")
                else:
                    sum_squares(f"uq{h - 1}", "q_odd" if (h - 1) % 2 else "q_even")

            def sum_k_squares(b):
                for h in (2 * b, 2 * b + 1):
                    pe.wait_ge(k_squares_ready, h + 1)
                    done(mm(claim(f"ss_uk{h}")[:, 0:T], mat("ones"), k_squares[:, 2 * (h % 2) + b % 2, :], True, True),
                         f"ss_uk{h}")

            kv_latent = (latent[:, 3:5, :], latent_lo[:, 3:5, :])
            for b in range(4):
                project(f"uk{b}", 2, kv_latent, (lambda i: pe.wait_ge(latent_ready, 4 + i)) if b == 0 else None)
                if b == 0:
                    sum_squares("uq7", "q_odd")
                else:
                    sum_k_squares(b - 1)
            sum_k_squares(3)
            project_tokens(["uv0", "uv1"], 2, kv_latent, 512)
            project_tokens(["sv0", "sv1"], KD, u_parts, 512)
            for b in range(4):
                project(f"su{b}", KD, u_parts)

            def scores(i):
                if i < 8:
                    ps = claim(f"mla{i}")
                    mm(ps[:, 0:P], pair_q[:, i, 0:P], pair_k[:, i, 0:P], True)
                    done(mm(ps[:, P:384], pair_q[:, i, P:T], pair_k[:, i, :], stop=True), f"mla{i}")
                else:
                    h = i - 8
                    evacuated(pe, f"qm{h}")
                    evacuated(pe, f"mem_k{h}")
                    ps = claim(f"mem{h}")
                    mm(ps[:, 0:T], qa[:, h, 0:P], mem_k[:, h, :], True)
                    done(mm(ps[:, T:2 * T], qa[:, h, P:T], mem_k[:, h, :], stop=True), f"mem{h}")

            def turn(i):
                pe.wait_ge(weights_ready, 8 + i + 1)
                w = logit[:, 1 - i % 2, :]
                if i < 8:
                    ps = claim(f"mlat{i}")
                    for j in range(3):
                        ins = turn_block(ps, j * P, w[:, j * P:(j + 1) * P])
                    done(ins, f"mlat{i}")
                else:
                    ps = claim(f"memt{i - 8}")
                    for kt in range(2):
                        for qt in range(2):
                            j = qt * 2 + kt
                            ins = turn_block(ps, (kt * 2 + qt) * P, w[:, j * P:(j + 1) * P])
                    done(ins, f"memt{i - 8}")

            def values(i):
                w = turned[:, i % 2, 0, :]
                if i < 8:
                    evacuated(pe, f"mlat{i}")
                    name = f"mlao{i // 2}"
                    ps = claim(name) if i % 2 == 0 else bank(name)
                    mm(ps[:, 0:T], pair_v[:, 0, i, :], w[:, 0:T], i % 2 == 0)
                    ins = mm(ps[:, P:T], pair_v[:, 1, i, :], w[:, T:T + P], stop=i % 2 == 1)
                    if i % 2:
                        done(ins, name)
                else:
                    h = i - 8
                    evacuated(pe, f"memt{h}")
                    ps = claim(f"memo{h}")
                    mm(ps[:, 0:T], mem_v[:, 0, h * P:(h + 1) * P], w[:, 0:T], True)
                    done(mm(ps[:, 0:T], mem_v[:, 1, h * P:(h + 1) * P], w[:, T:2 * T], stop=True), f"memo{h}")

            for n in ("uv0", "uv1", "mem_v0", "mem_v1"):
                evacuated(pe, n)
            pe.wait_ge(normed, 16)
            scores(0)
            project("gate0", KD, u_parts)
            project("gate1", KD, u_parts)
            for i in range(12):
                if i < 11:
                    project(f"gate{2 * i + 2}", KD, u_parts)
                    project(f"gate{2 * i + 3}", KD, u_parts)
                    scores(i + 1)
                if i:
                    values(i - 1)
                turn(i)
            pe.wait_ge(sg_ln_ready, TT)
            pe.wait_ge(sg_w_ready, 1)
            for b in range(4):
                for c in range(TT):
                    name = f"sg{b}{c}"
                    ps = claim(name)
                    mm(ps[:, 0:T], sg_v[:, c, b * P:(b + 1) * P], sg_w[:, 2 * b:2 * b + 2, :], True)
                    done(mm(ps[:, 0:T], mats[0:1, MAT["ones"], :], sg_b[:, b * T:(b + 1) * T], stop=True), name)
            values(11)

            pe.wait_ge(sg_ready, 4)
            for m in range(KD):
                project(f"br_a{m}", 4, (attn_a, attn_a_lo2))
                project(f"br_b{m}", 4, (attn_b, attn_b_lo2), (lambda i: evacuated(pe, f"mlao{i}")) if m == 0 else None)
                project(f"br_c{m}", 4, (attn_c, attn_c_lo2), (lambda i: evacuated(pe, f"memo{i}")) if m == 0 else None)
            for m in range(KD):
                project(f"mix2_{m}", KD, (merged, merged_lo2), (lambda i: pe.wait_ge(merged_ready, KD + i + 1)) if m == 0 else None)
            sum_gathered("x4_ss", ROW_4)
            swiglu("f2", ROW_4, KF + KF2)

        @block.gpsimd
        def _(pool):
            def load_ada_early(n):
                r = n % len(ada_early)
                if n >= len(ada_early):
                    pool.wait_ge(ada_used, n - len(ada_early) + 1)
                pool.dma_start(ada_early[r], ada[n]).then_inc(ada_early_full[r], 16)

            def load_ada(n):
                pool.wait_ge(ada_used, max(n - ADA_RING + 1, ADA_EARLY))
                pool.dma_start(ada_ring[:, (n - ADA_EARLY) % ADA_RING, :], ada[n]).then_inc(ada_full[(n - ADA_EARLY) % ADA_RING], 16)

            for n in range(2):
                load_ada_early(n)
            kcat_all, early = kcat[:], 2
            for t in (kcat_all, vcat[:], pair_k, pair_v[:]):
                pool.memset(t, 0.0).then_inc(zeros_ready, 1)
                if t is not kcat_all:
                    load_ada_early(early)
                    early += 1
            for n in range(early, len(ada_early)):
                load_ada_early(n)

            def split_slot(q):
                pool.wait_ge(slot_rounded, q + 1)
                w = slot_weights(split_slots[q])
                pool.tensor_tensor(R(w), w, R(slot_round(q)), ALU.subtract).then_inc(slot_split_by_pool, 1)

            split_slot(1)
            for n in range(len(ada_early), 15):
                load_ada_early(n)
            split_slot(3)
            load_ada_early(15)
            split_slot(5)
            split_slot(7)
            evacuated(pool, "bias")
            pool.memset(vcmp, 0.0).then_inc(zeros_ready, 1)
            for c in range(N_CMP):
                first = 2 * CMP_STRIDE - 1 + CMP_STRIDE * c
                last = pool.tensor_copy(bias_steps[:, :, c], bias_line[:, first:first + T])
            last.then_inc(lines_ready, 1)
            for n in range(ADA_EARLY, ADA_EARLY + ADA_RING):
                load_ada(n)
            pool.wait_ge(lines_ready, 1)
            for h in range(8):
                if h >= 6:
                    load_ada(ADA_EARLY + ADA_RING + h - 6)
                line = bias_line[h:h + 1, :]
                pool.dma_start(bias[:, h, :], bass.AP(line.tensor, line.offset + P - 1, [[line.ap[0][0], 1], [-1, P], [1, T]])
                               ).then_inc(loaded["bias"], 16)
                step = bias_steps[h:h + 1, :, :]
                for t in range(TT):
                    pool.dma_start(bias_cmp[:, h, t, :],
                                   bass.AP(step.tensor, step.offset + (T - 1 - t * P) * N_CMP,
                                           [[step.ap[0][0], 1], [-N_CMP, P], [1, N_CMP]])).then_inc(loaded["bias"], 16)
            for n in range(ADA_EARLY + ADA_RING + 2, 48):
                load_ada(n)

            at = {"q": first_of_pool, "gathered": 0}

            def split_slots_until(name):
                while at["q"] < len(split_slots) and split_slots[at["q"]] < slot_at[name] + HALVES:
                    q = at["q"]
                    at["q"] += 1
                    if by_pool(q):
                        split_slot(q)

            def gather_squares(row, last):
                for i in range(1, KD - 1):
                    split_slots_until(f"{last}{i}")
                    pool.wait_ge(row_squares_ready, row * KD + i + 1)
                    ins = pool.tensor_tensor(row_squares[:, i, :], row_squares[:, i - 1, :], row_squares[:, i, :], ALU.add)
                    if i < KD - 2:
                        at["gathered"] += 1
                        ins.then_inc(row_gathering, 1)
                        pool.wait_ge(row_gathering, at["gathered"])
                ins.then_inc(row_gathered, 1)

            split_slots_until("mb0")
            pool.wait_ge(ada_used, 48)
            pool.dma_start(sg_w[:, :, :], sg_w_d).then_inc(loaded["sg"], 16)
            pool.dma_start(sg_ln[:, :, :], sg_ln_d).then_inc(loaded["sg"], 16)
            gather_squares(ROW_1, "mix")
            pool.wait_ge(loaded["bias"], 16 * 24)
            pool.dma_start(sg_b, sg_b_d).then_inc(loaded["sg"], 16)
            pool.wait_ge(loaded["sg"], 48)
            pool.affine_select(out=sg_w[:, :, :], in_=sg_w[:, :, :], compare_op=ALU.is_ge, fill=0.0, base=0,
                               pattern=[[0, 8], [1, P]], channel_multiplier=-1).then_inc(sg_w_ready, 1)
            for row, last in ((ROW_2, "w2_"), (ROW_3, "f1d"), (ROW_4, "mix2_")):
                gather_squares(row, last)
            split_slots_until("f2d7")

        @block.scalar
        def _(act):
            n_squares, n_rinv, n_row = [0], [0], [0]
            step = chain(act, act_step)
            a = nc.scalar.activation

            def round_slot(q, n):
                act.wait_ge(slot_full[n % RING], 16 * (n // RING + 1))
                if q >= HALVES:
                    act.wait_ge(slot_used, split_slots[q - HALVES] + 1)
                a(R(slot_round(q)), slot_weights(n), ACT.Copy).then_inc(slot_rounded, 1)

            ahead = splitter(round_slot)

            def output(name, reach=HALVES):
                ahead(name, reach)
                full(act, name)

            def taken(name):
                ahead(name)
                evacuated(act, name)

            def square(name):
                n = n_squares[0]
                n_squares[0] += 1
                output(name)
                a(squares[:, n % SQ, :], bank(name)[:, 0:T], ACT.Square).then_inc(squares_ready, 1)

            def inv_rms(name, width, last_reader):
                n = n_rinv[0]
                n_rinv[0] += 1
                output("ss_" + name)
                free(a(log_ms[:, :], bank("ss_" + name)[:, 0:T], ACT.Ln, scale=1.0 / width, bias=col("eps")), "ss_" + name)
                taken("ss_" + name)
                if last_reader:
                    last_reader()
                a(rinv[:, n % 2, :], log_ms[:, :], ACT.Exp, scale=-0.5).then_inc(rinv_ready, 1)
                act.wait_ge(rinv_ready, n + 1)

            def row_square(dst, src, ready=None):
                for i in range(KD):
                    if ready:
                        ready(i)
                    a(dst[:, i, :], src[:, i, :], ACT.Square).then_inc(row_squares_ready, 1)

            def row_inv(name, reach=HALVES):
                n_row[0] += 1
                output(name, reach)
                free(a(log_ms[:, :], bank(name)[:, 0:T], ACT.Ln, scale=1.0 / D, bias=col("eps")), name)
                evacuated(act, name)
                a(row_rinv[:, :], log_ms[:, :], ACT.Exp, scale=-0.5).then_inc(row_rinv_ready, 1)
                act.wait_ge(row_rinv_ready, n_row[0])

            def round_row(row, hi, lo):
                for i in range(KD):
                    act.wait_ge(u_normed, row * KD + i + 1)
                    a(R(hi[:, i, :]), lo[:, i, :], ACT.Copy).then_inc(u_rounded, 1)

            def shift_row(row, shift, meanwhile=None):
                for i in range(KD):
                    if meanwhile and i in (2, 6):
                        ahead(meanwhile, i // 6)
                    act.wait_ge(u_normed, row * KD + i + 1)
                    a(R(u[:, i, :]), u_lo[:, i, :], ACT.Identity,
                      bias=mod[:, shift * 8 + i:shift * 8 + i + 1]).then_inc(u_rounded, 1)

            def copy(dst, name, src=None, **kw):
                output(name)
                free(a(dst, bank(name)[:, 0:T] if src is None else src, ACT.Copy, **kw), name)

            def spread_heads(dst, name):
                output(name)
                src = bank(name)[:, :].rearrange("p (b s d) -> p b s d", s=2, d=HD)
                dst = dst.rearrange("p (b s) c -> p b s c", s=2)
                a(dst[:, :, 0, 0:HD], src[:, :, 0, :], ACT.Copy)
                free(a(dst[:, :, 1, HD:P], src[:, :, 1, :], ACT.Copy), name)

            nc.scalar.preload_act_table_set("exp_and_others")
            act.wait_ge(loaded["cols"], 16)
            a(c_act[:, 0, :], cols[:, AT["c"]:AT["c"] + 8], ACT.Tanh, scale=0.5).then_inc(c_tanh_ready, 1)
            nc.scalar.preload_act_table_set("natural_log_exp_and_others")
            act.wait_ge(loaded["mem"], 16)
            row_square(row_squares, mem_n, lambda i: act.wait_ge(loaded["mem_end"], 16) if i == KD // 2 else None)
            ahead("mem_ss", 1)
            row_inv("mem_ss", 1)
            round_row(ROW_MEM, mem_n, mem_n_lo)
            square("mem_k0")
            act.wait_ge(loaded["x"], 16)
            row_square(merged, x)
            square("mem_k1")
            inv_rms("mem_k0", P, None)
            act.wait_ge(u_normed, KD)
            row_inv("x_ss")
            square("mem_k2")
            inv_rms("mem_k1", P, None)
            square("mem_k3")
            inv_rms("mem_k2", P, lambda: taken("mem_k0"))
            inv_rms("mem_k3", P, lambda: taken("mem_k1"))
            shift_row(ROW_X, 0, "mem_v0")
            for t in range(TT):
                copy(mem_v[:, t, :], f"mem_v{t}", bank(f"mem_v{t}")[:, :])

            act.wait_ge(zeros_ready, 4)
            for t in range(TT):
                output(f"vsw{t}")
                src = bank(f"vsw{t}")[:, 0:256].rearrange("p (r s d) -> p r s d", r=2, d=HD)
                a(vcat[:, t, :, 0, 0:HD], src[:, :, 0, :], ACT.Copy)
                free(a(vcat[:, t, :, 1, HD:P], src[:, :, 1, :], ACT.Copy), f"vsw{t}")
            for t in range(TT):
                spread_heads(pair_v[:, t, :, :], f"vsb{t}")
            copy(gate_raw, "ga", bank("ga")[0:24, 0:T])
            for w, n in enumerate(("kc", "vc")):
                copy(kc_ext[:, w, 0:T], n)
            square("ks")
            square("kw")
            inv_rms("ks", HD, lambda: taken("mem_k2"))
            for b in range(4):
                square(f"qa{b}")
                inv_rms(f"qa{b - 1}" if b else "kw", HD, lambda: taken(("mem_k3", "ks", "kw", "qa0")[b]))
            inv_rms("qa3", HD, lambda: taken("qa1"))
            for b in range(4):
                output(f"kb{b}")
                ps = bank(f"kb{b}")
                a(pair_k[LO, 2 * b, :], ps[LO, 0:T], ACT.Copy)
                free(a(pair_k[HI, 2 * b + 1, :], ps[HI, 0:T], ACT.Copy), f"kb{b}")
            for b in range(4):
                copy(pair_q[:, b, :], f"qb{b}", scale=HD ** -0.5)
            for w, n in enumerate("kv"):
                copy(cmp_sb[0:N_CMP + 2, w, :], f"cmp_hid_{n}", bank(f"cmp_hid_{n}")[0:N_CMP + 2, 0:P])

            def sb_log(h):
                output(f"sbz{h}")
                w = sbw[:, h % 2, :, :]
                step(a(w[:, 0, :], bank(f"sbz{h}")[:, 0:384], ACT.Abs))
                step(a(w[:, 0, :], w[:, 0, :], ACT.Exp, scale=-1.0))
                a(w[:, 1, :], w[:, 0, :], ACT.Ln, bias=1.0).then_inc(sb_log_ready, 1)

            def sb_exp(h):
                act.wait_ge(sb_logits_ready, h + 1)
                free(a(sbw[:, h % 2, 3, :], bank(f"sbz{h}")[:, 0:384], ACT.Exp), f"sbz{h}")

            sb_log(0)
            act.wait_ge(loaded["bias"], 16 * 24)
            for h in range(8):
                copy(gates[:, h, :], f"ma{h}")
                if h == 0:
                    nc.scalar.preload_act_table_set("exp_and_others")
                    for w, n in enumerate("kv"):
                        output(f"cmp_turn_{n}")
                        a(cmp_tanh[:, w, 0:N_CMP], bank(f"cmp_turn_{n}")[:, 0:N_CMP], ACT.Tanh, scale=0.5).then_inc(cmp_tanh_ready, 1)
                    output("ga_turn")
                    free(a(gate_tanh[:, :, :], bank("ga_turn")[:, 0:48].rearrange("p (t g) -> p t g", t=TT), ACT.Tanh, scale=0.5), "ga_turn")
                    nc.scalar.preload_act_table_set("natural_log_exp_and_others")
                if h == 1:
                    output("cmp_out_k")
                    a(cmp_k[:, 0, 0:N_CMP], bank("cmp_out_k")[:, 0:N_CMP], ACT.Copy)
                    free(a(cmp_k[:, 1, 0:N_CMP], bank("cmp_out_k")[:, 0:N_CMP], ACT.Square), "cmp_out_k")
                    output("cmp_out_v")
                    ps = bank("cmp_out_v")
                    act.wait_ge(zeros_ready, 5)
                    a(vcmp[0:N_CMP, 0, 0:HD], ps[0:N_CMP, 0:HD], ACT.Copy)
                    free(a(vcmp[0:N_CMP, 1, HD:P], ps[0:N_CMP, HD:P], ACT.Copy), "cmp_out_v")
                if h == 2:
                    output("ss_cmp")
                    free(a(cmp_k[:, 2, 0:N_CMP], bank("ss_cmp")[:, 0:N_CMP], ACT.Ln, scale=1.0 / HD, bias=col("eps")), "ss_cmp")
                    taken("ss_cmp")
                    a(cmp_k[:, 3, 0:N_CMP], cmp_k[:, 2, 0:N_CMP], ACT.Exp, scale=-0.5).then_inc(cmp_rinv_ready, 1)
                if h < 7:
                    sb_log(h + 1)
                sb_exp(h)

            def exps(i, parts):
                ahead(f"nsa{i}c" if i < 8 else f"mla{i - 8}")
                act.wait_ge(logits_ready, i + 1)
                for k, (src, dst) in parts.items():
                    ins = a(dst, src, ACT.Exp, bias=stats[:, i % 2, 0, k:k + 1], accum_out=stats[:, i % 2, 1, k:k + 1])
                ins.then_inc(weights_raw, 1)

            def nsa_exp(i):
                w = logit[:, 1 - i % 2, :]
                at = [w[:, 0:128], w[:, 128:256], w[:, 256:512], w[:, 512:768], w[:, 768:768 + N_CMP], w[:, 784:784 + N_CMP]]
                exps(i, {k: (s, s) for k, s in enumerate(at)})

            nsa_exp(0)
            nc.scalar.preload_act_table_set("exp_and_others")
            for i in range(8):
                output(f"mb{i}")
                free(a(gates[:, 8 + i, :], bank(f"mb{i}")[:, 0:T], ACT.Tanh, scale=0.5), f"mb{i}")
                if i % 2 == 0:
                    k = i
                    taken(f"ma{k + 1}")
                    a(gates[:, k:k + 2, :], gates[:, k:k + 2, :], ACT.Tanh, scale=0.5).then_inc(tanh_ready, 1)
                if i < 7:
                    nsa_exp(i + 1)
                copy(turned[:, i % 2, 0, 0:384], f"nsat{i}s", bank(f"nsat{i}s")[:, 0:384])
                copy(turned_c[0:N_CMP, i % 2, :, :], f"nsat{i}c",
                     bank(f"nsat{i}c")[0:N_CMP, 0:T].rearrange("p (t q) -> p t q", t=TT))

            def round_merged(before, lo):
                for m in range(KD):
                    ahead(f"{'up_sb' if before == 0 else 'br_c'}{m}")
                    act.wait_ge(merged_raw, before + m + 1)
                    a(R(merged[:, m, :]), lo[:, m, :], ACT.Copy).then_inc(merged_rounded, 1)

            def round_hidden(i):
                a(R(hidden[:, i, :]), hidden_lo[:, i, :], ACT.Copy).then_inc(hidden_rounded, 1)

            round_merged(0, merged_lo1)

            nc.scalar.preload_act_table_set("natural_log_exp_and_others")
            row_square(row_squares, x, lambda i: taken(f"mix{i}"))
            row_inv("x1_ss")
            shift_row(ROW_1, 3)
            nc.scalar.preload_act_table_set("silu_and_others")
            for m in range(KF):
                output(f"w1_{m}")
                if m >= 2:
                    act.wait_ge(hidden_raw, m - 1)
                free(a(part[:, m % 2, :], bank(f"w1_{m}")[:, 0:T], ACT.Relu), f"w1_{m}")
                if m:
                    act.wait_ge(hidden_raw, m)
                    round_hidden(m - 1)
            act.wait_ge(hidden_raw, KF)
            round_hidden(KF - 1)
            def square_and_round(row, last, i):
                taken(f"{last}{i}")
                a(row_squares[:, i, :], x[:, i, :], ACT.Square).then_inc(row_squares_ready, 1)
                act.wait_ge(u_normed, row * KD + i + 1)
                a(R(u[:, i, :]), u_lo[:, i, :], ACT.Copy).then_inc(u_rounded, 1)

            for i in range(KD):
                if i == 2:
                    act.wait_ge(rope_angle_ready, 1)
                    a(rope[:, :, :], rope[:, :, :], ACT.Sin).then_inc(rope_ready, 1)
                if i == 4:
                    nc.scalar.preload_act_table_set("natural_log_exp_and_others")
                square_and_round(ROW_2, "w2_", i)
            row_inv("x2_ss")
            nc.scalar.preload_act_table_set("silu_and_others")

            def swiglu(p, before):
                for m in range(KF2):
                    taken(f"{p}g{m}")
                    a(part[:, m % 2, :], part[:, m % 2, :], ACT.Silu).then_inc(silu_ready, 1)
                    if m:
                        act.wait_ge(hidden_raw, before + m)
                        round_hidden(m - 1)
                ahead(f"{p}u{KF2 - 1}")
                act.wait_ge(hidden_raw, before + KF2)
                round_hidden(KF2 - 1)

            swiglu("f1", KF)

            nc.scalar.preload_act_table_set("natural_log_exp_and_others")
            row_square(row_squares, x, lambda i: taken(f"f1d{i}"))
            row_inv("x3_ss")
            round_row(ROW_3, u, u_lo)

            def latent_block(i, name, gain, k):
                square(name)
                free(a(latent[:, i, :], bank(name)[:, 0:T], ACT.Copy, scale=col(gain, k)), name)

            for b in range(3):
                latent_block(b, f"cq{b}", "mla_cq_norm_2", b)
            inv_rms("cq", 384, lambda: taken("qa2"))
            latent_block(3, "ckv0", "mla_ckv_norm_2", 0)
            latent_block(4, "ckv1", "mla_ckv_norm_2", 1)
            output("kr")
            ps = bank("kr")
            for s in range(2):
                a(k_squares[HI, s, :], ps[HI, 0:T], ACT.Square, scale=0.5 ** 0.5)
                a(k_squares[LO, 2 + s, :], ps[LO, 0:T], ACT.Square, scale=0.5 ** 0.5)
            free(a(kr[:, 0, :], ps[:, 0:T], ACT.Copy, scale=col("mla_k_rope")), "kr")
            inv_rms("ckv", 256, lambda: taken("qa3"))
            square("qm0")
            square("qm1")
            inv_rms("qm0", P, lambda: act.wait_ge(latent_ready, 3))
            square("qm2")
            inv_rms("qm1", P, lambda: act.wait_ge(latent_ready, 5))
            square("qm3")
            inv_rms("qm2", P, lambda: taken("qm0"))
            square("uq0")
            inv_rms("qm3", P, lambda: taken("qm1"))
            for h in range(1, 8):
                square(f"uq{h}")
                inv_rms(f"uq{h - 1}", 96, lambda: taken(f"qm{h + 1}") if h < 3 else act.wait_ge(normed, h - 2))

            def k_square(b):
                output(f"uk{b}")
                ps = bank(f"uk{b}")
                a(k_squares[LO, b % 2, :], ps[LO, 0:T], ACT.Square).then_inc(k_squares_ready, 1)
                a(k_squares[HI, 2 + b % 2, :], ps[HI, 0:T], ACT.Square).then_inc(k_squares_ready, 1)

            k_square(0)
            inv_rms("uq7", 96, lambda: act.wait_ge(normed, 6))
            for b in range(4):
                if b < 3:
                    k_square(b + 1)
                for h in (2 * b, 2 * b + 1):
                    inv_rms(f"uk{h}", 96, lambda: act.wait_ge(normed, 7 + h))
            for t in range(TT):
                spread_heads(pair_v[:, t, :, :], f"uv{t}")
            nc.scalar.preload_act_table_set("gelu_and_others")
            for t in range(TT):
                output(f"sv{t}")
                free(a(sg_v[:, t, :], bank(f"sv{t}")[:, :], ACT.Gelu), f"sv{t}")
            for b in range(4):
                output(f"su{b}")
                free(a(attn_a[:, b, :], bank(f"su{b}")[:, 0:T], ACT.Gelu), f"su{b}")
            nc.scalar.preload_act_table_set("natural_log_exp_and_others")
            act.wait_ge(sg_var_ready, 1)
            step(a(sg_stat[:, :, 8], sg_stat[:, :, 7], ACT.Ln, bias=col("eps")))
            a(sg_stat[:, :, 9], sg_stat[:, :, 8], ACT.Exp, scale=-0.5).then_inc(sg_dev_ready, 1)

            nc.scalar.preload_act_table_set("exp_and_others")

            def attend(i):
                w = logit[:, 1 - i % 2, :]
                if i < 8:
                    exps(8 + i, {0: (w[:, 0:P],) * 2, 1: (w[:, P:384],) * 2})
                else:
                    ps = bank(f"mem{i - 8}")
                    ahead(f"mem{i - 8}")
                    act.wait_ge(logits_ready, 8 + i + 1)
                    a(w[:, 0:T], ps[:, 0:T], ACT.Exp, scale=P ** -0.5, bias=stats[:, i % 2, 0, 0:1],
                      accum_out=stats[:, i % 2, 1, 0:1])
                    a(w[:, T:2 * T], ps[:, T:2 * T], ACT.Exp, scale=P ** -0.5, bias=stats[:, i % 2, 0, 1:2],
                      accum_out=stats[:, i % 2, 1, 1:2]).then_inc(weights_raw, 1)
                    act.wait_ge(weights_raw, 8 + i + 1)
                    free(a(stats[:, i % 2, 3, 5:6], stats[:, i % 2, 1, 1:2], ACT.Copy), f"mem{i - 8}")

            act.wait_ge(half_bias_ready, 1)

            def two_gates(first):
                for g in (first, first + 1):
                    output(f"gate{g}")
                    free(a(gates[:, g, :], bank(f"gate{g}")[:, 0:T], ACT.Tanh, scale=0.5, bias=half_bias[:, g:g + 1]), f"gate{g}")

            attend(0)
            two_gates(0)
            for i in range(12):
                if i < 11:
                    two_gates(2 * i + 2)
                if i < 11:
                    attend(i + 1)
                if i < 8:
                    copy(turned[:, i % 2, 0, 0:384], f"mlat{i}", bank(f"mlat{i}")[:, 0:384])
                else:
                    copy(turned[:, i % 2, 0, :], f"memt{i - 8}", bank(f"memt{i - 8}")[:, :])
            round_merged(KD, merged_lo2)

            nc.scalar.preload_act_table_set("natural_log_exp_and_others")
            for i in range(KD):
                square_and_round(ROW_4, "mix2_", i)
            row_inv("x4_ss")
            nc.scalar.preload_act_table_set("silu_and_others")
            swiglu("f2", KF + KF2)
            for m in range(KD):
                ahead(f"f2d{m}")

        @block.vector
        def _(dve):
            v = nc.vector
            step = chain(dve, dve_step)
            n_rinv, n_ada = [0], [0]

            def split_slot(q, n):
                if by_pool(q):
                    return
                dve.wait_ge(slot_rounded, q + 1)
                w = slot_weights(n)
                v.tensor_tensor(R(w), w, R(slot_round(q)), ALU.subtract).then_inc(slot_split, 1)

            ahead = splitter(split_slot)

            def output(name):
                ahead(name)
                full(dve, name)

            def taken(name):
                ahead(name)
                evacuated(dve, name)

            def split_output(hi, lo, name):
                output(name)
                step(v.tensor_copy(R(hi), bank(name)[:, 0:T]))
                free(v.tensor_tensor(R(lo), bank(name)[:, 0:T], R(hi), ALU.subtract), name)

            def take_rinv():
                n = n_rinv[0]
                n_rinv[0] += 1
                dve.wait_ge(rinv_ready, n + 1)
                return rinv[:, n % 2, :]

            def normalise(name, outs, gain, rows=(slice(0, P),)):
                ahead("ss_" + name)
                r = take_rinv()
                for out, rr in zip(outs, rows):
                    ins = v.scalar_tensor_tensor(out=out, in0=bank(name)[rr, 0:T], scalar=col(gain, 0, rr), in1=r[rr, :],
                                                 op0=ALU.mult, op1=ALU.mult)
                free(ins, name)

            def norm_row(hi, lo, src, gain, row, shift=None, meanwhile=None):
                dve.wait_ge(row_rinv_ready, row + 1)
                for i in range(KD):
                    v.scalar_tensor_tensor(out=lo[:, i, :], in0=src[:, i, :], scalar=gain[:, i:i + 1], in1=row_rinv[:, :],
                                           op0=ALU.mult, op1=ALU.mult).then_inc(u_normed, 1)
                if meanwhile:
                    ahead(meanwhile, 0)
                for i in range(KD):
                    dve.wait_ge(u_rounded, row * KD + i + 1)
                    if shift is None:
                        ins = v.tensor_tensor(R(lo[:, i, :]), lo[:, i, :], R(hi[:, i, :]), ALU.subtract)
                    else:
                        ins = v.scalar_tensor_tensor(out=R(lo[:, i, :]), in0=lo[:, i, :], scalar=shift[:, i:i + 1],
                                                     in1=R(hi[:, i, :]), op0=ALU.add, op1=ALU.subtract)
                    ins.then_inc(u_ready, 1)

            def gains(name):
                return cols[:, AT[name]:AT[name] + KD]

            def ada_step():
                n = n_ada[0]
                n_ada[0] += 1
                j, k = n // KD, n % KD
                acc = ada_acc[:, j % 2, :]
                if n < ADA_EARLY:
                    dve.wait_ge(ada_early_full[n % len(ada_early)], 16 * (n // len(ada_early) + 1))
                    w = ada_early[n % len(ada_early)]
                else:
                    r = (n - ADA_EARLY) % ADA_RING
                    dve.wait_ge(ada_full[r], 16 * ((n - ADA_EARLY) // ADA_RING + 1))
                    w = ada_ring[:, r, :]
                c = c_act[:, 1, k:k + 1]
                if k == 0:
                    if j >= 2:
                        output(f"ada{j - 2}b")
                    v.tensor_scalar(acc, w, c, None, ALU.mult).then_inc(ada_used, 1)
                else:
                    dve.wait_ge(ada_used, n)
                    v.scalar_tensor_tensor(out=acc, in0=w, scalar=c, in1=acc, op0=ALU.mult, op1=ALU.add).then_inc(ada_used, 1)
                if k == KD - 1:
                    dve.wait_ge(ada_used, n + 1)
                    v.tensor_copy(c_act[:, 0, 0:1], c_act[:, 1, 0:1]).then_inc(ada_summed, 1)

            def ada_reduce(j):
                at = mod[:, j * 8:(j + 1) * 8]
                for half in range(2):
                    name = f"ada{j}{'ab'[half]}"
                    output(name)
                    free(v.tensor_reduce(out=at[:, half * 4:half * 4 + 4], in_=bank(name)[:, :].rearrange("p (k i) -> p k i", i=P),
                                         axis=AX.X, op=ALU.add), name)
                taken(f"ada{j}a")
                taken(f"ada{j}b")
                b = cols[:, AT["ada_b"] + j * 8:AT["ada_b"] + (j + 1) * 8]
                if j in (1, 4):
                    step(v.scalar_tensor_tensor(out=at, in0=at, scalar=1.0, in1=b, op0=ALU.add, op1=ALU.add))
                    v.tensor_tensor(at, at, gains("norm1_g" if j == 1 else "norm2_g"), ALU.mult).then_inc(mod_ready, 1)
                elif j == 2:
                    step(v.tensor_tensor(at, at, b, ALU.add))
                    v.tensor_scalar(at, at, 0.5, None, ALU.mult).then_inc(mod_ready, 1)
                else:
                    v.tensor_tensor(at, at, b, ALU.add).then_inc(mod_ready, 1)

            v.memset(mat("ones"), 1.0).then_inc(ones_ready, 1)
            dve.wait_ge(c_tanh_ready, 1)
            step(v.tensor_scalar(c_act[:, 0, :], c_act[:, 0, :], 0.5, 0.5, ALU.mult, ALU.add))
            step(v.tensor_tensor(c_act[:, 1, :], c_act[:, 0, :], cols[:, AT["c"]:AT["c"] + 8], ALU.mult))
            for _ in range(2):
                ada_step()
            ahead("mem_ss", 1)
            norm_row(mem_n, mem_n_lo, mem_n, gains("mem_norm_2"), ROW_MEM)
            ahead("mem_ss")
            for _ in range(5):
                ada_step()
            for b in range(4):
                normalise(f"mem_k{b}", [mem_k[:, b, :]], "mem_k_norm_2")
                for _ in range((3, 3, 2, 1)[b]):
                    ada_step()
                if b == 2:
                    output("bias")
                    free(v.tensor_copy(bias_line, bank("bias")[0:8, :]), "bias")
            v.tensor_scalar(half_bias[:, :], cols[:, AT["b_gate_2"]:AT["b_gate_2"] + 24], 0.5, None, ALU.mult).then_inc(half_bias_ready, 1)
            ada_reduce(0)
            ada_reduce(1)
            dve.wait_ge(mod_ready, 2)
            norm_row(u, u_lo, x, mod[:, 8:16], ROW_X, mod[:, 0:8], "mem_v0")

            dve.wait_ge(zeros_ready, 4)
            for n, off in (("ks", 0), ("kw", P)):
                ahead("ss_" + n)
                r = take_rinv()
                late = 272 + off
                for s, rr in enumerate((LO, HI)):
                    for first, dst in ((0, off), (P, late)):
                        ins = v.scalar_tensor_tensor(out=kcat[rr, s, dst:dst + P], in0=bank(n)[rr, first:first + P],
                                                     scalar=col("k_slc_norm" if n == "ks" else "k_win_norm", 0, rr),
                                                     in1=r[rr, first:first + P], op0=ALU.mult, op1=ALU.mult)
                free(ins, n)
                ada_step()
            for b in range(4):
                normalise(f"qa{b}", [qa[:, b, :]], "q_norm")
                ada_step()
            for b in range(4):
                ahead(f"kb{b}")
                ada_step()
            for b in range(3):
                ahead(f"qb{b}")
                ada_step()
            ada_reduce(2)
            for _ in range(3):
                ada_step()
            ada_reduce(3)
            for _ in range(2):
                ada_step()

            before = mat("before")

            def softplus(h):
                ahead(f"sbz{h}")
                dve.wait_ge(sb_log_ready, h + 1)
                w = sbw[:, h % 2, :, :]
                step(v.scalar_tensor_tensor(out=w[:, 2, :], in0=bank(f"sbz{h}")[:, 0:384], scalar=0.0, in1=w[:, 1, :],
                                            op0=ALU.max, op1=ALU.add))
                v.tensor_tensor(w[:, 2, 0:P], w[:, 2, 0:P], before, ALU.mult)
                v.tensor_tensor(w[:, 2, T:T + P], w[:, 2, T:T + P], before, ALU.mult).then_inc(softplus_ready, 1)

            softplus(0)
            for h in range(8):
                if h == 0:
                    for w, n in enumerate("kv"):
                        ahead(f"cmp_turn_{n}")
                        dve.wait_ge(cmp_tanh_ready, w + 1)
                        th = cmp_tanh[:, w, 0:N_CMP]
                        step(v.tensor_scalar(th, th, 0.5, 0.5, ALU.mult, ALU.add))
                        free(v.tensor_tensor(cmp_turned[:, w, 0:N_CMP], th, bank(f"cmp_turn_{n}")[:, 0:N_CMP], ALU.mult), f"cmp_turn_{n}")
                    taken("ga_turn")
                    step(v.tensor_scalar(gate_tanh[:, :, :], gate_tanh[:, :, :], 0.5, 0.5, ALU.mult, ALU.add))
                    for t in range(TT):
                        g = gate_tanh[:, t, :].rearrange("p (h r) -> p h r", r=3)
                        v.tensor_copy(gate_t[:, :, 2 * t:2 * t + 2], g[:, :, 1:3])
                        v.tensor_scalar(gate_t[:, :, 4 + t], g[:, :, 0], col("sees_a_block", t), None, ALU.mult).then_inc(gate_t_ready, 1)
                if h == 2:
                    ahead("ss_cmp")
                    dve.wait_ge(cmp_rinv_ready, 1)
                    for s, rr in enumerate((LO, HI)):
                        ins = v.scalar_tensor_tensor(out=kcat[rr, s, T:T + N_CMP], in0=cmp_k[rr, 0, 0:N_CMP],
                                                     scalar=col("k_cmp_norm", 0, rr), in1=cmp_k[rr, 3, 0:N_CMP],
                                                     op0=ALU.mult, op1=ALU.mult)
                    ins.then_inc(cmp_k_ready, 1)
                if h < 7:
                    softplus(h + 1)
                for _ in range(2 if h < 6 else 1):
                    ada_step()
                if h and h % 2 == 0:
                    split_output(attn_b[:, h // 2 - 1, :], attn_b_lo1[:, h // 2 - 1, :], f"sbo{h // 2 - 1}")
                if h == 5:
                    ada_reduce(4)

            def nsa_logits(i):
                h = i // 2 + 4 * (i % 2)
                w, st = logit[:, 1 - i % 2, :], stats[:, i % 2, :, :]
                if i >= 2:
                    output(f"nsat{i - 2}c")
                early = w[:, 0:256].rearrange("p (r k) -> p r k", r=2)
                late = w[:, 256:768].rearrange("p (r k) -> p r k", r=2)

                def add(out, ps, b):
                    return v.scalar_tensor_tensor(out=out, in0=ps, scalar=HD ** -0.5, in1=b, op0=ALU.mult, op1=ALU.add)

                def both(b):
                    return b.unsqueeze(1).to_broadcast([P, 2, P])

                for c, t, dst, b in (("a", 0, early, bias[:, h, P:T]), ("b", 1, late[:, :, 0:P], bias[:, h, 0:P])):
                    output(f"nsa{i}{c}")
                    ps = bank(f"nsa{i}{c}")
                    add(dst, ps[:, 0:256].rearrange("p (r k) -> p r k", r=2), both(b))
                    free(add(w[:, 768 + 16 * t:768 + 16 * t + N_CMP], ps[:, T:T + N_CMP], bias_cmp[:, h, t, :]), f"nsa{i}{c}")
                output(f"nsa{i}c")
                free(add(late[:, :, P:T], bank(f"nsa{i}c")[:, 0:256].rearrange("p (r k) -> p r k", r=2), both(bias[:, h, P:T])), f"nsa{i}c")
                for c in "abc":
                    taken(f"nsa{i}{c}")
                v.tensor_reduce(out=st[:, 0, 0:2], in_=early, axis=AX.X, op=ALU.max, negate=True)
                v.tensor_reduce(out=st[:, 0, 4:6], in_=w[:, 768:800].rearrange("p (t k) -> p t k", t=2)[:, :, 0:N_CMP],
                                axis=AX.X, op=ALU.max, negate=True)
                v.tensor_reduce(out=st[:, 0, 2:4], in_=late, axis=AX.X, op=ALU.max, negate=True).then_inc(logits_ready, 1)

            def scale_weights(i, n, parts, gate=None):
                dve.wait_ge(weights_raw, i + 1)
                st = stats[:, i % 2, :, :]
                step(v.tensor_scalar(st[:, 2, 0:n], st[:, 1, 0:n], 1e-30, None, ALU.max))
                step(v.reciprocal(st[:, 3 if gate is None else 2, 0:n], st[:, 2, 0:n]))
                if gate is not None:
                    step(v.tensor_tensor(st[:, 3, 0:n], st[:, 2, 0:n], gate, ALU.mult))
                for k, p in enumerate(parts):
                    ins = v.tensor_scalar(p, p, st[:, 3, k:k + 1], None, ALU.mult)
                ins.then_inc(weights_ready, 1)

            def nsa_scale(i):
                w = logit[:, 1 - i % 2, :]
                scale_weights(i, 6, [w[:, 0:128], w[:, 128:256], w[:, 256:512], w[:, 512:768], w[:, 768:768 + N_CMP],
                                     w[:, 784:784 + N_CMP]], gate_t[:, i // 2 + 4 * (i % 2), :])

            dve.wait_ge(loaded["bias"], 16 * 24)
            nsa_logits(0)
            split_output(attn_b[:, 3, :], attn_b_lo1[:, 3, :], "sbo3")
            nsa_logits(1)
            dve.wait_ge(gate_t_ready, TT)
            nsa_scale(0)
            ada_reduce(5)
            for i in range(8):
                output(f"nsat{i}w")
                free(v.tensor_copy(turned[:, i % 2, 1, 0:384], bank(f"nsat{i}w")[:, 0:384]), f"nsat{i}w")
                if i and i % 2 == 0:
                    split_output(attn_a[:, i // 2 - 1, :], attn_a_lo1[:, i // 2 - 1, :], f"nsao{i // 2 - 1}")
                if i < 6:
                    nsa_logits(i + 2)
                if i < 7:
                    nsa_scale(i + 1)
            split_output(attn_a[:, 3, :], attn_a_lo1[:, 3, :], "nsao3")

            def rest_of_merged(n, m, lo):
                dve.wait_ge(merged_rounded, n + 1)
                v.tensor_tensor(R(lo[:, m, :]), lo[:, m, :], R(merged[:, m, :]), ALU.subtract).then_inc(merged_ready, 1)

            def rest_of_hidden(n, i):
                dve.wait_ge(hidden_rounded, n + 1)
                v.tensor_tensor(R(hidden_lo[:, i, :]), hidden_lo[:, i, :], R(hidden[:, i, :]), ALU.subtract).then_inc(hidden_ready, 1)

            for m in range(KD):
                dve.wait_ge(tanh_ready, m // 2 + 1)
                taken(f"mb{m}")
                for n, g, dst in ((f"up_nsa{m}", m, merged_lo1[:, m, :]), (f"up_sb{m}", 8 + m, part[:, m % 2, :])):
                    output(n)
                    free(v.scalar_tensor_tensor(out=dst, in0=gates[:, g, :], scalar=1.0, in1=bank(n)[:, 0:T],
                                                op0=ALU.add, op1=ALU.mult), n)
                taken(f"up_nsa{m}")
                taken(f"up_sb{m}")
                v.tensor_tensor(merged_lo1[:, m, :], merged_lo1[:, m, :], part[:, m % 2, :], ALU.add).then_inc(merged_raw, 1)
                if m:
                    rest_of_merged(m - 1, m - 1, merged_lo1)
                dve.wait_ge(merged_raw, m + 1)
            rest_of_merged(KD - 1, KD - 1, merged_lo1)

            def add_residual(name, m, gate):
                output(name)
                free(v.scalar_tensor_tensor(out=x[:, m, :], in0=bank(name)[:, 0:T], scalar=gate, in1=x[:, m, :],
                                            op0=ALU.mult, op1=ALU.add), name)

            dve.wait_ge(mod_ready, 6)
            for m in range(KD):
                add_residual(f"mix{m}", m, mod[:, 16 + m:17 + m])

            for i in range(KD):
                taken(f"mix{i}")
            norm_row(u, u_lo, x, mod[:, 32:40], ROW_1, mod[:, 24:32])

            def rope_steps():
                dve.wait_ge(loaded["pos"], 16)
                step(v.tensor_copy(pos[:, :], pos_i[:, :]))
                yield
                for r in range(4):
                    step(v.tensor_scalar(rope[:, r, :], pos[:, :], col("angle", r), None, ALU.mult))
                    yield
                step(v.tensor_scalar(rope_n, rope[:, :, :], 1.0 / TWO_PI, BIG, ALU.mult, ALU.add))
                yield
                step(v.tensor_scalar(rope_n, rope_n, -BIG, None, ALU.add))
                yield
                for c in (PI_1, PI_2, PI_3):
                    step(v.scalar_tensor_tensor(out=rope[:, :, :], in0=rope_n, scalar=-c, in1=rope[:, :, :], op0=ALU.mult, op1=ALU.add))
                    yield
                for r in range(4):
                    step(v.tensor_scalar(rope[:, r, :], rope[:, r, :], col("phase", r), None, ALU.add))
                    yield
                step(v.tensor_scalar(rope_n, rope[:, :, :], PI_LIMIT, -TWO_PI, ALU.is_gt, ALU.mult))
                yield
                step(v.tensor_tensor(rope[:, :, :], rope[:, :, :], rope_n, ALU.add))
                yield
                v.tensor_scalar(rope[:, :, :], rope[:, :, :], PI_LIMIT, -PI_LIMIT, ALU.min, ALU.max).then_inc(rope_angle_ready, 1)
                yield

            steps = rope_steps()
            for m in range(KF):
                taken(f"w1_{m}")
                v.tensor_tensor(hidden_lo[:, m, :], part[:, m % 2, :], part[:, m % 2, :], ALU.mult).then_inc(hidden_raw, 1)
                if m:
                    rest_of_hidden(m - 1, m - 1)
                next(steps, None)
            rest_of_hidden(KF - 1, KF - 1)

            def add_and_split(last, gate, gain, row):
                for m in range(KD):
                    add_residual(f"{last}{m}", m, gate(m))
                    taken(f"{last}{m}")
                    v.tensor_scalar(u_lo[:, m, :], x[:, m, :], gain[:, m:m + 1], None, ALU.mult).then_inc(u_normed, 1)
                    for i in ([m - 1] if m else []) + ([m] if m == KD - 1 else []):
                        dve.wait_ge(u_rounded, row * KD + i + 1)
                        v.tensor_tensor(R(u_lo[:, i, :]), u_lo[:, i, :], R(u[:, i, :]), ALU.subtract).then_inc(u_ready, 1)

            add_and_split("w2_", lambda m: mod[:, 40 + m:41 + m], gains("ffn1_norm_2"), ROW_2)

            def swiglu(p, row, before):
                dve.wait_ge(row_rinv_ready, row + 1)
                for m in range(KF2):
                    output(f"{p}g{m}")
                    if m >= 2:
                        dve.wait_ge(hidden_raw, before + m - 1)
                    free(v.tensor_tensor(part[:, m % 2, :], bank(f"{p}g{m}")[:, 0:T], row_rinv[:, :], ALU.mult), f"{p}g{m}")
                    output(f"{p}u{m}")
                    free(v.tensor_tensor(hidden_lo[:, m, :], bank(f"{p}u{m}")[:, 0:T], row_rinv[:, :], ALU.mult), f"{p}u{m}")
                    taken(f"{p}u{m}")
                    dve.wait_ge(silu_ready, before - KF + m + 1)
                    v.tensor_tensor(hidden_lo[:, m, :], hidden_lo[:, m, :], part[:, m % 2, :], ALU.mult).then_inc(hidden_raw, 1)
                    if m:
                        rest_of_hidden(before + m - 1, m - 1)
                rest_of_hidden(before + KF2 - 1, KF2 - 1)
                for m in range(KD):
                    add_residual(f"{p}d{m}", m, 0.5)
                for m in range(KD):
                    taken(f"{p}d{m}")

            swiglu("f1", ROW_2, KF)

            norm_row(u, u_lo, x, gains("mix_norm_2"), ROW_3)
            for first, n, last, sums, meanwhile in ((0, 3, "cq2", "ss_cq", "ckv1"), (3, 2, "ckv1", "ss_ckv", "qm0")):
                taken(last)
                ahead(sums)
                r = take_rinv()
                for i in range(first, first + n):
                    ahead(meanwhile)
                    z, lo = latent[:, i, :], latent_lo[:, i, :]
                    step(v.tensor_tensor(lo, z, r, ALU.mult))
                    step(v.tensor_tensor(R(z), z, r, ALU.mult))
                    v.tensor_tensor(R(lo), lo, R(z), ALU.subtract).then_inc(latent_ready, 1)
            for b in range(3):
                normalise(f"qm{b}", [qa[:, b, :]], "mem_q_norm_2")
            dve.wait_ge(rope_ready, 1)
            output("kr_rot")
            taken("kr")
            step(v.tensor_tensor(kr[:, 1, :], kr[:, 0, :], rope[:, ROPE_C, :], ALU.mult))
            free(v.tensor_tensor(part[:, 0, :], bank("kr_rot")[:, 0:T], rope[:, ROPE_S, :], ALU.mult), "kr_rot")
            taken("kr_rot")
            v.tensor_tensor(kr[:, 1, :], kr[:, 1, :], part[:, 0, :], ALU.add).then_inc(k_pe_ready, 1)
            dve.wait_ge(k_pe_ready, 1)

            def mla_q_gain(h):
                dve.wait_ge(squares_ready, 19 + h + 1)
                odd = h % 2
                if h >= 2:
                    dve.wait_ge(normed, h - 1)
                free(v.scalar_tensor_tensor(out=part[:, h % 2, :], in0=bank(f"uq{h}")[:, 0:T],
                                            scalar=col("mla_q_odd" if odd else "mla_q_even"), in1=rope[:, ROPE_QO if odd else ROPE_QE, :],
                                            op0=ALU.mult, op1=ALU.mult), f"uq{h}")

            def mla_q_norm(h):
                taken(f"uq{h}")
                r = take_rinv()
                v.tensor_tensor(pair_q[:, h, :], part[:, h % 2, :], r, ALU.mult).then_inc(normed, 1)

            mla_q_gain(0)
            normalise("qm3", [qa[:, 3, :]], "mem_q_norm_2")
            for h in range(8):
                if h < 7:
                    mla_q_gain(h + 1)
                mla_q_norm(h)
            for h in range(8):
                name, (own, pe_rows) = f"uk{h // 2}", ((LO, HI), (HI, LO))[h % 2]
                ahead(f"ss_uk{h}")
                r = take_rinv()
                ins = v.scalar_tensor_tensor(out=pair_k[own, h, :], in0=bank(name)[own, 0:T], scalar=col("mla_k_nope", 0, own),
                                             in1=r[own, :], op0=ALU.mult, op1=ALU.mult)
                if h % 2:
                    free(ins, name)
                v.tensor_tensor(pair_k[pe_rows, h, :], kr[pe_rows, 1, :], r[pe_rows, :], ALU.mult).then_inc(normed, 1)

            for t in range(TT):
                taken(f"sv{t}")
                step(v.bn_stats(sg_stat[:, t, 0:6], sg_v[:, t, :]))
                ins = v.bn_aggr(sg_stat[:, t, 6:8], sg_stat[:, t, 0:6])
            ins.then_inc(sg_var_ready, 1)

            def sg_norm():
                ahead("su3")
                dve.wait_ge(sg_dev_ready, 1)
                dve.wait_ge(loaded["sg"], 48)
                for t in range(TT):
                    s = sg_v[:, t, :]
                    step(v.tensor_scalar(s, s, sg_stat[:, t, 6:7], sg_stat[:, t, 9:10], ALU.subtract, ALU.mult))
                    step(v.tensor_tensor(s, s, sg_ln[:, 0, :], ALU.mult))
                    v.tensor_tensor(s, s, sg_ln[:, 1, :], ALU.add).then_inc(sg_ln_ready, 1)

            def logits(i):
                w, st = logit[:, 1 - i % 2, :], stats[:, i % 2, :, :]
                if i >= 2:
                    output(f"mlat{i - 2}" if i < 10 else f"memt{i - 10}")
                if i < 8:
                    name = f"mla{i}"
                    output(name)
                    ps = bank(name)
                    scale = 96 ** -0.5
                    v.scalar_tensor_tensor(out=w[:, 0:P], in0=ps[:, 0:P], scalar=scale, in1=mat("not_after"), op0=ALU.mult, op1=ALU.add)
                    v.tensor_scalar(w[:, P:T], ps[:, P:T], scale, None, ALU.mult)
                    free(v.scalar_tensor_tensor(out=w[:, T:384], in0=ps[:, T:384], scalar=scale, in1=mat("not_after"),
                                                op0=ALU.mult, op1=ALU.add), name)
                    taken(name)
                    v.tensor_reduce(out=st[:, 0, 0:1], in_=w[:, 0:P], axis=AX.X, op=ALU.max, negate=True)
                    v.tensor_reduce(out=st[:, 0, 1:2], in_=w[:, P:384], axis=AX.X, op=ALU.max, negate=True).then_inc(logits_ready, 1)
                else:
                    name = f"mem{i - 8}"
                    output(name)
                    step(v.tensor_reduce(out=st[:, 0, 2:4], in_=bank(name)[:, :].rearrange("p (t k) -> p t k", t=2),
                                         axis=AX.X, op=ALU.max, negate=True))
                    v.tensor_scalar(st[:, 0, 0:2], st[:, 0, 2:4], P ** -0.5, None, ALU.mult).then_inc(logits_ready, 1)

            def attend_scale(i):
                w = logit[:, 1 - i % 2, :]
                scale_weights(8 + i, 2, [w[:, 0:P], w[:, P:384]] if i < 8 else [w[:, 0:T], w[:, T:2 * T]])

            logits(0)
            attend_scale(0)
            logits(1)
            attend_scale(1)
            sg_norm()
            for i in range(12):
                if 0 < i < 11:
                    logits(i + 1)
                if i and i % 2 == 0 and i <= 8:
                    split_output(attn_b[:, i // 2 - 1, :], attn_b_lo2[:, i // 2 - 1, :], f"mlao{i // 2 - 1}")
                if i >= 9:
                    split_output(attn_c[:, i - 9, :], attn_c_lo2[:, i - 9, :], f"memo{i - 9}")
                if 0 < i < 11:
                    attend_scale(i + 1)
            for b in range(4):
                taken(f"su{b}")
                for c in range(TT):
                    name = f"sg{b}{c}"
                    output(name)
                    for s, rr in enumerate((LO, HI)):
                        dst = attn_a[rr, b, c * P:(c + 1) * P]
                        ins = v.tensor_tensor(attn_a_lo2[rr, b, c * P:(c + 1) * P], dst, bank(name)[rr, s * P:(s + 1) * P], ALU.mult)
                    free(ins, name)
                    taken(name)
                step(v.tensor_copy(R(attn_a[:, b, :]), attn_a_lo2[:, b, :]))
                v.tensor_tensor(R(attn_a_lo2[:, b, :]), attn_a_lo2[:, b, :], R(attn_a[:, b, :]), ALU.subtract).then_inc(sg_ready, 1)
            split_output(attn_c[:, 3, :], attn_c_lo2[:, 3, :], "memo3")

            for m in range(KD):
                for k, c in enumerate("abc"):
                    taken(f"gate{8 * k + m}")
                    n = f"br_{c}{m}"
                    output(n)
                    dst = merged_lo2[:, m, :] if k == 0 else part[:, k - 1, :]
                    free(v.scalar_tensor_tensor(out=dst, in0=gates[:, 8 * k + m, :], scalar=1.0, in1=bank(n)[:, 0:T],
                                                op0=ALU.add, op1=ALU.mult), n)
                for c in "abc":
                    taken(f"br_{c}{m}")
                step(v.tensor_tensor(merged_lo2[:, m, :], merged_lo2[:, m, :], part[:, 0, :], ALU.add))
                v.tensor_tensor(merged_lo2[:, m, :], merged_lo2[:, m, :], part[:, 1, :], ALU.add).then_inc(merged_raw, 1)
                dve.wait_ge(merged_raw, KD + m + 1)
                if m:
                    rest_of_merged(KD + m - 1, m - 1, merged_lo2)
            rest_of_merged(2 * KD - 1, KD - 1, merged_lo2)
            add_and_split("mix2_", lambda m: 0.5, gains("ffn2_norm_2"), ROW_4)
            swiglu("f2", ROW_4, KF + KF2)


def lay_out(a):
    a = {k: np.asarray(v) for k, v in a.items()}
    sq = {k: (v[0] if k not in ("x", "c", "rel_bias", "mem_2", "positions_2") else v) for k, v in a.items()}

    def block_diagonal(w):
        out = np.zeros(w.shape[:-2] + (P, P), w.dtype)
        out[..., 0:64, 0:64] = w
        out[..., 64:, 64:] = w
        return out

    src = dict(sq)
    for n in ("cmp_k_w1", "cmp_v_w1"):
        src[n] = block_diagonal(sq[n].reshape(32, HD, HD))
    chunks = stream_chunks()
    n_slots = -(-len(chunks) // SLOT)
    stream = np.zeros((n_slots, P, SLOT, P), np.float32)
    for i, (name, rows, cols) in enumerate(chunks):
        w = src[name]
        stream[i // SLOT, :, i % SLOT, :] = w[rows] if cols is None else w[np.ix_(rows, cols)]
    ada = sq["ada_w"].reshape(KD, P, 6, D).transpose(2, 0, 1, 3).reshape(48, P, D)
    mats, buckets, consts = shape_constants()
    q, k = sq["mla_q_norm_2"], sq["mla_k_norm_2"]
    pe = np.concatenate([q[64:96], q[80:96], q[64:80]])
    twice = lambda v: np.concatenate([v, v])
    vec = {n: sq[n] for n in ("norm1_g", "norm2_g", "ffn1_norm_2", "mix_norm_2", "ffn2_norm_2", "mem_norm_2", "ada_b",
                              "b_gate_2", "mla_cq_norm_2", "mla_ckv_norm_2", "mem_q_norm_2", "mem_k_norm_2")}
    vec["c"] = a["c"]
    vec["q_norm"] = twice(sq["q_norm_g"])
    for i, n in enumerate(("k_cmp_norm", "k_slc_norm", "k_win_norm")):
        vec[n] = twice(sq["k_norm_g"][i])
    vec["mla_q_even"] = np.concatenate([q[0:64], pe])
    vec["mla_q_odd"] = np.concatenate([pe, q[0:64]])
    vec["mla_k_nope"] = twice(k[0:64])
    vec["mla_k_rope"] = np.concatenate([k[64:96]] * 4)
    vec.update(consts)
    cols = np.concatenate([np.asarray(vec[n], np.float32).reshape(c, P) for n, c in VECTORS]).T

    def feature_major(v):
        return np.ascontiguousarray(v.reshape(T, KD, P).transpose(2, 1, 0))

    table = np.concatenate([a["rel_bias"], np.ones((1, 8), np.float32)])
    pos_rows = sq["cmp_pos"].T
    out = {
        "stream": stream.reshape(n_slots, P, SLOT * P), "ada": ada, "x_t": feature_major(a["x"]),
        "mem_t": feature_major(a["mem_2"]), "cols": cols, "mats": mats.transpose(1, 0, 2), "buckets": buckets,
        "table": table, "pos": np.broadcast_to(a["positions_2"], (P, T)),
        "cmp_w2": np.stack([block_diagonal(sq["cmp_k_w2"]), block_diagonal(sq["cmp_v_w2"])], 1),
        "cmp_pos": np.concatenate([pos_rows, pos_rows]),
        "sg_w": sq["sg_w_2"].transpose(2, 0, 1), "sg_b": sq["sg_b_2"].reshape(1, 8 * P),
        "sg_ln": np.broadcast_to(np.stack([sq["sg_ln_g_2"], sq["sg_ln_b_2"]])[None], (P, 2, 512)),
    }
    return {n: np.ascontiguousarray(v) for n, v in out.items()}


def kernel(**inputs):
    import concourse.bacc as bacc
    from concourse.bass_utils import run_bass_kernel_spmd

    arrays = lay_out(inputs)
    nc = bacc.Bacc("TRN2", target_bir_lowering=False, num_devices=1)
    args = [nc.dram_tensor(f"in_{n}", v.shape, mybir.dt.from_np(v.dtype), kind="ExternalInput").ap() for n, v in arrays.items()]
    out = nc.dram_tensor("out_t", (P, KD, T), F32, kind="ExternalOutput").ap()
    build(nc, *args, out)
    r = run_bass_kernel_spmd(nc, [{f"in_{n}": v for n, v in arrays.items()}], core_ids=[0])
    got = np.asarray(r.results[0]["out_t"])
    return np.ascontiguousarray(got.transpose(2, 1, 0)).reshape(1, T, D)
```
